# Optimizing a Trainium2 kernel written in Bass

```python
import jax, jax.numpy as jnp
from jax import lax
import numpy as np

"""Hybrid bidirectional encoder layer (Hymba-style parallel head groups).

Each layer: RMSNorm -> one combined input projection whose columns are split between
(A) a multi-scale centred-pooling mixer (4 channel groups, windows 2/4/8/16) and
(B) a bidirectional chunkwise-parallel mLSTM (4 heads, matrix memory, exp input gate,
sigmoid forget gate, running-max stabiliser, one scan per direction) -> concat ->
one output projection -> residual; then RMSNorm -> hierarchical MoE (top-1 group,
top-2 experts inside the group, SwiGLU experts) -> residual. Final RMSNorm.
The same parameters process x_prompt (BATCH, SEQ, D_MODEL) and
x_sample (DEC_BATCH, DEC_SEQ, D_MODEL); returns (y_prompt, y_sample) with the same shapes.
"""

D_MODEL = 1024
BATCH = 1
SEQ = 256
DEPTH = 1
DEC_BATCH = 1
DEC_SEQ = 1024
PAST_LEN = 128

D_MIX = D_MODEL
POOL_WIDTH = D_MIX // 2
POOL_WINDOWS = (2, 4, 8, 16)
POOL_GROUP = POOL_WIDTH // len(POOL_WINDOWS)
MLSTM_WIDTH = D_MIX - POOL_WIDTH
MLSTM_HEADS = 4
MLSTM_HEAD_DIM = MLSTM_WIDTH // MLSTM_HEADS
CHUNK = 128
N_GATE_COLS = 4 * MLSTM_HEADS
OFF_POOL = 0
OFF_Q = OFF_POOL + POOL_WIDTH
OFF_K = OFF_Q + MLSTM_WIDTH
OFF_V = OFF_K + MLSTM_WIDTH
OFF_O = OFF_V + MLSTM_WIDTH
OFF_G = OFF_O + MLSTM_WIDTH
P_IN = OFF_G + N_GATE_COLS
N_GROUPS = 4
EXPERTS_PER_GROUP = 8
N_EXPERTS = N_GROUPS * EXPERTS_PER_GROUP
TOP_K_INNER = 2
D_EXPERT = D_MODEL // 2
MOE_BLOCK = 128
EPS = 1e-6

kernel_name = "hymba_pool_mlstm_hmoe_encoder"

def rmsnorm(x, g):
    x32 = x.astype(jnp.float32)
    y = x32 * lax.rsqrt(jnp.mean(x32 * x32, axis=-1, keepdims=True) + EPS)
    return (y * g.astype(jnp.float32)).astype(x.dtype)

def multiscale_pool(u, w_pool, scale):
    B, S, C = u.shape
    u32 = u.astype(jnp.float32)
    cs = jnp.concatenate([jnp.zeros((B, 1, C), jnp.float32), jnp.cumsum(u32, axis=1)], axis=1)
    pos = jnp.arange(S)
    outs = []
    for g, w in enumerate(POOL_WINDOWS):
        sl = slice(g * POOL_GROUP, (g + 1) * POOL_GROUP)
        lo = jnp.clip(pos - w // 2, 0, S)
        hi = jnp.clip(pos + w // 2, 0, S)
        csg = cs[..., sl]
        cnt = (hi - lo).astype(jnp.float32)[None, :, None]
        d = (csg[:, hi] - csg[:, lo]) / cnt - u32[..., sl]
        outs.append(jnp.einsum('bsc,ce->bse', d, w_pool[g].astype(jnp.float32)))
    return jnp.concatenate(outs, axis=-1) * scale.astype(jnp.float32)

def mlstm_chunkwise(q, k, v, ig, lf):
    B, S, H, d = q.shape
    nc = S // CHUNK
    to_c = lambda a: a.reshape(B, nc, CHUNK, H, d).transpose(1, 0, 3, 2, 4)
    to_cg = lambda a: a.reshape(B, nc, CHUNK, H).transpose(1, 0, 3, 2)
    mask = jnp.tril(jnp.ones((CHUNK, CHUNK), bool))

    def step(carry, xs):
        C, n, m = carry
        qc, kc, vc, ic, fc = xs
        b = jnp.cumsum(fc, axis=-1)
        logw = jnp.where(mask, b[..., :, None] - b[..., None, :] + ic[..., None, :], -jnp.inf)
        inter_log = b + m[..., None]
        m_row = jnp.maximum(inter_log, jnp.max(logw, axis=-1))
        s = jnp.einsum('bhjd,bhsd->bhjs', qc, kc) * jnp.exp(logw - m_row[..., None])
        inter = jnp.exp(inter_log - m_row)
        num = jnp.einsum('bhjs,bhsd->bhjd', s, vc) + inter[..., None] * jnp.einsum('bhed,bhjd->bhje', C, qc)
        den = jnp.sum(s, axis=-1) + inter * jnp.einsum('bhd,bhjd->bhj', n, qc)
        h = num / jnp.maximum(jnp.abs(den), jnp.exp(-m_row))[..., None]
        bL = b[..., -1]
        logu = bL[..., None] - b + ic
        m_new = jnp.maximum(bL + m, jnp.max(logu, axis=-1))
        u = jnp.exp(logu - m_new[..., None])
        decay = jnp.exp(bL + m - m_new)
        C_new = decay[..., None, None] * C + jnp.einsum('bhs,bhse,bhsd->bhed', u, vc, kc)
        n_new = decay[..., None] * n + jnp.einsum('bhs,bhsd->bhd', u, kc)
        return (C_new, n_new, m_new), h

    init = (jnp.zeros((B, H, d, d), jnp.float32), jnp.zeros((B, H, d), jnp.float32),
            jnp.zeros((B, H), jnp.float32))
    _, hs = lax.scan(step, init, (to_c(q), to_c(k), to_c(v), to_cg(ig), to_cg(lf)))
    return hs.transpose(1, 0, 3, 2, 4).reshape(B, S, H, d)

def bidir_mlstm(proj, gate_b, head_g):
    B, S, _ = proj.shape
    H, d = MLSTM_HEADS, MLSTM_HEAD_DIM
    p32 = proj.astype(jnp.float32)
    q = p32[..., OFF_Q:OFF_K].reshape(B, S, H, d)
    k = p32[..., OFF_K:OFF_V].reshape(B, S, H, d) * (d ** -0.5)
    v = p32[..., OFF_V:OFF_O].reshape(B, S, H, d)
    o = p32[..., OFF_O:OFF_G]
    g = p32[..., OFF_G:P_IN] + gate_b.astype(jnp.float32)
    ig_f, ig_b = g[..., 0:H], g[..., H:2 * H]
    lf_f, lf_b = jax.nn.log_sigmoid(g[..., 2 * H:3 * H]), jax.nn.log_sigmoid(g[..., 3 * H:4 * H])
    h_f = mlstm_chunkwise(q, k, v, ig_f, lf_f)
    h_b = jnp.flip(mlstm_chunkwise(*(jnp.flip(a, axis=1) for a in (q, k, v, ig_b, lf_b))), axis=1)
    h = h_f + h_b
    h = h * lax.rsqrt(jnp.mean(h * h, axis=-1, keepdims=True) + EPS)
    h = h.reshape(B, S, MLSTM_WIDTH) * head_g.astype(jnp.float32)
    return jax.nn.sigmoid(o) * h

def hier_moe(xn, w_rg, b_rg, w_re, b_re, w_gate, w_up, w_down):
    B, S, D = xn.shape
    T = B * S
    xt = xn.reshape(T, D)
    gl = jnp.matmul(xt, w_rg).astype(jnp.float32) + b_rg.astype(jnp.float32)
    g_idx = jnp.argmax(gl, axis=-1)
    g_w = jnp.take_along_axis(jax.nn.softmax(gl, axis=-1), g_idx[:, None], axis=-1)[:, 0]
    el = (jnp.matmul(xt, w_re.reshape(D, N_EXPERTS)).astype(jnp.float32)
          .reshape(T, N_GROUPS, EXPERTS_PER_GROUP) + b_re.astype(jnp.float32))
    el_sel = jnp.take_along_axis(el, g_idx[:, None, None], axis=1)[:, 0]
    top_v, top_i = lax.top_k(el_sel, TOP_K_INNER)
    ew = jax.nn.softmax(top_v, axis=-1) * g_w[:, None]
    e = (g_idx[:, None] * EXPERTS_PER_GROUP + top_i).reshape(-1).astype(jnp.int32)
    tok = jnp.repeat(jnp.arange(T, dtype=jnp.int32), TOP_K_INNER)
    wt = ew.reshape(-1)
    order = jnp.argsort(e)
    se, stok, swt = e[order], tok[order], wt[order]
    counts = jnp.bincount(e, length=N_EXPERTS)
    starts = jnp.cumsum(counts) - counts
    pcounts = ((counts + MOE_BLOCK - 1) // MOE_BLOCK) * MOE_BLOCK
    pends = jnp.cumsum(pcounts)
    pstarts = pends - pcounts
    N = T * TOP_K_INNER
    dest = pstarts[se] + (jnp.arange(N) - starts[se])
    nb = (N + MOE_BLOCK - 1) // MOE_BLOCK + N_EXPERTS
    P = nb * MOE_BLOCK
    row_tok = jnp.full((P,), T, jnp.int32).at[dest].set(stok)
    xpad = jnp.concatenate([xt, jnp.zeros((1, D), xt.dtype)], axis=0)
    xrows = xpad[row_tok].reshape(nb, MOE_BLOCK, D)
    block_e = jnp.clip(jnp.searchsorted(pends, jnp.arange(nb) * MOE_BLOCK, side='right'), 0, N_EXPERTS - 1)

    def expert_block(args):
        xb, eb = args
        hb = jax.nn.silu(jnp.matmul(xb, w_gate[eb])) * jnp.matmul(xb, w_up[eb])
        return jnp.matmul(hb, w_down[eb])

    yrows = lax.map(expert_block, (xrows, block_e)).reshape(P, D)
    y = jax.ops.segment_sum(yrows[dest] * swt[:, None].astype(yrows.dtype), stok, num_segments=T)
    return y.reshape(B, S, D)

def encoder(x, norm1_g, w_in, pool_w, pool_scale, gate_b, head_norm_g, w_out, norm2_g,
            router_group_w, router_group_b, router_expert_w, router_expert_b,
            expert_w_gate, expert_w_up, expert_w_down, final_norm_g):
    for l in range(DEPTH):
        xn = rmsnorm(x, norm1_g[l])
        proj = jnp.matmul(xn, w_in[l])
        a = multiscale_pool(proj[..., OFF_POOL:OFF_Q], pool_w[l], pool_scale[l])
        m = bidir_mlstm(proj, gate_b[l], head_norm_g[l])
        mix = jnp.concatenate([a, m], axis=-1).astype(x.dtype)
        x = x + jnp.matmul(mix, w_out[l])
        xn2 = rmsnorm(x, norm2_g[l])
        x = x + hier_moe(xn2, router_group_w[l], router_group_b[l], router_expert_w[l],
                         router_expert_b[l], expert_w_gate[l], expert_w_up[l], expert_w_down[l])
    return rmsnorm(x, final_norm_g)

def setup_inputs(seed: int = 0) -> dict:
    key = jax.random.key(seed)
    ks = jax.random.split(key, 20)
    f32 = jnp.float32
    nrm = lambda k, shape, s: jax.random.normal(k, shape, f32) * s
    H = MLSTM_HEADS
    i_bias = nrm(ks[6], (DEPTH, 2 * H), 0.1)
    f_bias = jnp.tile(jnp.linspace(3.0, 6.0, H, dtype=f32), 2)[None, :] + nrm(ks[7], (DEPTH, 2 * H), 0.1)
    return {
        "x_prompt": nrm(ks[0], (BATCH, SEQ, D_MODEL), 1.0),
        "x_sample": nrm(ks[1], (DEC_BATCH, DEC_SEQ, D_MODEL), 1.0),
        "norm1_g": 1.0 + nrm(ks[2], (DEPTH, D_MODEL), 0.05),
        "w_in": nrm(ks[3], (DEPTH, D_MODEL, P_IN), D_MODEL ** -0.5),
        "pool_w": nrm(ks[4], (DEPTH, len(POOL_WINDOWS), POOL_GROUP, POOL_GROUP), POOL_GROUP ** -0.5),
        "pool_scale": 1.0 + nrm(ks[5], (DEPTH, POOL_WIDTH), 0.1),
        "gate_b": jnp.concatenate([i_bias, f_bias], axis=-1),
        "head_norm_g": 1.0 + nrm(ks[8], (DEPTH, MLSTM_WIDTH), 0.05),
        "w_out": nrm(ks[9], (DEPTH, D_MIX, D_MODEL), D_MIX ** -0.5),
        "norm2_g": 1.0 + nrm(ks[10], (DEPTH, D_MODEL), 0.05),
        "router_group_w": nrm(ks[11], (DEPTH, D_MODEL, N_GROUPS), D_MODEL ** -0.5),
        "router_group_b": nrm(ks[12], (DEPTH, N_GROUPS), 0.01),
        "router_expert_w": nrm(ks[13], (DEPTH, D_MODEL, N_GROUPS, EXPERTS_PER_GROUP), D_MODEL ** -0.5),
        "router_expert_b": nrm(ks[14], (DEPTH, N_GROUPS, EXPERTS_PER_GROUP), 0.01),
        "expert_w_gate": nrm(ks[15], (DEPTH, N_EXPERTS, D_MODEL, D_EXPERT), D_MODEL ** -0.5),
        "expert_w_up": nrm(ks[16], (DEPTH, N_EXPERTS, D_MODEL, D_EXPERT), D_MODEL ** -0.5),
        "expert_w_down": nrm(ks[17], (DEPTH, N_EXPERTS, D_EXPERT, D_MODEL), D_EXPERT ** -0.5),
        "final_norm_g": 1.0 + nrm(ks[18], (D_MODEL,), 0.05),
    }

def reference(x_prompt, x_sample, norm1_g, w_in, pool_w, pool_scale, gate_b, head_norm_g, w_out,
              norm2_g, router_group_w, router_group_b, router_expert_w, router_expert_b,
              expert_w_gate, expert_w_up, expert_w_down, final_norm_g):
    y_prompt = encoder(x_prompt, norm1_g, w_in, pool_w, pool_scale, gate_b, head_norm_g, w_out,
                       norm2_g, router_group_w, router_group_b, router_expert_w, router_expert_b,
                       expert_w_gate, expert_w_up, expert_w_down, final_norm_g)
    y_sample = encoder(x_sample, norm1_g, w_in, pool_w, pool_scale, gate_b, head_norm_g, w_out,
                       norm2_g, router_group_w, router_group_b, router_expert_w, router_expert_b,
                       expert_w_gate, expert_w_up, expert_w_down, final_norm_g)
    return (y_prompt, y_sample)


_drawn_inputs = setup_inputs


def setup_inputs(seed=0):
    import zlib

    import numpy as np

    out = dict(_drawn_inputs(seed))
    spreads = {}
    factors = {'router_group_b': 3.399, 'router_expert_b': 3.554}
    for name, (base, spread) in spreads.items():
        noise = np.random.default_rng([zlib.crc32(name.encode()), seed]).standard_normal(out[name].shape)
        drawn = base * np.exp(spread * noise) if base else spread * noise
        out[name] = __import__('jax').numpy.asarray(drawn.astype(out[name].dtype))
    for name, factor in factors.items():
        out[name] = (out[name] * factor).astype(out[name].dtype)
    return out
```

```python
from contextlib import ExitStack

import numpy as np

import concourse.bass as bass
from concourse import mybir

F32 = mybir.dt.float32
F32R = mybir.dt.float32r
BF16 = mybir.dt.bfloat16
I32 = mybir.dt.int32
ALU = mybir.AluOpType
ACT = mybir.ActivationFunctionType
AX = mybir.AxisListType

P = 128
KB = 1024
EPS = 1e-6
MASKED = -1e30


def build(nc, x_prompt, x_sample, norm1_g, w_in, pool_w, pool_scale, gate_b, head_norm_g, w_out,
          norm2_g, router_group_w, router_group_b, router_expert_w, router_expert_b,
          expert_w_gate, expert_w_up, expert_w_down, final_norm_g, y_prompt, y_sample):
    S0, D = x_prompt.shape[1:]
    S1 = x_sample.shape[1]
    T = S0 + S1
    NT = T // P
    C0 = S0 // P
    KD = D // P
    NG = pool_w.shape[1]
    WINDOWS = (2, 4, 8, 16)
    H = head_norm_g.shape[1] // P
    PW, MW = NG * P, H * P
    GR = router_group_w.shape[2]
    EPG = router_expert_w.shape[3]
    E = GR * EPG
    F = expert_w_gate.shape[3]
    KF = F // P
    NL = GR + E
    CAP = T
    SEGS = [(0, 512), (512, 512), (1024, 256)]
    assert (NT, KD, NG, H, KF, E) == (10, 8, 4, 4, 4, 32) and D == 1024

    xn2_dram = nc.dram_tensor("xn2_scratch", (T, D), F32).ap()
    x1_dram = nc.dram_tensor("x1_scratch", (T, D), F32).ap()
    y_dram = nc.dram_tensor("expert_rows", (2 * T + P, D), F32).ap()
    list_dram = nc.dram_tensor("row_lists", (E * CAP, 1), I32).ap()
    pooled_dram = nc.dram_tensor("pooledT", (PW, T), F32).ap()
    ogate_dram = nc.dram_tensor("ogateT", (MW, T), F32).ap()

    def tokens(t, a, b):
        return (a[0, t * P:(t + 1) * P, :] if t < C0 else b[0, (t - C0) * P:(t - C0 + 1) * P, :])

    base = (nc.sbuf_base + 63) // 64 * 64
    top = [base]

    def at(name, off, shape, dt):
        return nc.alloc_sbuf_tensor_at(name, shape, dt, offset=off)

    def const(name, shape, dt=F32):
        size = int(np.prod(shape[1:])) * (2 if dt == BF16 else 4)
        off = top[0]
        top[0] += (size + 31) // 32 * 32
        return at(name, off, shape, dt)

    ident = const("ident", [P, P])
    identb = const("identb", [P, P], BF16)
    maskb = const("maskb", [P, 2, P], BF16)
    laterb = const("laterb", [P, P], BF16)
    onesb = const("onesb", [P, P], BF16)
    zero_row = const("zero_row", [64, P])
    sel = const("sel", [64, 8, P])
    edge = const("edge", [P, NG, 16])
    wpool = const("wpool", [P, NG, P])
    pscale = const("pscale", [P, NG])
    hgain = const("hgain", [P, H])
    gbias = const("gbias", [64, 2])
    rw = const("rw", [P, KD, NL])
    rbias = const("rbias", [P, NL])
    ramp_i = const("ramp_i", [P, EPG + E], I32)
    ramp = const("ramp", [P, EPG])
    ebase = const("ebase", [P, E])
    rowval = const("rowval", [P, 2, NT], I32)
    epsc = const("epsc", [P, 1])
    onec = const("onec", [P, 1])
    cols = const("cols", [P, NT, 4, 8])
    decay = const("decay", [P, 8, NT])
    stat = const("stat", [P, 4, NT])
    negm = const("negm", [64, T])
    sentinel = at("sentinel", top[0] - 4 * T, [80, E * CAP // 80], I32)
    mprev = const("mprev", [64, NT])
    mlast = const("mlast", [64, NT])
    rgs = const("rgs", [P, NT, GR])
    rd21 = const("rd21", [P, NT])
    wts = const("wts", [P, 4, NT])
    chosen = const("chosen", [P, NT, E], BF16)
    half_steps = const("half_steps", [1, 4], I32)
    R0 = (top[0] + 63) // 64 * 64

    X0 = R0
    xT_hi = at("xT_hi", X0, [P, KD, T], F32R)
    xT_lo = at("xT_lo", X0 + 40 * KB, [P, KD, T], F32R)
    W0 = X0 + 80 * KB
    w_hi = at("w_hi", W0, [P, 4, KD, P], F32R)
    w_lo = at("w_lo", W0 + 16 * KB, [P, 4, KD, P], F32R)
    w_st = at("w_st", W0 + 32 * KB, [P, 2, KD, P], F32)
    Q0 = W0 + 40 * KB
    qT = at("qT", Q0, [P, H, T], F32)
    kT = at("kT", Q0 + 20 * KB, [P, H, T], F32)
    v = at("v", Q0 + 40 * KB, [P, NT, H, P + 1], F32)
    PADW = 8 + S0 + 8 + S1 + 8
    pos = [8, 16 + S0]
    u_ext = at("u_ext", Q0, [P, NG, PADW], F32)
    ps_a = at("ps_a", Q0 + 4 * NG * PADW, [P, PADW], F32)
    ps_b = at("ps_b", Q0 + 4 * (NG + 1) * PADW, [P, PADW], F32)
    A0 = Q0 + 4 * (NG + 2) * PADW
    x_in = at("x_in", A0, [P, 3, D], F32)
    xn = at("xn", A0 + 12 * KB, [P, 2, D], F32)
    g1_b = at("g1_b", A0 + 20 * KB, [P, D], F32)
    junk = at("junk", A0 + 24 * KB, [P, D], F32)
    g_i, g_f, g_e, g_b, g_m = (at(n, A0 + 5 * KB * i, [64, T], F32)
                               for i, n in enumerate(("g_i", "g_f", "g_e", "g_b", "g_m")))
    V0 = Q0 + 40 * KB + 4 * NT * H * (P + 1)
    ev = at("ev", V0, [P, 4, 512], F32)
    END = V0 + 8 * KB
    assert END <= nc.sbuf_usable_end, (END, nc.sbuf_usable_end, R0)

    h_fb = at("h_fb", X0, [P, 2, NT, MW], F32)
    wo_hi = at("wo_hi", X0 + 40 * KB, [P, KD, D], F32R)
    state = at("state", X0 + 72 * KB, [P, 2, H, P + 1], F32)
    dn = at("dn", X0 + 77 * KB, [P, 2, 2], F32)
    rdn = at("rdn", X0 + 77 * KB + 64, [P, 2, 2], F32)
    wo_lo = at("wo_lo", W0, [P, KD, D], F32R)
    uk = at("uk", V0, [P, 2, 2, P], F32)
    wgt = at("wgt", V0 + 2 * KB, [P, 2, 2, P], F32)
    sT = at("sT", V0 + 4 * KB, [P, 2, 2, P], F32)
    tq = at("tq", X0 + 77 * KB + 128, [P, 2, 2, P + 1], F32)

    c_off = [Q0]

    def cbuf(name, shape, dt=F32):
        off = c_off[0]
        c_off[0] += (int(np.prod(shape[1:])) * 4 + 31) // 32 * 32
        return at(name, off, shape, dt)

    mixf = cbuf("mixf", [P, 2, KD, P])
    mix_hi = cbuf("mix_hi", [P, 2, KD, P], F32R)
    mix_lo = cbuf("mix_lo", [P, 2, KD, P], F32R)
    x_c = cbuf("x_c", [P, 2, D])
    x1 = cbuf("x1", [P, 2, D])
    xn2 = cbuf("xn2", [P, 2, D])
    og = cbuf("og", [P, 2, H, P])
    g2_b = at("g2_b", X0 + 72 * KB, [P, D], F32)
    xn2T = cbuf("xn2T", [P, KD, P])
    hsum = at("hsum", X0 + 76 * KB, [P, MW], F32)
    hsq = at("hsq", X0 + 78 * KB, [P, MW], F32)
    sq_c = at("sq_c", W0 + 32 * KB, [P, D], F32)
    rt = cbuf("rt", [P, 512], F32)
    slot_i = cbuf("slot_i", [P, 2, 2], I32)
    assert c_off[0] <= END, (c_off[0], END)

    m_off = [X0]

    def mbuf(name, shape, dt=F32):
        off = m_off[0]
        m_off[0] += (int(np.prod(shape[1:])) * 4 + 31) // 32 * 32
        return at(name, off, shape, dt)

    NST, NRG = 12, 6
    e_st = mbuf("e_st", [P, NST, 2, 512])
    e_hi = mbuf("e_hi", [P, NRG, 2, 512], F32R)
    e_lo = mbuf("e_lo", [P, NRG, 2, 512], F32R)
    gx = mbuf("gx", [P, 2, D])
    ex_hi = mbuf("ex_hi", [P, 2, KD, P], F32R)
    ex_lo = mbuf("ex_lo", [P, 2, KD, P], F32R)
    sg = mbuf("sg", [P, F])
    hh = mbuf("hh", [P, F])
    ht_hi = mbuf("ht_hi", [P, KF, P], F32R)
    ht_lo = mbuf("ht_lo", [P, KF, P], F32R)
    yo = mbuf("yo", [P, 2, D])
    row_raw = mbuf("row_raw", [P, 2], I32)
    row_s = mbuf("row_s", [P, 2], I32)
    row_g = mbuf("row_g", [P, 2], I32)
    row_f = mbuf("row_f", [P, 4])
    assert m_off[0] <= END
    gf_b = at("gf_b", X0, [P, D], F32)
    f_y = at("f_y", X0 + 4 * KB, [P, 3, 2, D], F32)
    f_x = at("f_x", X0 + 28 * KB, [P, 3, D], F32)
    f_o = at("f_o", X0 + 40 * KB, [P, 2, D], F32)
    f_sq = at("f_sq", X0 + 48 * KB, [P, D], F32)

    psum = nc.alloc_psum_tensor("psum", [P, 8, 512], F32)

    def two(i):
        return psum[:, i:i + 2, :]

    ctx = ExitStack()
    with ctx:
        ctx.enter_context(nc.allow_non_contiguous_dma(reason="one word to a partition"))

        def sem(name):
            return ctx.enter_context(nc.semaphore(name))

        consts_in, g1_in, list_set = sem("consts_in"), sem("g1_in"), sem("list_set")
        x_load = [sem(f"x_load{i}") for i in range(3)]
        w_load = [sem(f"w_load{i}") for i in range(2)]
        ev_out = [sem(f"ev_out{i}") for i in range(4)]
        pool_step, consts_done, bias_zero, edges_done, gate_slot_zero = (
            sem(n) for n in ("pool_step", "consts_done", "bias_zero", "edges_done", "gate_slot_zero"))
        sq_done, root_done, xn_done, xt_ready, xhi_done, xlo_done = (
            sem(n) for n in ("sq_done", "root_done", "xn_done", "xt_ready", "xhi_done", "xlo_done"))
        pads_zero, whi_done, wlo_done, proj_ready, act_took, gates_took, v_took = (
            sem(n) for n in ("pads_zero", "whi_done", "wlo_done", "proj_ready", "act_took", "gates_took", "v_took"))
        pooled, mixer_ready, ev_full = sem("pooled"), sem("mixer_ready"), sem("ev_full")
        g_abs, g_exp, g_ln, rows_ready, turned, dec_ready, cols_done, v_ones, state_zero = (
            sem(n) for n in ("g_abs", "g_exp", "g_ln", "rows_ready", "turned", "dec_ready", "cols_done", "v_ones",
                             "state_zero"))
        kq_ready, nm_ready, uk_done, wgt_done, s_done, kv_ready, num_done, state_done, h_done = (
            sem(n) for n in ("kq_ready", "nm_ready", "uk_done", "wgt_done", "s_done", "kv_ready", "num_done", "state_done", "h_done"))
        wo_load = [sem(f"wo_load{i}") for i in range(2)]
        wohi_done, wolo_done = sem("wohi_done"), sem("wolo_done")
        c_in = [sem(f"c_in{i}") for i in range(2)]
        g2_in = sem("g2_in")
        hsum_done, hsq_done, hss_done, hroot_done, hn_done, hT_ready, mixf_done, mixhi_done, mixlo_done = (
            sem(n) for n in ("hsum_done", "hsq_done", "hss_done", "hroot_done", "hn_done", "hT_ready", "mixf_done",
                             "mixhi_done", "mixlo_done"))
        out_ready, x1_done, x1root_done, xn2_done, xn2T_ready, xn2T_done, logits_ready = (
            sem(n) for n in ("out_ready", "x1_done", "x1root_done", "xn2_done", "xn2T_ready", "xn2T_done", "logits_ready"))
        x1_out = [sem(f"x1_out{i}") for i in range(2)]
        xn2_out = [sem(f"xn2_out{i}") for i in range(2)]
        list_out = [sem(f"list_out{i}") for i in range(2)]
        chosen_done, rank_ready, slots_done, count_ready, rounds_done, wexp_done, wts_done = (
            sem(n) for n in ("chosen_done", "rank_ready", "slots_done", "count_ready", "rounds_done", "wexp_done",
                             "wts_done"))
        e_load = [sem(f"e_load{i}") for i in range(NST)]
        ehi_done, elo_done, piece_used, row_load, row_done, rows_copied, gx_load, ext_ready, exhi_done, exlo_done = (
            sem(n) for n in ("ehi_done", "elo_done", "piece_used", "row_load", "row_done", "rows_copied", "gx_load",
                             "ext_ready", "exhi_done", "exlo_done"))
        sg_done, h_ready, ht_ready, hthi_done, htlo_done, y_left, y_right, y_out, row_step = (
            sem(n) for n in ("sg_done", "h_ready", "ht_ready", "hthi_done", "htlo_done", "y_left", "y_right", "y_out",
                             "row_step"))
        f_in = [sem(f"f_in{i}") for i in range(3)]
        f_out = [sem(f"f_out{i}") for i in range(2)]
        gf_in, f_sum, f_root, f_done = sem("gf_in"), sem("f_sum"), sem("f_root"), sem("f_done")
        pool_past = sem("pool_past")
        dve_step, act_step = sem("dve_step"), sem("act_step")

        block = ctx.enter_context(nc.Block())

        U, G, O, K, Q, VV = 0, NG, NG + 1, NG + 1 + H, NG + 1 + 2 * H, NG + 1 + 3 * H
        NSL = VV + H
        COL = {U: 0, Q: PW, K: PW + MW, VV: PW + 2 * MW, O: PW + 3 * MW}
        GATES = PW + 4 * MW
        N_EDGE = sum(w - 1 for w in WINDOWS)
        N_CONST = 20

        proj, mixer_after = [], {}
        for first, count, kind in ((U, NG, "u"), (G, 1, "g"), (O, H, "o"), (K, H, "k"), (Q, H, "q")):
            for s in range(len(SEGS)):
                proj += [(kind, first + c, s) for c in range(count)]
                if kind == "o" and s < 2:
                    mixer_after[len(proj) - 1] = (2 * s, 2 * s + 1)
        NPROJ = len(proj)

        last_use = {m: n + 1 for n, (_, m, _) in enumerate(proj)}

        def act_results(n):
            return sum(kind in "ukq" for kind, _, _ in proj[:n])

        def bank_free(eng, n):
            if n < 4:
                return
            m = n - 4
            if m < NPROJ and proj[m][0] == "g":
                eng.wait_ge(gates_took, proj[m][2] + 1)
            elif m < NPROJ and proj[m][0] == "o":
                eng.wait_ge(ev_full, place["o", proj[m][1] - O, proj[m][2]] + 1)
            elif m < NPROJ:
                eng.wait_ge(act_took, act_results(m + 1))
            else:
                eng.wait_ge(v_took, m - NPROJ + 1)

        ring = []
        for n, (kind, m, s) in enumerate(proj):
            if kind == "o":
                ring.append(("o", m - O, s))
            for g in mixer_after.get(n, ()):
                ring += [("a", g, s2) for s2 in range(len(SEGS))]
        place = {key: i for i, key in enumerate(ring)}

        def chunk_of(step, back):
            if not back:
                return step
            return C0 - 1 - step if step < C0 else NT - 1 - (step - C0)

        NU = 4 * NT

        def unit(n):
            step, pair, d = n // 4, n // 2 % 2, n % 2
            return step, pair, d, chunk_of(step, d)

        def carries(step):
            return step not in (C0 - 1, NT - 1)

        def wait(eng, s, value):
            if not isinstance(value, int) or value >= 1:
                eng.wait_ge(s, value)

        def load_half_steps(eng):
            eng.wait_ge(rounds_done, 1)
            return eng.value_load(half_steps[0:1, 0:1], min_val=0, max_val=E // 2 * (NT - 1)) + E // 2

        def gu_piece(i, c):
            if isinstance(i, int) and i == 0:
                return c, c, c % NRG, 1
            return 12 * i - 4 + c, (8 + c) % NST, (2 + c) % NRG, i + c // 4

        def down_piece(i, c):
            return 12 * i + 4 + c, 4 + c, (4 + c) % NRG, i + 1

        def last_piece(i, c):
            return 12 * i + 8 + c, 8 + c, (2 + c) % NRG, i + 1

        @block.sync
        def _(sp):
            def slice_in(m):
                if m >= 2:
                    sp.wait_ge(wlo_done, m - 1)
                if m == G:
                    sp.wait_ge(gate_slot_zero, 1)
                    for blk in range(4):
                        c = GATES + H * blk
                        sp.dma_start(w_st[:, m % 2, :, 32 * blk:32 * blk + H],
                                     w_in[0, :, c:c + H].rearrange("(p k) n -> p k n", k=KD)).then_inc(w_load[m % 2], 16)
                    return
                first = max(x for x in COL if x <= m)
                c = COL[first] + (m - first) * P
                sp.dma_start(w_st[:, m % 2, :, :],
                             w_in[0, :, c:c + P].rearrange("(p k) n -> p k n", k=KD)).then_inc(w_load[m % 2], 16)

            slice_in(0)
            slice_in(1)
            for dst, src in (
                (wpool[:, :, :], pool_w[0].rearrange("g c e -> c g e")),
                (pscale[:, :], pool_scale[0].rearrange("(g c) -> c g", c=P)),
                (hgain[:, :], head_norm_g[0].rearrange("(h c) -> c h", c=P)),
                (rw[:, :, 0:GR], router_group_w[0].rearrange("(p k) n -> p k n", k=KD)),
                (rw[:, :, GR:NL], router_expert_w[0].rearrange("(p k) g e -> p k (g e)", k=KD)),
                (rbias[:, 0:GR], router_group_b[0:1, :].broadcast_to([P, GR])),
                (rbias[:, GR:NL], router_expert_b[0:1].rearrange("a g e -> a (g e)").broadcast_to([P, E])),
            ):
                sp.dma_start(dst, src).then_inc(consts_in, 16)
            sp.wait_ge(bias_zero, 1)
            for d in range(2):
                for kind in range(2):
                    c = kind * 2 * H + d * H
                    sp.dma_start(gbias[32 * d:32 * d + H, kind:kind + 1],
                                 gate_b[0:1, c:c + H].rearrange("a h -> h a")).then_inc(consts_in, 16)
            for m in range(2, NSL):
                slice_in(m)
            for i in range(KD):
                if i < 2:
                    sp.wait_ge(wlo_done, NSL)
                else:
                    sp.wait_ge(wolo_done, i - 1)
                sp.dma_start(w_st[:, i % 2, :, :].rearrange("p k n -> p (k n)"),
                             w_out[0, i * P:(i + 1) * P, :]).then_inc(wo_load[i % 2], 16)
            for i in range(4):
                sp.wait_ge(ev_out[i], 16 * len(ring[i::4]))
            sp.wait_ge(h_done, NU)
            sp.wait_ge(state_done, NU)
            sp.dma_start(g2_b[:, :], norm2_g[0:1, :].broadcast_to([P, D])).then_inc(g2_in, 16)

            def x1_store(t):
                sp.wait_ge(x1_done, t + 1)
                sp.dma_start(x1_dram[t * P:(t + 1) * P, :], x1[:, t % 2, :]).then_inc(x1_out[t % 2], 16)

            for t in range(NT):
                if t >= 2:
                    sp.wait_ge(x1_done, t - 1)
                    sp.wait_ge(mixlo_done, t - 1)
                sp.dma_start(x_c[:, t % 2, :], tokens(t, x_prompt, x_sample)).then_inc(c_in[t % 2], 16)
                sp.dma_start(mixf[:, t % 2, 0:NG, :], pooled_dram[:, t * P:(t + 1) * P]
                             .rearrange("(g p) n -> p g n", p=P)).then_inc(c_in[t % 2], 16)
                sp.dma_start(og[:, t % 2, :, :], ogate_dram[:, t * P:(t + 1) * P]
                             .rearrange("(g p) n -> p g n", p=P)).then_inc(c_in[t % 2], 16)
                if t >= 2:
                    x1_store(t - 2)
            x1_store(NT - 2)
            x1_store(NT - 1)
            for i in range(2):
                sp.wait_ge(x1_out[i], 16 * (NT // 2))

            def piece_in(piece, src, d2):
                number, slot, _, _ = piece
                wait(sp, elo_done, number - NST + 1)
                dst = e_st[:, slot, :, :]
                sp.dma_start(dst if d2 else dst.rearrange("p a n -> p (a n)"), src).then_inc(e_load[slot], 16)

            def gu_in(i, c):
                w = expert_w_up if c % 2 else expert_w_gate
                kk = 2 * (c // 2)
                piece_in(gu_piece(i, c), w[0, bass.ds(i % E, 1), :, :]
                         .rearrange("a (p k) n -> p (a k) n", k=KD)[:, kk:kk + 2, :], True)

            def down_in(piece, e, c):
                piece_in(piece, expert_w_down[0, bass.ds(e % E, 1), :, :]
                         .rearrange("a (p k) n -> p (a k) n", k=KF)[:, c, :], False)

            sp.wait_ge(out_ready, NT)
            for c in range(8):
                gu_in(0, c)
            n_half = load_half_steps(sp)

            def step(i):
                for c in range(8):
                    gu_in(i, c)
                for c in range(4):
                    down_in(down_piece(i, c), i - 1, c)

            step(1)
            with sp.Fori(1, n_half) as j:
                step(2 * j)
                step(2 * j + 1)
            last = 2 * n_half - 1
            for c in range(4):
                down_in(last_piece(last, c), last, c)

            sp.wait_ge(y_out, 32 * n_half)
            sp.dma_start(gf_b[:, :], final_norm_g.rearrange("(a d) -> a d", a=1).broadcast_to([P, D])).then_inc(gf_in, 16)
            for t in range(NT + 1):
                if t < NT:
                    if t >= 3:
                        sp.wait_ge(f_done, t - 2)
                    for k in range(2):
                        sp.dma_start(f_y[:, t % 3, k, :],
                                     y_dram[k * T + t * P:k * T + (t + 1) * P, :]).then_inc(f_in[t % 3], 16)
                    sp.dma_start(f_x[:, t % 3, :], x1_dram[t * P:(t + 1) * P, :]).then_inc(f_in[t % 3], 16)
                if t >= 1:
                    sp.wait_ge(f_done, t)
                    sp.dma_start(tokens(t - 1, y_prompt, y_sample),
                                 f_o[:, (t - 1) % 2, :]).then_inc(f_out[(t - 1) % 2], 16)
            for i in range(2):
                sp.wait_ge(f_out[i], 16 * (NT // 2))

        @block.gpsimd
        def _(pool):
            def x_in_tile(t):
                if t >= 3:
                    pool.wait_ge(xn_done, t - 2)
                pool.dma_start(x_in[:, t % 3, :], tokens(t, x_prompt, x_sample)).then_inc(x_load[t % 3], 16)

            for t in range(3):
                x_in_tile(t)
                if t == 0:
                    pool.dma_start(g1_b[:, :], norm1_g[0:1, :].broadcast_to([P, D])).then_inc(g1_in, 16)
            pool.memset(gbias[:, :], 0.0).then_inc(bias_zero, 1)
            pool.memset(ident[:, :], 0.0).then_inc(pool_step, 1)
            pool.memset(epsc[:, :], EPS).then_inc(consts_done, 1)
            pool.memset(onec[:, :], 1.0).then_inc(consts_done, 1)
            pool.wait_ge(pool_step, 1)
            pool.affine_select(out=ident[:, :], in_=ident[:, :], compare_op=ALU.not_equal, fill=1.0, base=0,
                               pattern=[[-1, P]], channel_multiplier=1).then_inc(consts_done, 1)
            for t in range(3, NT):
                x_in_tile(t)
            pool.memset(zero_row[:, :], 0.0).then_inc(consts_done, 1)
            pool.memset(onesb[:, :], 1.0).then_inc(consts_done, 1)
            for tile, value in ((identb[:, :], 0.0), (maskb[:, :, :], 0.0), (laterb[:, :], 1.0), (sel[:, :, :], 0.0),
                                (edge[:, :, :], 1.0)):
                pool.memset(tile, value).then_inc(pool_step, 1)
            pool.wait_ge(pool_step, 6)
            pool.affine_select(out=identb[:, :], in_=identb[:, :], compare_op=ALU.not_equal, fill=1.0, base=0,
                               pattern=[[-1, P]], channel_multiplier=1).then_inc(consts_done, 1)
            for d, sign in enumerate((1, -1)):
                pool.affine_select(out=maskb[:, d, :], in_=maskb[:, d, :], compare_op=ALU.is_ge, fill=MASKED, base=0,
                                   pattern=[[sign, P]], channel_multiplier=-sign).then_inc(consts_done, 1)
            pool.affine_select(out=laterb[:, :], in_=laterb[:, :], compare_op=ALU.is_ge, fill=0.0, base=-1,
                               pattern=[[1, P]], channel_multiplier=-1).then_inc(consts_done, 1)
            for r in range(2 * H):
                pool.affine_select(out=sel[:, r, :], in_=sel[:, r, :], compare_op=ALU.not_equal, fill=1.0,
                                   base=-(32 * (r // H) + r % H), pattern=[[0, P]],
                                   channel_multiplier=1).then_inc(consts_done, 1)
            for g, w in enumerate(WINDOWS):
                for j in range(w // 2):
                    pool.memset(edge[:, g, j:j + 1], w / (j + w // 2)).then_inc(edges_done, 1)
                for j in range(w // 2 - 1):
                    pool.memset(edge[:, g, 15 - j:16 - j], w / (j + 1 + w // 2)).then_inc(edges_done, 1)
            pool.iota(rowval[:, :, :], pattern=[[T, 2], [P, NT]], base=0, channel_multiplier=1).then_inc(consts_done, 1)
            pool.iota(sentinel[:, :], pattern=[[0, E * CAP // 80 // P], [1, P]], base=2 * T,
                      channel_multiplier=0).then_inc(pool_step, 1)
            pool.iota(ramp_i[:, 0:EPG], pattern=[[-1, EPG]], base=EPG, channel_multiplier=0).then_inc(pool_step, 1)
            pool.iota(ramp_i[:, EPG:EPG + E], pattern=[[CAP, E]], base=0, channel_multiplier=0).then_inc(pool_step, 1)
            pool.wait_ge(pool_step, 9)
            pool.tensor_copy(ramp[:, :], ramp_i[:, 0:EPG]).then_inc(consts_done, 1)
            pool.tensor_copy(ebase[:, :], ramp_i[:, EPG:EPG + E]).then_inc(consts_done, 1)
            pool.dma_start(list_dram.rearrange("(q n) a -> q (n a)", q=80), sentinel[:, :]).then_inc(list_set, 16)

            for i, (kind, c, s) in enumerate(ring):
                a, n = SEGS[s]
                dram = ogate_dram if kind == "o" else pooled_dram
                pool.wait_ge(ev_full, i + 1)
                pool.dma_start(dram[c * P:(c + 1) * P, a:a + n], ev[:, i % 4, 0:n]).then_inc(ev_out[i % 4], 16)

            pool.wait_ge(list_set, 16)

            def entries_out(t):
                pool.wait_ge(slots_done, t + 1)
                for k in range(2):
                    pool.indirect_dma_start(
                        out=list_dram, out_offset=bass.IndirectOffsetOnAxis(ap=slot_i[:, t % 2, k:k + 1], axis=0),
                        in_=rowval[:, k, t:t + 1], in_offset=None).then_inc(list_out[t % 2], 16)

            for t in range(NT):
                pool.wait_ge(xn2_done, t + 1)
                pool.dma_start(xn2_dram[t * P:(t + 1) * P, :], xn2[:, t % 2, :]).then_inc(xn2_out[t % 2], 16)
                if t >= 2:
                    entries_out(t - 2)
            entries_out(NT - 2)
            entries_out(NT - 1)
            for i in range(2):
                pool.wait_ge(list_out[i], 16 * NT)
                pool.wait_ge(xn2_out[i], 16 * (NT // 2))

            def rows_in(i, b):
                wait(pool, rows_copied, i - 1)
                wait(pool, ext_ready, i - 1)
                pool.sem_inc(pool_past, 1)
                pool.dma_start(row_raw[:, b:b + 1],
                               list_dram[bass.ds((i % E) * CAP + (i // E) * P, P), :]).then_inc(row_load, 16)
                pool.wait_ge(row_done, i + 1)
                pool.sem_inc(pool_past, 1)
                pool.indirect_dma_start(
                    out=gx[:, b, :], out_offset=None, in_=xn2_dram,
                    in_offset=bass.IndirectOffsetOnAxis(ap=row_g[:, b:b + 1], axis=0)).then_inc(gx_load, 16)

            def rows_out(i, b):
                pool.wait_ge(y_left, i + 1)
                pool.wait_ge(y_right, i + 1)
                pool.sem_inc(pool_past, 1)
                pool.indirect_dma_start(
                    out=y_dram, out_offset=bass.IndirectOffsetOnAxis(ap=row_s[:, b:b + 1], axis=0),
                    in_=yo[:, b, :], in_offset=None).then_inc(y_out, 16)
                pool.wait_ge(y_out, 16 * (i + 1))

            rows_in(0, 0)
            rows_in(1, 1)
            rows_in(2, 0)
            n_half = load_half_steps(pool)
            with pool.Fori(1, n_half) as j:
                rows_in(2 * j + 1, 1)
                rows_out(2 * j - 2, 0)
                rows_in(2 * j + 2, 0)
                rows_out(2 * j - 1, 1)
            rows_out(2 * n_half - 2, 0)
            rows_out(2 * n_half - 1, 1)

        @block.tensor
        def _(pe):
            def product3(out, a, b, start, stop):
                (a_hi, a_lo), (b_hi, b_lo) = a, b
                pe.matmul(out, a_hi, b_hi, start=start, stop=False)
                pe.matmul(out, a_hi, b_lo, start=False, stop=False)
                return pe.matmul(out, a_lo, b_hi, start=False, stop=stop)

            def x_transposes(t):
                pe.wait_ge(xn_done, t + 1)
                if t >= 2:
                    pe.wait_ge(xlo_done, t - 1)
                for k in range(KD):
                    last = pe.transpose(psum[:, 4 + 2 * (t % 2) + k // 4, (k % 4) * P:(k % 4 + 1) * P],
                                        xn[:, t % 2, k:D:KD], ident[:, :])
                last.then_inc(xt_ready, 1)

            pe.wait_ge(consts_done, 3)
            for t in range(4):
                x_transposes(t)

            def mix_pooled(g):
                pe.wait_ge(pooled, g + 1)
                for s in range(len(SEGS)):
                    j = 3 * g + s - 4
                    if j >= 0:
                        pe.wait_ge(ev_full, place["a", j // 3, j % 3] + 1)
                    out = psum[:, 4 + (3 * g + s) % 4, :]
                    a, n = SEGS[s]
                    parts = [(0, 0, S0), (S0, 1, a + n - S0)] if s == 0 else [(0, 1, n)]
                    for col, seq, m in parts:
                        first = pos[seq] + a + col - (S0 if seq else 0)
                        last = pe.matmul(out[:, col:col + m], wpool[:, g, :], u_ext[:, g, first:first + m],
                                         start=True, stop=True)
                    last.then_inc(mixer_ready, 1)

            pe.wait_ge(consts_in, 16 * 11)
            for n, (kind, m, s) in enumerate(proj):
                a, length = SEGS[s]
                pe.wait_ge(wlo_done, m + 1)
                pe.wait_ge(xlo_done, (a + length) // P)
                bank_free(pe, n)
                for k in range(KD):
                    last = product3(psum[:, n % 4, 0:length], (w_hi[:, m % 4, k, :], w_lo[:, m % 4, k, :]),
                                    (xT_hi[:, k, a:a + length], xT_lo[:, k, a:a + length]), k == 0, k == KD - 1)
                last.then_inc(proj_ready, 1)
                if n < NT - 4:
                    x_transposes(4 + n)
                for g in mixer_after.get(n, ()):
                    mix_pooled(g)
                if kind == "o" and n + 1 < NPROJ and proj[n + 1][0] == "k":
                    pe.wait_ge(ev_full, place["a", NG - 1, 2] + 1)
                    pe.wait_ge(rows_ready, 1)
                    for c in range(NT):
                        for kind4, row in enumerate((g_m, g_e, g_i, g_b)):
                            o = (c % 3) * 144 + kind4 * 36
                            last = pe.transpose(psum[:, 4 + c // 3, o:o + 36], row[0:36, c * P:(c + 1) * P],
                                                ident[0:36, 0:36])
                    last.then_inc(turned, 1)
                    for r in range(2 * H):
                        last = pe.matmul(psum[:, 7, 256 + r * NT:256 + (r + 1) * NT], sel[:, r, :], mlast[:, :],
                                         start=True, stop=True)
                    last.then_inc(dec_ready, 1)
            for t in range(NT):
                n = NPROJ + t
                if t == 0:
                    pe.wait_ge(wlo_done, NSL)
                bank_free(pe, n)
                for k in range(KD):
                    tok = slice(t * P, (t + 1) * P)
                    last = product3(psum[:, n % 4, :], (xT_hi[:, k, tok], xT_lo[:, k, tok]),
                                    (w_hi[:, :, k, :], w_lo[:, :, k, :]), k == 0, k == KD - 1)
                last.then_inc(proj_ready, 1)

            def unit_scores(n):
                step, pair, d, ck = unit(n)
                tok = slice(ck * P, (ck + 1) * P)
                heads = (2 * pair, 2 * pair + 1)
                if n >= 2:
                    pe.wait_ge(state_done, n - 1)
                    pe.wait_ge(wgt_done, n - 1)
                for hh_, h in enumerate(heads):
                    pe.transpose(psum[:, 4 * d, hh_ * P:(hh_ + 1) * P], kT[:, h, tok], ident[:, :])
                for hh_, h in enumerate(heads):
                    last = pe.matmul(psum[:, 4 * d, (2 + hh_) * P:(3 + hh_) * P], kT[:, h, tok], qT[:, h, tok],
                                     start=True, stop=True)
                last.then_inc(kq_ready, 1)
                for hh_, h in enumerate(heads):
                    out = psum[:, 4 * d + 1, hh_ * P:(hh_ + 1) * P]
                    pe.matmul(out, identb[:, :], maskb[:, d, :], start=True, stop=False)
                    last = pe.matmul(out, sel[:, d * H + h, :], negm[:, tok], start=False, stop=True)
                last.then_inc(nm_ready, 1)

            def unit_rows(n):
                step, pair, d, ck = unit(n)
                tok = slice(ck * P, (ck + 1) * P)
                heads = (2 * pair, 2 * pair + 1)
                if n >= 2:
                    pe.wait_ge(num_done, n - 1)
                if n >= 4:
                    pe.wait_ge(state_done, n - 3)
                for hh_, h in enumerate(heads):
                    pe.matmul(psum[:, 4 * d + 3, hh_ * (P + 1):(hh_ + 1) * (P + 1)], qT[:, h, tok],
                              state[:, d, h, :], start=True, stop=True)
                pe.wait_ge(s_done, n + 1)
                pe.wait_ge(uk_done, n + 1)
                for hh_, h in enumerate(heads):
                    last = pe.matmul(psum[:, 4 * d + 2, hh_ * (P + 1):(hh_ + 1) * (P + 1)], sT[:, d, hh_, :],
                                     v[:, ck, h, :], start=True, stop=True)
                if carries(step):
                    for hh_, h in enumerate(heads):
                        last = pe.matmul(psum[:, 4 * d, hh_ * (P + 1):(hh_ + 1) * (P + 1)], uk[:, d, hh_, :],
                                         v[:, ck, h, :], start=True, stop=True)
                last.then_inc(kv_ready, 1)

            pe.wait_ge(v_took, NT)
            pe.wait_ge(v_ones, 1)
            pe.wait_ge(state_zero, 1)
            pe.wait_ge(cols_done, 1)
            unit_scores(0)
            for n in range(NU):
                if n + 1 < NU:
                    unit_scores(n + 1)
                unit_rows(n)

            def h_transposes(t):
                pe.wait_ge(hn_done, t + 1)
                for k in range(H):
                    last = pe.transpose(psum[:, 4, k * P:(k + 1) * P], hsum[:, k * P:(k + 1) * P], ident[:, :])
                last.then_inc(hT_ready, 1)

            def out_rows(t):
                pe.wait_ge(mixlo_done, t + 1)
                if t >= 2:
                    pe.wait_ge(x1_done, t - 1)
                for k in range(KD):
                    for half in range(2):
                        c = slice(half * 512, (half + 1) * 512)
                        last = product3(psum[:, 2 * (t % 2) + half, :], (mix_hi[:, t % 2, k, :], mix_lo[:, t % 2, k, :]),
                                        (wo_hi[:, k, c], wo_lo[:, k, c]), k == 0, k == KD - 1)
                last.then_inc(out_ready, 1)

            def xn2_transposes(t):
                pe.wait_ge(xn2_done, t + 1)
                if t >= 1:
                    pe.wait_ge(xn2T_done, t)
                for k in range(KD):
                    last = pe.transpose(psum[:, 5 + k // 4, (k % 4) * P:(k % 4 + 1) * P], xn2[:, t % 2, k:D:KD],
                                        ident[:, :])
                last.then_inc(xn2T_ready, 1)

            def router(t):
                pe.wait_ge(xn2T_done, t + 1)
                if t >= 1:
                    pe.wait_ge(slots_done, t)
                for k in range(KD):
                    last = pe.matmul(psum[:, 7, 0:NL], xn2T[:, k, :], rw[:, k, :], start=(k == 0), stop=(k == KD - 1))
                last.then_inc(logits_ready, 1)

            def ranks(t):
                pe.wait_ge(chosen_done, t + 1)
                for t2 in range(t):
                    pe.matmul(psum[:, 7, 64:64 + E], onesb[:, :], chosen[:, t2, :], start=(t2 == 0), stop=False)
                pe.matmul(psum[:, 7, 64:64 + E], laterb[:, :], chosen[:, t, :], start=(t == 0),
                          stop=True).then_inc(rank_ready, 1)

            pe.wait_ge(wolo_done, KD)
            pe.wait_ge(num_done, NU)
            pe.wait_ge(consts_done, N_CONST)
            for t in range(-1, NT + 2):
                if 0 <= t + 1 < NT:
                    h_transposes(t + 1)
                if 0 <= t - 2 < NT:
                    router(t - 2)
                if 0 <= t < NT:
                    out_rows(t)
                if 0 <= t - 1 < NT:
                    xn2_transposes(t - 1)
                if 0 <= t - 2 < NT:
                    ranks(t - 2)
            pe.wait_ge(slots_done, NT)
            for t in range(NT):
                last = pe.matmul(psum[:, 7, 128:128 + E], onesb[:, :], chosen[:, t, :], start=(t == 0), stop=(t == NT - 1))
            last.then_inc(count_ready, 1)

            def ex_transposes(i, b):
                pe.wait_ge(gx_load, 16 * (i + 1))
                wait(pe, exlo_done, i)
                for k in range(KD):
                    last = pe.transpose(psum[:, 2 + k // 4, (k % 4) * P:(k % 4 + 1) * P], gx[:, b, k:D:KD], ident[:, :])
                last.then_inc(ext_ready, 1)

            def gate_up(i, b):
                pe.wait_ge(exlo_done, i + 1)
                wait(pe, h_ready, i)
                for c in range(8):
                    number, _, r, _ = gu_piece(i, c)
                    pe.wait_ge(elo_done, number + 1)
                    for kk in range(2):
                        k = 2 * (c // 2) + kk
                        last = product3(psum[:, c % 2, :], (ex_hi[:, b, k, :], ex_lo[:, b, k, :]),
                                        (e_hi[:, r, kk, :], e_lo[:, r, kk, :]), k == 0, k == KD - 1)
                    last.then_inc(piece_used, 1)

            def down(piece, i):
                pe.wait_ge(htlo_done, i + 1)
                wait(pe, y_left, i)
                wait(pe, y_right, i)
                for c in range(4):
                    number, _, r, _ = piece(c)
                    pe.wait_ge(elo_done, number + 1)
                    for half in range(2):
                        last = product3(psum[:, 4 + half, :], (ht_hi[:, c, :], ht_lo[:, c, :]),
                                        (e_hi[:, r, half, :], e_lo[:, r, half, :]), c == 0, c == 3)
                    last.then_inc(piece_used, 1)

            def h_turn(i):
                pe.wait_ge(h_ready, i + 1)
                for k in range(KF):
                    last = pe.transpose(psum[:, 6, k * P:(k + 1) * P], hh[:, k:F:KF], ident[:, :])
                last.then_inc(ht_ready, 1)

            def step(i, b):
                gate_up(i, b)
                ex_transposes(i + 1, 1 - b)
                down(lambda c: down_piece(i, c), i - 1)
                h_turn(i)

            ex_transposes(0, 0)
            gate_up(0, 0)
            ex_transposes(1, 1)
            h_turn(0)
            step(1, 1)
            n_half = load_half_steps(pe)
            with pe.Fori(1, n_half) as j:
                step(2 * j, 0)
                step(2 * j + 1, 1)
            last_i = 2 * n_half - 1
            down(lambda c: last_piece(last_i, c), last_i)

        @block.scalar
        def _(act):
            steps = [0]

            def link(ins):
                steps[0] += 1
                ins.then_inc(act_step, 1)
                act.wait_ge(act_step, steps[0])

            def w_part(m):
                act.wait_ge(w_load[m % 2], 16 * (m // 2 + 1 + (3 if m >= G and m % 2 == G % 2 else 0)))
                if m >= 4:
                    act.wait_ge(proj_ready, last_use[m - 4])
                act.activation(w_hi[:, m % 4, :, :], w_st[:, m % 2, :, :], ACT.Copy).then_inc(whi_done, 1)

            def x_part(t):
                act.wait_ge(xt_ready, t + 1)
                b = 4 + 2 * (t % 2)
                for half in range(2):
                    ins = act.activation(xT_hi[:, 4 * half:4 * half + 4, t * P:(t + 1) * P],
                                         psum[:, b + half, :].rearrange("p (k n) -> p k n", k=4), ACT.Copy)
                ins.then_inc(xhi_done, 1)

            def ring_slot(i):
                if i >= 4:
                    act.wait_ge(ev_out[i % 4], 16 * (i // 4))

            def take(n):
                kind, m, s = proj[n]
                a, length = SEGS[s]
                src = psum[:, n % 4, 0:length]
                if kind != "g":
                    act.wait_ge(proj_ready, n + 1)
                if kind == "u":
                    act.wait_ge(pads_zero, 1)
                    parts = [(0, pos[0], S0), (S0, pos[1], length - S0)] if s == 0 else [(0, pos[1] + a - S0, length)]
                    for col, first, w in parts:
                        ins = act.activation(u_ext[:, m, first:first + w], src[:, col:col + w], ACT.Copy)
                    ins.then_inc(act_took, 1)
                elif kind == "o":
                    i = place["o", m - O, s]
                    ring_slot(i)
                    act.activation(ev[:, i % 4, 0:length], src, ACT.Sigmoid).then_inc(ev_full, 1)
                elif kind == "k":
                    if m == K and s == 0:
                        act.wait_ge(dec_ready, 1)
                    act.activation(kT[:, m - K, a:a + length], src, ACT.Copy, scale=float(P) ** -0.5).then_inc(act_took, 1)
                elif kind == "q":
                    act.activation(qT[:, m - Q, a:a + length], src, ACT.Copy).then_inc(act_took, 1)
                if s == len(SEGS) - 1 and m + 4 < NSL:
                    w_part(m + 4)
                if kind == "o" and m == O + 1 and s == 0:
                    act.wait_ge(g_abs, 1)
                    act.activation(g_e[:, :], g_e[:, :], ACT.Exp).then_inc(g_exp, 1)
                    act.wait_ge(g_exp, 1)
                    act.activation(g_e[:, :], g_e[:, :], ACT.Ln, bias=onec[0:64, :], scale=1.0).then_inc(g_ln, 1)
                for g in mixer_after.get(n, ()):
                    for s2 in range(len(SEGS)):
                        i = place["a", g, s2]
                        ring_slot(i)
                        act.wait_ge(mixer_ready, 3 * g + s2 + 1)
                        act.activation(ev[:, i % 4, 0:SEGS[s2][1]], psum[:, 4 + (3 * g + s2) % 4, 0:SEGS[s2][1]],
                                       ACT.Copy, scale=pscale[:, g:g + 1]).then_inc(ev_full, 1)
            act.wait_ge(consts_done, 2)
            for t in range(NT):
                act.wait_ge(x_load[t % 3], 16 * (t // 3 + 1))
                act.activation(junk[:, :], x_in[:, t % 3, :], ACT.Square,
                               accum_out=stat[:, 0, t:t + 1]).then_inc(sq_done, 1)
                act.wait_ge(sq_done, t + 1)
                act.activation(stat[:, 1, t:t + 1], stat[:, 0, t:t + 1], ACT.Sqrt, bias=epsc[:, :],
                               scale=1.0 / D).then_inc(root_done, 1)
                if t == NT - 1:
                    take(0)
                if t >= 1:
                    x_part(t - 1)
                if 2 <= t < 6:
                    w_part(t - 2)
            take(1)
            x_part(NT - 1)
            for n in range(2, NPROJ):
                take(n)

            act.wait_ge(turned, 1)
            act.wait_ge(dec_ready, 1)
            for b in range(4):
                cs = min(3, NT - 3 * b)
                for kind4 in range(4):
                    for d in range(2):
                        src = psum[:, 4 + b, 0:cs * 144].rearrange("p (c r) -> p c r", c=cs)
                        o = kind4 * 36 + 32 * d
                        act.activation(cols[:, 3 * b:3 * b + cs, kind4, d * H:(d + 1) * H], src[:, :, o:o + H],
                                       ACT.Exp if kind4 else ACT.Copy)
            act.activation(decay[:, :, :], psum[:, 7, 256:256 + 2 * H * NT].rearrange("p (r c) -> p r c", r=2 * H),
                           ACT.Exp).then_inc(cols_done, 1)
            for t in range(NT):
                act.wait_ge(proj_ready, NPROJ + t + 1)
                src = psum[:, (NPROJ + t) % 4, :].rearrange("p (h n) -> p h n", h=H)
                if t == 0:
                    act.wait_ge(v_ones, 1)
                act.activation(v[:, t, 0:H - 1, 0:P], src[:, 1:H, :], ACT.Copy)
                act.activation(v[:, t, H - 1, 0:P], src[:, 0, :], ACT.Copy).then_inc(v_took, 1)
            for i in range(4):
                act.wait_ge(ev_out[i], 16 * len(ring[i::4]))

            act.wait_ge(cols_done, 1)
            for n in range(NU):
                step, pair, d, ck = unit(n)
                act.wait_ge(kq_ready, n + 1)
                if n >= 2:
                    act.wait_ge(kv_ready, n - 1)
                for hh_ in range(2):
                    r = d * H + 2 * pair + hh_
                    ins = act.activation(uk[:, d, hh_, :], psum[:, 4 * d, hh_ * P:(hh_ + 1) * P], ACT.Copy,
                                         scale=cols[:, ck, 3, r:r + 1])
                ins.then_inc(uk_done, 1)
                act.wait_ge(nm_ready, n + 1)
                if n >= 2:
                    act.wait_ge(s_done, n - 1)
                for hh_ in range(2):
                    r = d * H + 2 * pair + hh_
                    ins = act.activation(wgt[:, d, hh_, :], psum[:, 4 * d + 1, hh_ * P:(hh_ + 1) * P], ACT.Exp,
                                         bias=cols[:, ck, 0, r:r + 1])
                ins.then_inc(wgt_done, 1)
                if n % 4 == 3 and step < KD:
                    i = step
                    act.wait_ge(wo_load[i % 2], 16 * (i // 2 + 1))
                    act.activation(wo_hi[:, i, :], w_st[:, i % 2, :, :].rearrange("p k n -> p (k n)"),
                                   ACT.Copy).then_inc(wohi_done, 1)

            def h_root(t):
                act.wait_ge(hsum_done, t + 1)
                act.activation(hsq[:, :], hsum[:, :], ACT.Square).then_inc(hsq_done, 1)
                act.wait_ge(hss_done, t + 1)
                act.activation(rt[:, 4:8], rt[:, 0:4], ACT.Sqrt, bias=epsc[:, :], scale=1.0 / P).then_inc(hroot_done, 1)
                act.wait_ge(mixf_done, t + 1)
                if t >= 2:
                    act.wait_ge(out_ready, t - 1)
                act.activation(mix_hi[:, t % 2, :, :], mixf[:, t % 2, :, :], ACT.Copy).then_inc(mixhi_done, 1)

            act.wait_ge(h_done, NU)
            act.wait_ge(wolo_done, KD)
            for t in range(-1, NT + 1):
                if t + 1 < NT:
                    h_root(t + 1)
                if 0 <= t < NT:
                    act.wait_ge(x1_done, t + 1)
                    if t >= 1:
                        act.wait_ge(x1root_done, t)
                    link(act.activation(sq_c[:, :], x1[:, t % 2, :], ACT.Square, accum_out=stat[:, 2, t:t + 1]))
                    act.activation(stat[:, 3, t:t + 1], stat[:, 2, t:t + 1], ACT.Sqrt, bias=epsc[:, :],
                                   scale=1.0 / D).then_inc(x1root_done, 1)
                if 0 <= t - 1:
                    act.wait_ge(xn2T_ready, t)
                    if t >= 2:
                        act.wait_ge(logits_ready, t - 1)
                    for half in range(2):
                        ins = act.activation(xn2T[:, 4 * half:4 * half + 4, :],
                                             psum[:, 5 + half, :].rearrange("p (k n) -> p k n", k=4), ACT.Copy)
                    ins.then_inc(xn2T_done, 1)
            act.wait_ge(chosen_done, NT)
            act.activation(rgs[:, :, :], rgs[:, :, :], ACT.Exp)
            act.activation(rd21[:, :], rd21[:, :], ACT.Exp).then_inc(wexp_done, 1)

            def hi_part(piece):
                number, slot, r, loads = piece
                act.wait_ge(e_load[slot], 16 * loads)
                wait(act, piece_used, number - NRG + 1)
                act.activation(e_hi[:, r, :, :], e_st[:, slot, :, :], ACT.Copy).then_inc(ehi_done, 1)

            def ex_hi_part(i, b):
                act.wait_ge(ext_ready, i + 1)
                for half in range(2):
                    ins = act.activation(ex_hi[:, b, 4 * half:4 * half + 4, :],
                                         psum[:, 2 + half, :].rearrange("p (k n) -> p k n", k=4), ACT.Copy)
                ins.then_inc(exhi_done, 1)

            def ht_hi_part(i):
                act.wait_ge(ht_ready, i + 1)
                act.activation(ht_hi[:, :, :], psum[:, 6, :].rearrange("p (k n) -> p k n", k=KF),
                               ACT.Copy).then_inc(hthi_done, 1)

            def y_half(i, b, whole):
                act.wait_ge(piece_used, whole)
                act.activation(yo[:, b, 0:512], psum[:, 4, :], ACT.Copy).then_inc(y_left, 1)

            def silu(i):
                act.wait_ge(piece_used, gu_piece(i, 7)[0] + 1)
                wait(act, h_ready, i)
                act.activation(sg[:, :], psum[:, 0, :], ACT.Silu).then_inc(sg_done, 1)

            def step(i, b):
                for c in range(2):
                    hi_part(gu_piece(i, c))
                ht_hi_part(i - 1)
                hi_part(gu_piece(i, 2))
                if not isinstance(i, int) or i >= 2:
                    y_half(i - 2, b, down_piece(i - 1, 3)[0] + 1)
                for c in range(3, 8):
                    hi_part(gu_piece(i, c))
                for c in range(2):
                    hi_part(down_piece(i, c))
                silu(i)
                ex_hi_part(i + 1, 1 - b)
                for c in range(2, 4):
                    hi_part(down_piece(i, c))

            act.wait_ge(rounds_done, 1)
            for c in range(4):
                hi_part(gu_piece(0, c))
            ex_hi_part(0, 0)
            for c in range(4, 8):
                hi_part(gu_piece(0, c))
            silu(0)
            ex_hi_part(1, 1)
            step(1, 1)
            n_half = load_half_steps(act)
            with act.Fori(1, n_half) as j:
                step(2 * j, 0)
                step(2 * j + 1, 1)
            last_i = 2 * n_half - 1
            ht_hi_part(last_i)
            y_half(last_i - 1, 0, down_piece(last_i, 3)[0] + 1)
            for c in range(4):
                hi_part(last_piece(last_i, c))
            y_half(last_i, 1, last_piece(last_i, 3)[0] + 1)

            for t in range(NT):
                act.wait_ge(f_sum, t + 1)
                if t >= 1:
                    act.wait_ge(f_root, t)
                link(act.activation(f_sq[:, :], f_x[:, t % 3, :], ACT.Square, accum_out=wts[:, 2, t:t + 1]))
                act.activation(wts[:, 3, t:t + 1], wts[:, 2, t:t + 1], ACT.Sqrt, bias=epsc[:, :],
                               scale=1.0 / D).then_inc(f_root, 1)

        @block.vector
        def _(dve):
            steps = [0]

            def link(ins):
                steps[0] += 1
                ins.then_inc(dve_step, 1)
                dve.wait_ge(dve_step, steps[0])

            def w_part(m):
                dve.wait_ge(whi_done, m + 1)
                dve.tensor_tensor(w_lo[:, m % 4, :, :], w_st[:, m % 2, :, :], w_hi[:, m % 4, :, :].bitcast(F32),
                                  ALU.subtract).then_inc(wlo_done, 1)
                if m == G - 2:
                    dve.wait_ge(wlo_done, m + 1)
                    dve.memset(w_st[:, G % 2, :, :], 0.0).then_inc(gate_slot_zero, 1)

            def x_part(t):
                dve.wait_ge(xhi_done, t + 1)
                b = 4 + 2 * (t % 2)
                for half in range(2):
                    k = slice(4 * half, 4 * half + 4)
                    ins = dve.tensor_tensor(xT_lo[:, k, t * P:(t + 1) * P],
                                            psum[:, b + half, :].rearrange("p (k n) -> p k n", k=4),
                                            xT_hi[:, k, t * P:(t + 1) * P].bitcast(F32), ALU.subtract)
                ins.then_inc(xlo_done, 1)

            for first, width in ((0, 8), (pos[0] + S0, 8), (pos[1] + S1, 8)):
                ins = dve.memset(u_ext[:, :, first:first + width], 0.0)
            ins.then_inc(pads_zero, 1)
            dve.wait_ge(g1_in, 16)
            for t in range(NT):
                dve.wait_ge(root_done, t + 1)
                link(dve.reciprocal(stat[:, 1, t:t + 1], stat[:, 1, t:t + 1]))
                if t >= 2:
                    dve.wait_ge(xt_ready, t - 1)
                dve.scalar_tensor_tensor(out=xn[:, t % 2, :], in0=x_in[:, t % 3, :], scalar=stat[:, 1, t:t + 1],
                                         in1=g1_b[:, :], op0=ALU.mult, op1=ALU.mult).then_inc(xn_done, 1)
                if t >= 1:
                    x_part(t - 1)
                if 2 <= t < 6:
                    w_part(t - 2)
            x_part(NT - 1)

            def pool_group(g):
                w = WINDOWS[g]
                dve.wait_ge(act_took, 2 * NG + g + 1)
                wait(dve, pooled, g)
                src, bufs, r = u_ext[:, g, :], (ps_a, ps_b), 1
                link(dve.tensor_tensor(ps_a[:, 1:PADW], src[:, 0:PADW - 1], src[:, 1:PADW], ALU.add))
                lo, hi, cur = 1, PADW, 0
                while 2 * r < w:
                    lo, hi = lo + r, hi - r
                    link(dve.tensor_tensor(bufs[1 - cur][:, lo:hi], bufs[cur][:, lo - r:hi - r],
                                           bufs[cur][:, lo + r:hi + r], ALU.add))
                    cur, r = 1 - cur, 2 * r
                sums = bufs[cur]
                for seq, length in enumerate((S0, S1)):
                    for c, e in ((pos[seq], 0), (pos[seq] + length - 8, 8)):
                        ins = dve.tensor_tensor(sums[:, c:c + 8], sums[:, c:c + 8], edge[:, g, e:e + 8], ALU.mult)
                link(ins)
                for seq, length in enumerate((S0, S1)):
                    a = pos[seq]
                    ins = dve.scalar_tensor_tensor(out=u_ext[:, g, a:a + length], in0=sums[:, a:a + length],
                                                   scalar=1.0 / w, in1=u_ext[:, g, a:a + length],
                                                   op0=ALU.mult, op1=ALU.subtract)
                ins.then_inc(pooled, 1)

            def by_direction(fn):
                fn(slice(0, 32), slice(0, T), slice(0, T))
                ins = None
                for a, b in ((0, S0), (S0, T)):
                    rev = slice(b - 1, a - 1 if a else None, -1)
                    ins = fn(slice(32, 64), slice(a, b), rev)
                return ins

            def turn(dst, src):
                return by_direction(lambda r, o, i: dve.tensor_copy(dst[r, o], src[r, i]))

            def ends(x):
                return x[:, :].rearrange("p (c n) -> p c n", n=P)[:, :, P - 1]

            def starts(x):
                return x[:, :].rearrange("p (c n) -> p c n", n=P)[:, :, 0]

            def per_chunk(x):
                return x[:, :].unsqueeze(2).broadcast_to([64, NT, P])

            def chunked(x):
                return x[:, :].rearrange("p (c n) -> p c n", n=P)

            def gates_in(s, n):
                a, length = SEGS[s]
                dve.wait_ge(proj_ready, n + 1)
                if s == 0:
                    dve.wait_ge(consts_in, 16 * 11)
                dve.tensor_scalar(g_i[:, a:a + length], psum[0:64, n % 4, 0:length], gbias[:, 0:1], None, ALU.add)
                dve.tensor_scalar(g_f[:, a:a + length], psum[64:P, n % 4, 0:length], gbias[:, 1:2], None,
                                  ALU.add).then_inc(gates_took, 1)

            def gate_rows():
                dve.wait_ge(g_ln, 1)
                link(dve.scalar_tensor_tensor(out=g_f[:, :], in0=g_f[:, :], scalar=0.0, in1=g_e[:, :],
                                              op0=ALU.min, op1=ALU.subtract))
                turn(g_b, g_f)
                link(turn(g_e, g_i))
                for c in range(NT):
                    ins = dve.tensor_tensor_scan(g_f[:, c * P:(c + 1) * P], g_b[:, c * P:(c + 1) * P],
                                                 zero_row[:, :], 0.0, ALU.add, ALU.add)
                link(ins)
                dve.tensor_tensor(g_e[:, :], g_e[:, :], g_f[:, :], ALU.subtract)
                dve.memset(mprev[:, :], 0.0)
                link(dve.memset(g_b[:, :], 0.0))
                b_end, move = ends(g_f), starts(g_b)
                dve.tensor_copy(move[:, 1:C0], b_end[:, 0:C0 - 1])
                link(dve.tensor_copy(move[:, C0 + 1:NT], b_end[:, C0:NT - 1]))
                for a, b in ((0, S0), (S0, T)):
                    ins = dve.tensor_tensor_scan(g_m[:, a:b], g_b[:, a:b], g_e[:, a:b], 0.0, ALU.add, ALU.max)
                link(ins)
                m_end = ends(g_m)
                for a, b in ((0, C0), (C0, NT)):
                    dve.tensor_tensor(mprev[:, a + 1:b], m_end[:, a:b - 1], b_end[:, a:b - 1], ALU.add)
                link(dve.tensor_copy(mlast[:, :], m_end))
                dve.wait_ge(list_set, 16)
                by_direction(lambda r, o, i: dve.tensor_scalar(negm[r, o], g_m[r, i], -1.0, None, ALU.mult))
                dve.tensor_tensor(chunked(g_i), per_chunk(mprev), chunked(g_m), ALU.subtract)
                link(dve.scalar_tensor_tensor(out=g_b[:, :], in0=g_f[:, :], scalar=-1.0, in1=g_m[:, :],
                                              op0=ALU.mult, op1=ALU.subtract))
                link(dve.tensor_tensor(chunked(g_f), chunked(g_e), per_chunk(mlast), ALU.subtract))
                link(turn(g_m, g_e))
                link(turn(g_e, g_i))
                link(turn(g_i, g_b))
                turn(g_b, g_f)
                dve.tensor_tensor(mlast[:, :], mprev[:, :], mlast[:, :], ALU.subtract).then_inc(rows_ready, 1)

            for n, (kind, m, s) in enumerate(proj):
                if kind == "g":
                    gates_in(s, n)
                if s == len(SEGS) - 1 and m + 4 < NSL:
                    w_part(m + 4)
                if kind == "g" and s == len(SEGS) - 1:
                    dve.wait_ge(gates_took, 3)
                    dve.scalar_tensor_tensor(out=g_e[:, :], in0=g_f[:, :], scalar=-1.0, in1=g_f[:, :],
                                             op0=ALU.mult, op1=ALU.min).then_inc(g_abs, 1)
                    dve.wait_ge(edges_done, N_EDGE)
                    pool_group(0)
                    pool_group(1)
                    gate_rows()
                    pool_group(2)
                    pool_group(3)
            dve.wait_ge(dec_ready, 1)
            dve.memset(v[:, :, :, P:P + 1], 1.0).then_inc(v_ones, 1)
            dve.wait_ge(proj_ready, NPROJ + NT)
            dve.memset(state[:, :, :, :], 0.0).then_inc(state_zero, 1)

            def pair_of(x):
                return x[:, 0:2 * (P + 1)].rearrange("p (h n) -> p h n", h=2)

            def weighted(n):
                step, pair, d, ck = unit(n)
                dve.wait_ge(wgt_done, n + 1)
                if n >= 2:
                    dve.wait_ge(kv_ready, n - 1)
                dve.tensor_tensor(sT[:, d, :, :], psum[:, 4 * d, 2 * P:4 * P].rearrange("p (h n) -> p h n", h=2),
                                  wgt[:, d, :, :], ALU.mult).then_inc(s_done, 1)

            def heads_out(n):
                step, pair, d, ck = unit(n)
                r = d * H + 2 * pair
                dve.wait_ge(kv_ready, n + 1)
                if carries(step):
                    for hh_ in range(2):
                        ins = dve.scalar_tensor_tensor(
                            out=state[:, d, 2 * pair + hh_, :], in0=state[:, d, 2 * pair + hh_, :],
                            scalar=decay[:, r + hh_, step:step + 1],
                            in1=psum[:, 4 * d, hh_ * (P + 1):(hh_ + 1) * (P + 1)], op0=ALU.mult, op1=ALU.add)
                else:
                    ins = dve.memset(state[:, d, 2 * pair:2 * pair + 2, :], 0.0)
                ins.then_inc(state_done, 1)
                wait(dve, h_done, n - 1)
                link(dve.tensor_tensor(tq[:, d, :, :], pair_of(psum[:, 4 * d + 3, :]),
                                       cols[:, ck, 1, r:r + 2].unsqueeze(2).broadcast_to([P, 2, P + 1]), ALU.mult))
                dve.tensor_tensor(tq[:, d, :, :], tq[:, d, :, :], pair_of(psum[:, 4 * d + 2, :]), ALU.add).then_inc(num_done, 1)
                dve.wait_ge(num_done, n + 1)
                link(dve.tensor_tensor(dn[:, d, :], tq[:, d, :, P], cols[:, ck, 2, r:r + 2], ALU.max))
                link(dve.scalar_tensor_tensor(out=dn[:, d, :], in0=tq[:, d, :, P], scalar=-1.0,
                                              in1=dn[:, d, :], op0=ALU.mult, op1=ALU.max))
                link(dve.reciprocal(rdn[:, d, :], dn[:, d, :]))
                dve.tensor_tensor(h_fb[:, d, ck, 2 * pair * P:(2 * pair + 2) * P].rearrange("p (h n) -> p h n", h=2),
                                  tq[:, d, :, 0:P], rdn[:, d, :].unsqueeze(2).broadcast_to([P, 2, P]),
                                  ALU.mult).then_inc(h_done, 1)

            dve.wait_ge(cols_done, 1)
            for n in range(NU + 1):
                if n < NU:
                    weighted(n)
                if n >= 1:
                    heads_out(n - 1)
                if n % 4 == 0 and 1 <= n // 4 <= KD:
                    i = n // 4 - 1
                    dve.wait_ge(wohi_done, i + 1)
                    dve.tensor_tensor(wo_lo[:, i, :], w_st[:, i % 2, :, :].rearrange("p k n -> p (k n)"),
                                      wo_hi[:, i, :].bitcast(F32), ALU.subtract).then_inc(wolo_done, 1)

            def mix(t):
                b = t % 2
                if t >= 1:
                    dve.wait_ge(hT_ready, t)
                dve.tensor_tensor(hsum[:, :], h_fb[:, 0, t, :], h_fb[:, 1, t, :], ALU.add).then_inc(hsum_done, 1)
                dve.wait_ge(hsq_done, t + 1)
                dve.tensor_reduce(rt[:, 0:4], hsq[:, :].rearrange("p (h n) -> p h n", h=H), AX.X,
                                  ALU.add).then_inc(hss_done, 1)
                dve.wait_ge(hroot_done, t + 1)
                link(dve.reciprocal(rt[:, 8:12], rt[:, 4:8]))
                dve.tensor_tensor(hsum[:, :].rearrange("p (h n) -> p h n", h=H),
                                  hsum[:, :].rearrange("p (h n) -> p h n", h=H),
                                  rt[:, 8:12].unsqueeze(2).broadcast_to([P, H, P]), ALU.mult).then_inc(hn_done, 1)
                dve.wait_ge(c_in[b], 48 * (t // 2 + 1))
                dve.wait_ge(hT_ready, t + 1)
                for k in range(H):
                    ins = dve.scalar_tensor_tensor(out=mixf[:, b, NG + k, :], in0=psum[:, 4, k * P:(k + 1) * P],
                                                   scalar=hgain[:, k:k + 1], in1=og[:, b, k, :],
                                                   op0=ALU.mult, op1=ALU.mult)
                ins.then_inc(mixf_done, 1)
                dve.wait_ge(mixhi_done, t + 1)
                dve.tensor_tensor(mix_lo[:, b, :, :], mixf[:, b, :, :], mix_hi[:, b, :, :].bitcast(F32),
                                  ALU.subtract).then_inc(mixlo_done, 1)

            def second_norm(t):
                b = t % 2
                dve.wait_ge(out_ready, t + 1)
                if t >= 2:
                    dve.wait_ge(x1_out[b], 16 * (t // 2))
                    dve.wait_ge(xn2_out[b], 16 * (t // 2))
                    dve.wait_ge(x1root_done, t - 1)
                dve.tensor_tensor(x1[:, b, :].rearrange("p (a n) -> p a n", a=2),
                                  x_c[:, b, :].rearrange("p (a n) -> p a n", a=2), two(2 * b),
                                  ALU.add).then_inc(x1_done, 1)
                dve.wait_ge(x1root_done, t + 1)
                link(dve.reciprocal(stat[:, 3, t:t + 1], stat[:, 3, t:t + 1]))
                if t >= 2:
                    dve.wait_ge(xn2T_ready, t - 1)
                if t == 0:
                    dve.wait_ge(g2_in, 16)
                dve.scalar_tensor_tensor(out=xn2[:, b, :], in0=x1[:, b, :], scalar=stat[:, 3, t:t + 1],
                                         in1=g2_b[:, :], op0=ALU.mult, op1=ALU.mult).then_inc(xn2_done, 1)

            lg, el = rt[:, 16:16 + GR], rt[:, 16 + GR:16 + NL]
            gtop, gr, etop, er, etop2 = (rt[:, 52 + i:53 + i] for i in range(5))
            eq, oh_g, oh_e = rt[:, 60:68], rt[:, 68:72], rt[:, 72:88]
            esel, esel2 = rt[:, 88:96], rt[:, 96:104]
            emask, both, prod, rank = rt[:, 128:160], rt[:, 160:224], rt[:, 224:288], rt[:, 288:320]
            slot_f = rt[:, 320:322]

            def first_max(values, n, top, key, one_hot):
                link(dve.tensor_reduce(top, values, AX.X, ALU.max))
                link(dve.scalar_tensor_tensor(out=eq[:, 0:n], in0=values, scalar=top, in1=ramp[:, EPG - n:EPG],
                                              op0=ALU.is_ge, op1=ALU.mult))
                link(dve.tensor_reduce(key, eq[:, 0:n], AX.X, ALU.max))
                link(dve.tensor_scalar(one_hot, ramp[:, EPG - n:EPG], key, None, ALU.is_equal))

            def route(t):
                dve.wait_ge(logits_ready, t + 1)
                wait(dve, chosen_done, t)
                link(dve.tensor_tensor(rt[:, 16:16 + NL], psum[:, 7, 0:NL], rbias[:, :], ALU.add))
                first_max(lg, GR, gtop, gr, oh_g)
                dve.tensor_scalar(rgs[:, t, :], lg, gtop, None, ALU.subtract)
                by_group = emask.rearrange("p (g e) -> p g e", g=GR)
                link(dve.tensor_tensor(by_group, el.rearrange("p (g e) -> p g e", g=GR),
                                       oh_g.unsqueeze(2).broadcast_to([P, GR, EPG]), ALU.mult))
                link(dve.tensor_reduce(esel, emask.rearrange("p (g e) -> p e g", g=GR), AX.X, ALU.add))
                first_max(esel, EPG, etop, er, oh_e[:, 0:EPG])
                link(dve.scalar_tensor_tensor(out=esel2, in0=oh_e[:, 0:EPG], scalar=MASKED, in1=esel,
                                              op0=ALU.mult, op1=ALU.add))
                first_max(esel2, EPG, etop2, er, oh_e[:, EPG:2 * EPG])
                dve.tensor_tensor(rd21[:, t:t + 1], etop2, etop, ALU.subtract)
                for k in range(2):
                    ins = dve.tensor_tensor(both[:, k * E:(k + 1) * E].rearrange("p (g e) -> p g e", g=GR),
                                            oh_g.unsqueeze(2).broadcast_to([P, GR, EPG]),
                                            oh_e[:, k * EPG:(k + 1) * EPG].unsqueeze(1).broadcast_to([P, GR, EPG]),
                                            ALU.mult)
                link(ins)
                dve.tensor_tensor(chosen[:, t, :], both[:, 0:E], both[:, E:2 * E], ALU.add).then_inc(chosen_done, 1)

            def list_rows(t):
                dve.wait_ge(rank_ready, t + 1)
                wait(dve, slots_done, t)
                link(dve.tensor_tensor(rank, psum[:, 7, 64:64 + E], ebase[:, :], ALU.add))
                link(dve.tensor_tensor(prod.rearrange("p (k e) -> p k e", k=2), both.rearrange("p (k e) -> p k e", k=2),
                                       rank.unsqueeze(1).broadcast_to([P, 2, E]), ALU.mult))
                link(dve.tensor_reduce(slot_f, prod.rearrange("p (k e) -> p k e", k=2), AX.X, ALU.add))
                if t >= 2:
                    dve.wait_ge(list_out[t % 2], 32 * (t // 2))
                dve.tensor_copy(slot_i[:, t % 2, :], slot_f).then_inc(slots_done, 1)

            dve.wait_ge(consts_done, N_CONST)
            dve.wait_ge(h_done, NU)
            for t in range(-1, NT + 2):
                if t + 1 < NT:
                    mix(t + 1)
                if 0 <= t - 2 < NT:
                    route(t - 2)
                if 0 <= t < NT:
                    second_norm(t)
                if 0 <= t - 2 < NT:
                    list_rows(t - 2)
            dve.wait_ge(count_ready, 1)
            link(dve.tensor_reduce(rt[0:1, 330:331], psum[0:1, 7, 128:128 + E], AX.X, ALU.max))
            link(dve.tensor_scalar(half_steps[0:1, 1:2], rt[0:1, 330:331], -1.0, None, ALU.add))
            link(dve.tensor_scalar(half_steps[0:1, 2:3], half_steps[0:1, 1:2], 7, None, ALU.logical_shift_right))
            dve.tensor_scalar(half_steps[0:1, 0:1], half_steps[0:1, 2:3], 4, None,
                              ALU.logical_shift_left).then_inc(rounds_done, 1)
            dve.wait_ge(wexp_done, 1)
            dve.tensor_scalar(wts[:, 1, :], rd21[:, :], 1.0, None, ALU.add)
            link(dve.tensor_reduce(wts[:, 0, :], rgs[:, :, :], AX.X, ALU.add))
            link(dve.tensor_tensor(wts[:, 2, :], wts[:, 0, :], wts[:, 1, :], ALU.mult))
            link(dve.reciprocal(wts[:, 0, :], wts[:, 2, :]))
            link(dve.tensor_tensor(wts[:, 1, :], wts[:, 0, :], rd21[:, :], ALU.mult))

            def lo_part(piece):
                number, slot, r, _ = piece
                dve.wait_ge(ehi_done, number + 1)
                dve.tensor_tensor(e_lo[:, r, :, :], e_st[:, slot, :, :], e_hi[:, r, :, :].bitcast(F32),
                                  ALU.subtract).then_inc(elo_done, 1)

            def ex_lo_part(i, b):
                dve.wait_ge(exhi_done, i + 1)
                for half in range(2):
                    k = slice(4 * half, 4 * half + 4)
                    ins = dve.tensor_tensor(ex_lo[:, b, k, :], psum[:, 2 + half, :].rearrange("p (k n) -> p k n", k=4),
                                            ex_hi[:, b, k, :].bitcast(F32), ALU.subtract)
                ins.then_inc(exlo_done, 1)

            def ht_lo_part(i):
                dve.wait_ge(hthi_done, i + 1)
                dve.tensor_tensor(ht_lo[:, :, :], psum[:, 6, :].rearrange("p (k n) -> p k n", k=KF),
                                  ht_hi[:, :, :].bitcast(F32), ALU.subtract).then_inc(htlo_done, 1)

            def source_rows(i, b):
                dve.wait_ge(row_load, 16 * (i + 1))
                wait(dve, gx_load, 16 * (i - 1))
                wait(dve, row_done, i)
                dve.tensor_copy(row_f[:, 0:1], row_raw[:, b:b + 1]).then_inc(row_step, 1)
                dve.wait_ge(row_step, 3 * i + 1)
                dve.tensor_scalar(row_f[:, 1:2], row_f[:, 0:1], float(T), float(T), ALU.is_ge, ALU.mult).then_inc(row_step, 1)
                dve.wait_ge(row_step, 3 * i + 2)
                dve.tensor_tensor(row_f[:, 2:3], row_f[:, 0:1], row_f[:, 1:2], ALU.subtract).then_inc(row_step, 1)
                dve.wait_ge(row_step, 3 * i + 3)
                dve.tensor_scalar(row_g[:, b:b + 1], row_f[:, 2:3], float(T - 1), None, ALU.min).then_inc(row_done, 1)

            def keep_rows(i, b):
                wait(dve, y_out, 16 * (i - 1))
                dve.tensor_copy(row_s[:, b:b + 1], row_raw[:, b:b + 1]).then_inc(rows_copied, 1)

            def y_half(i, b, whole):
                dve.wait_ge(piece_used, whole)
                dve.tensor_copy(yo[:, b, 512:1024], psum[:, 5, :]).then_inc(y_right, 1)

            def hidden(i):
                dve.wait_ge(sg_done, i + 1)
                wait(dve, ht_ready, i)
                dve.tensor_tensor(hh[:, :], psum[:, 1, :], sg[:, :], ALU.mult).then_inc(h_ready, 1)

            def step(i, b):
                for c in range(2):
                    lo_part(gu_piece(i, c))
                ht_lo_part(i - 1)
                source_rows(i + 1, 1 - b)
                lo_part(gu_piece(i, 2))
                if not isinstance(i, int) or i >= 2:
                    y_half(i - 2, b, down_piece(i - 1, 3)[0] + 1)
                for c in range(3, 8):
                    lo_part(gu_piece(i, c))
                for c in range(2):
                    lo_part(down_piece(i, c))
                hidden(i)
                ex_lo_part(i + 1, 1 - b)
                for c in range(2, 4):
                    lo_part(down_piece(i, c))
                keep_rows(i, b)

            for c in range(4):
                lo_part(gu_piece(0, c))
            source_rows(0, 0)
            ex_lo_part(0, 0)
            source_rows(1, 1)
            for c in range(4, 8):
                lo_part(gu_piece(0, c))
            hidden(0)
            ex_lo_part(1, 1)
            keep_rows(0, 0)
            step(1, 1)
            n_half = load_half_steps(dve)
            with dve.Fori(1, n_half) as j:
                step(2 * j, 0)
                step(2 * j + 1, 1)
            last_i = 2 * n_half - 1
            ht_lo_part(last_i)
            y_half(last_i - 1, 0, down_piece(last_i, 3)[0] + 1)
            for c in range(4):
                lo_part(last_piece(last_i, c))
            y_half(last_i, 1, last_piece(last_i, 3)[0] + 1)

            for t in range(NT):
                b = t % 3
                dve.wait_ge(f_in[b], 48 * (t // 3 + 1))
                link(dve.scalar_tensor_tensor(out=f_x[:, b, :], in0=f_y[:, b, 0, :], scalar=wts[:, 0, t:t + 1],
                                              in1=f_x[:, b, :], op0=ALU.mult, op1=ALU.add))
                dve.scalar_tensor_tensor(out=f_x[:, b, :], in0=f_y[:, b, 1, :], scalar=wts[:, 1, t:t + 1],
                                         in1=f_x[:, b, :], op0=ALU.mult, op1=ALU.add).then_inc(f_sum, 1)
                dve.wait_ge(f_root, t + 1)
                link(dve.reciprocal(wts[:, 3, t:t + 1], wts[:, 3, t:t + 1]))
                if t == 0:
                    dve.wait_ge(gf_in, 16)
                if t >= 2:
                    dve.wait_ge(f_out[t % 2], 16 * (t // 2))
                dve.scalar_tensor_tensor(out=f_o[:, t % 2, :], in0=f_x[:, b, :], scalar=wts[:, 3, t:t + 1],
                                         in1=gf_b[:, :], op0=ALU.mult, op1=ALU.mult).then_inc(f_done, 1)


_INS = ["x_prompt", "x_sample", "norm1_g", "w_in", "pool_w", "pool_scale", "gate_b", "head_norm_g", "w_out",
        "norm2_g", "router_group_w", "router_group_b", "router_expert_w", "router_expert_b",
        "expert_w_gate", "expert_w_up", "expert_w_down", "final_norm_g"]


def kernel(**inputs):
    import numpy as _np
    import concourse.bacc as _bacc
    from concourse import mybir as _mybir
    from concourse.bass_utils import run_bass_kernel_spmd as _run

    nc = _bacc.Bacc("TRN2", target_bir_lowering=False, num_devices=1)
    arrays, args = {}, []
    for name in _INS:
        a = _np.ascontiguousarray(inputs[name])
        arrays[f"in_{name}_dram"] = a
        args.append(nc.dram_tensor(f"in_{name}_dram", a.shape, _mybir.dt.from_np(a.dtype), kind="ExternalInput").ap())
    for i, name in enumerate(("x_prompt", "x_sample")):
        args.append(nc.dram_tensor(f"out_{i}_dram", inputs[name].shape, _mybir.dt.float32, kind="ExternalOutput").ap())
    build(nc, *args)
    r = _run(nc, [arrays], core_ids=[0])
    return tuple(r.results[0][f"out_{i}_dram"] for i in range(2))
```

```python
from contextlib import ExitStack

import numpy as np

import concourse.bass as bass
from concourse import mybir

F32 = mybir.dt.float32
F32R = mybir.dt.float32r
BF16 = mybir.dt.bfloat16
I32 = mybir.dt.int32
ALU = mybir.AluOpType
ACT = mybir.ActivationFunctionType
AX = mybir.AxisListType

P = 128
KB = 1024
EPS = 1e-6
MASKED = -1e30


def build(nc, x_prompt, x_sample, norm1_g, w_in, pool_w, pool_scale, gate_b, head_norm_g, w_out,
          norm2_g, router_group_w, router_group_b, router_expert_w, router_expert_b,
          expert_w_gate, expert_w_up, expert_w_down, final_norm_g, y_prompt, y_sample):
    S0, D = x_prompt.shape[1:]
    S1 = x_sample.shape[1]
    T = S0 + S1
    NT = T // P
    C0 = S0 // P
    KD = D // P
    NG = pool_w.shape[1]
    WINDOWS = (2, 4, 8, 16)
    H = head_norm_g.shape[1] // P
    PW, MW = NG * P, H * P
    GR = router_group_w.shape[2]
    EPG = router_expert_w.shape[3]
    E = GR * EPG
    F = expert_w_gate.shape[3]
    KF = F // P
    NL = GR + E
    CAP = T
    SEGS = [(0, 512), (512, 512), (1024, 256)]
    assert (NT, KD, NG, H, KF, E) == (10, 8, 4, 4, 4, 32) and D == 1024

    xn2_dram = nc.dram_tensor("xn2_scratch", (T, D), F32).ap()
    y_dram = nc.dram_tensor("expert_rows", (2 * T + P, D), F32).ap()
    list_dram = nc.dram_tensor("row_lists", (E * CAP, 1), I32).ap()
    pooled_dram = nc.dram_tensor("pooledT", (PW, T), F32).ap()
    ogate_dram = nc.dram_tensor("ogateT", (MW, T), F32).ap()

    def tokens(t, a, b):
        return (a[0, t * P:(t + 1) * P, :] if t < C0 else b[0, (t - C0) * P:(t - C0 + 1) * P, :])

    base = (nc.sbuf_base + 63) // 64 * 64
    top = [base]

    def at(name, off, shape, dt):
        return nc.alloc_sbuf_tensor_at(name, shape, dt, offset=off)

    def const(name, shape, dt=F32):
        size = int(np.prod(shape[1:])) * (2 if dt == BF16 else 4)
        off = top[0]
        top[0] += (size + 31) // 32 * 32
        return at(name, off, shape, dt)

    ident = const("ident", [P, P])
    identb = const("identb", [P, P], BF16)
    maskb = const("maskb", [P, 2, P], BF16)
    laterb = const("laterb", [P, P], BF16)
    onesb = const("onesb", [P, P], BF16)
    zero_row = const("zero_row", [64, P])
    sel = const("sel", [64, 8, P])
    edge = const("edge", [P, NG, 16])
    wpool = const("wpool", [P, NG, P])
    pscale = const("pscale", [P, NG])
    hgain = const("hgain", [P, H])
    gbias = const("gbias", [64, 2])
    rw = const("rw", [P, KD, NL])
    rbias = const("rbias", [P, NL])
    ramp_i = const("ramp_i", [P, EPG + E], I32)
    ramp = const("ramp", [P, EPG])
    ebase = const("ebase", [P, E])
    rowval = const("rowval", [P, 2, NT], I32)
    epsc = const("epsc", [P, 1])
    onec = const("onec", [P, 1])
    cols = const("cols", [P, NT, 4, 8])
    decay = const("decay", [P, 8, NT])
    stat = const("stat", [P, 4, NT])
    hstat = const("hstat", [P, 2, NT, H])
    slot_i = const("slot_i", [P, NT, 2], I32)
    negm = const("negm", [64, T])
    rt = at("rt", top[0] - 4 * T, [P, 512], F32)
    sentinel = at("sentinel", top[0] - 4 * T, [80, E * CAP // 80], I32)
    mprev = const("mprev", [64, NT])
    mlast = const("mlast", [64, NT])
    rgs = const("rgs", [P, NT, GR])
    rd21 = const("rd21", [P, NT])
    wts = const("wts", [P, 4, NT])
    chosen = const("chosen", [P, NT, E], BF16)
    half_steps = const("half_steps", [1, 4], I32)
    R0 = (top[0] + 63) // 64 * 64

    X0 = R0
    xT_hi = at("xT_hi", X0, [P, KD, T], F32R)
    xT_lo = at("xT_lo", X0 + 40 * KB, [P, KD, T], F32R)
    W0 = X0 + 80 * KB
    w_hi = at("w_hi", W0, [P, 4, KD, P], F32R)
    w_lo = at("w_lo", W0 + 16 * KB, [P, 4, KD, P], F32R)
    w_st = at("w_st", W0 + 32 * KB, [P, 2, KD, P], F32)
    Q0 = W0 + 40 * KB
    qT = at("qT", Q0, [P, H, T], F32)
    kT = at("kT", Q0 + 20 * KB, [P, H, T], F32)
    v = at("v", Q0 + 40 * KB, [P, NT, H, P + 1], F32)
    PADW = 8 + S0 + 8 + S1 + 8
    pos = [8, 16 + S0]
    u_ext = at("u_ext", Q0, [P, NG, PADW], F32)
    ps_a = at("ps_a", Q0 + 4 * NG * PADW, [P, PADW], F32)
    ps_b = at("ps_b", Q0 + 4 * (NG + 1) * PADW, [P, PADW], F32)
    A0 = Q0 + 4 * (NG + 2) * PADW
    x_in = at("x_in", A0, [P, 3, D], F32)
    xn = at("xn", A0 + 12 * KB, [P, 2, D], F32)
    g1_b = at("g1_b", A0 + 20 * KB, [P, D], F32)
    junk = at("junk", A0 + 24 * KB, [P, D], F32)
    g_i, g_f, g_e, g_b, g_m = (at(n, A0 + 5 * KB * i, [64, T], F32)
                               for i, n in enumerate(("g_i", "g_f", "g_e", "g_b", "g_m")))
    V0 = Q0 + 40 * KB + 4 * NT * H * (P + 1)
    ev = at("ev", V0, [P, 4, 512], F32)
    END = V0 + 8 * KB
    assert END <= nc.sbuf_usable_end, (END, nc.sbuf_usable_end, R0)

    h_fb = at("h_fb", X0, [P, 2, NT, MW], F32)
    wo_hi = at("wo_hi", X0 + 40 * KB, [P, KD, D], F32R)
    state = at("state", X0 + 72 * KB, [P, 2, H, P + 1], F32)
    dn = at("dn", X0 + 77 * KB, [P, 2, 2], F32)
    rdn = at("rdn", X0 + 77 * KB + 64, [P, 2, 2], F32)
    wo_lo = at("wo_lo", W0, [P, KD, D], F32R)
    uk = at("uk", V0, [P, 2, 2, P], F32)
    wgt = at("wgt", V0 + 2 * KB, [P, 2, 2, P], F32)
    sT = at("sT", V0 + 4 * KB, [P, 2, 2, P], F32)
    tq = at("tq", X0 + 77 * KB + 128, [P, 2, 2, P + 1], F32)

    c_off = [Q0]

    def cbuf(name, shape, dt=F32):
        off = c_off[0]
        c_off[0] += (int(np.prod(shape[1:])) * 4 + 31) // 32 * 32
        return at(name, off, shape, dt)

    mixf = cbuf("mixf", [P, 2, KD, P])
    mix_hi = cbuf("mix_hi", [P, 2, KD, P], F32R)
    mix_lo = cbuf("mix_lo", [P, 2, KD, P], F32R)
    xn2T = cbuf("xn2T", [P, KD, P])
    x1 = at("x1", END - 4 * NT * D, [P, NT, D], F32)
    g2_b = at("g2_b", X0 + 72 * KB, [P, D], F32)
    og = at("og", X0 + 76 * KB, [P, 2, H, P], F32)
    xn2 = at("xn2", W0 + 32 * KB, [P, 2, D], F32)
    sq_c = at("sq_c", X0 + 36 * KB, [P, D], F32)
    assert c_off[0] <= END - 4 * NT * D

    m_off = [X0]

    def mbuf(name, shape, dt=F32):
        off = m_off[0]
        m_off[0] += (int(np.prod(shape[1:])) * 4 + 31) // 32 * 32
        return at(name, off, shape, dt)

    NST, NRG = 12, 6
    gx = mbuf("gx", [P, 2, D])
    yo = mbuf("yo", [P, 2, D])
    sg = mbuf("sg", [P, F])
    hh = mbuf("hh", [P, F])
    e_st = mbuf("e_st", [P, NST, 2, 512])
    e_hi = mbuf("e_hi", [P, NRG, 2, 512], F32R)
    e_lo = mbuf("e_lo", [P, NRG, 2, 512], F32R)
    ex_hi = mbuf("ex_hi", [P, 2, KD, P], F32R)
    ex_lo = mbuf("ex_lo", [P, 2, KD, P], F32R)
    ht_hi = mbuf("ht_hi", [P, KF, P], F32R)
    ht_lo = mbuf("ht_lo", [P, KF, P], F32R)
    row_raw = mbuf("row_raw", [P, 2], I32)
    row_s = mbuf("row_s", [P, 2], I32)
    row_g = mbuf("row_g", [P, 2], I32)
    row_f = mbuf("row_f", [P, 4])
    assert m_off[0] <= END - 4 * NT * D
    gf_b = at("gf_b", X0, [P, D], F32)
    f_y = at("f_y", X0 + 4 * KB, [P, NT, 2, D], F32)
    f_sq = at("f_sq", X0 + (4 + 8 * NT) * KB, [P, D], F32)

    psum = nc.alloc_psum_tensor("psum", [P, 8, 512], F32)

    def two(i):
        return psum[:, i:i + 2, :]

    ctx = ExitStack()
    with ctx:
        ctx.enter_context(nc.allow_non_contiguous_dma(reason="one word to a partition"))

        def sem(name):
            return ctx.enter_context(nc.semaphore(name))

        consts_in, g1_in, list_set = sem("consts_in"), sem("g1_in"), sem("list_set")
        x_load = [sem(f"x_load{i}") for i in range(3)]
        w_load = [sem(f"w_load{i}") for i in range(2)]
        ev_out = [sem(f"ev_out{i}") for i in range(4)]
        pool_step, consts_done, bias_zero, edges_done, gate_slot_zero = (
            sem(n) for n in ("pool_step", "consts_done", "bias_zero", "edges_done", "gate_slot_zero"))
        sq_done, root_done, xn_done, xt_ready, xhi_done, xlo_done = (
            sem(n) for n in ("sq_done", "root_done", "xn_done", "xt_ready", "xhi_done", "xlo_done"))
        pads_zero, whi_done, wlo_done, proj_ready, act_took, gates_took, v_took = (
            sem(n) for n in ("pads_zero", "whi_done", "wlo_done", "proj_ready", "act_took", "gates_took", "v_took"))
        pooled, mixer_ready, ev_full = sem("pooled"), sem("mixer_ready"), sem("ev_full")
        g_abs, g_exp, g_ln, rows_ready, turned, dec_ready, cols_done, v_ones, state_zero = (
            sem(n) for n in ("g_abs", "g_exp", "g_ln", "rows_ready", "turned", "dec_ready", "cols_done", "v_ones",
                             "state_zero"))
        kq_ready, nm_ready, uk_done, wgt_done, s_done, kv_ready, num_done, state_done, h_done = (
            sem(n) for n in ("kq_ready", "nm_ready", "uk_done", "wgt_done", "s_done", "kv_ready", "num_done", "state_done", "h_done"))
        wo_load = [sem(f"wo_load{i}") for i in range(2)]
        wohi_done, wolo_done = sem("wohi_done"), sem("wolo_done")
        c_in = [sem(f"c_in{i}") for i in range(2)]
        g2_in = sem("g2_in")
        xc_in = [sem(f"xc_in{i}") for i in range(2)]
        hsum_done, hss_done, hroot_done, hrecip_done, hn_done, hT_ready, mixf_done, mixhi_done, mixlo_done = (
            sem(n) for n in ("hsum_done", "hss_done", "hroot_done", "hrecip_done", "hn_done", "hT_ready", "mixf_done",
                             "mixhi_done", "mixlo_done"))
        out_ready, x1_done, x1root_done, xn2_done, xn2T_ready, xn2T_done, logits_ready, logits_taken = (
            sem(n) for n in ("out_ready", "x1_done", "x1root_done", "xn2_done", "xn2T_ready", "xn2T_done", "logits_ready",
                             "logits_taken"))
        xn2_out = [sem(f"xn2_out{i}") for i in range(2)]
        list_out = [sem(f"list_out{i}") for i in range(2)]
        chosen_done, rank_ready, slots_done, count_ready, rounds_done, wexp_done, wts_done = (
            sem(n) for n in ("chosen_done", "rank_ready", "slots_done", "count_ready", "rounds_done", "wexp_done",
                             "wts_done"))
        e_load = [sem(f"e_load{i}") for i in range(NST)]
        row_load = [sem(f"row_load{i}") for i in range(2)]
        gx_load = [sem(f"gx_load{i}") for i in range(2)]
        ehi_done, elo_done, piece_used, row_done, rows_copied, ext_ready, exhi_done, exlo_done = (
            sem(n) for n in ("ehi_done", "elo_done", "piece_used", "row_done", "rows_copied",
                             "ext_ready", "exhi_done", "exlo_done"))
        sg_done, h_ready, ht_ready, hthi_done, htlo_done, y_left, y_right, y_out, row_step = (
            sem(n) for n in ("sg_done", "h_ready", "ht_ready", "hthi_done", "htlo_done", "y_left", "y_right", "y_out",
                             "row_step"))
        f_in = [sem(f"f_in{i}") for i in range(NT)]
        f_out, gf_in, f_sum, f_root, f_done = sem("f_out"), sem("gf_in"), sem("f_sum"), sem("f_root"), sem("f_done")
        pool_past = sem("pool_past")
        dve_step, act_step = sem("dve_step"), sem("act_step")

        block = ctx.enter_context(nc.Block())

        U, G, O, K, Q, VV = 0, NG, NG + 1, NG + 1 + H, NG + 1 + 2 * H, NG + 1 + 3 * H
        NSL = VV + H
        COL = {U: 0, Q: PW, K: PW + MW, VV: PW + 2 * MW, O: PW + 3 * MW}
        GATES = PW + 4 * MW
        N_EDGE = sum(w - 1 for w in WINDOWS)
        N_CONST = 20

        proj, mixer_after = [], {}
        for first, count, kind in ((U, NG, "u"), (G, 1, "g"), (O, H, "o"), (K, H, "k"), (Q, H, "q")):
            for s in range(len(SEGS)):
                proj += [(kind, first + c, s) for c in range(count)]
                if kind == "o" and s < 2:
                    mixer_after[len(proj) - 1] = (2 * s, 2 * s + 1)
        NPROJ = len(proj)

        last_use = {m: n + 1 for n, (_, m, _) in enumerate(proj)}

        def act_results(n):
            return sum(kind in "ukq" for kind, _, _ in proj[:n])

        def bank_free(eng, n):
            if n < 4:
                return
            m = n - 4
            if m < NPROJ and proj[m][0] == "g":
                eng.wait_ge(gates_took, proj[m][2] + 1)
            elif m < NPROJ and proj[m][0] == "o":
                eng.wait_ge(ev_full, place["o", proj[m][1] - O, proj[m][2]] + 1)
            elif m < NPROJ:
                eng.wait_ge(act_took, act_results(m + 1))
            else:
                eng.wait_ge(v_took, m - NPROJ + 1)

        ring = []
        for n, (kind, m, s) in enumerate(proj):
            if kind == "o":
                ring.append(("o", m - O, s))
            for g in mixer_after.get(n, ()):
                ring += [("a", g, s2) for s2 in range(len(SEGS))]
        place = {key: i for i, key in enumerate(ring)}

        def chunk_of(step, back):
            if not back:
                return step
            return C0 - 1 - step if step < C0 else NT - 1 - (step - C0)

        NU = 4 * NT

        def unit(n):
            step, pair, d = n // 4, n // 2 % 2, n % 2
            return step, pair, d, chunk_of(step, d)

        def complete_after(t):
            return 4 * (C0 if t < C0 else max(t, NT - 1 + C0 - t) + 1)

        order = sorted(range(NT), key=complete_after)
        EARLY = NT - 4

        def carries(step):
            return step not in (C0 - 1, NT - 1)

        def wait(eng, s, value):
            if not isinstance(value, int) or value >= 1:
                eng.wait_ge(s, value)

        def slot_loads(i, b):
            return 8 * i + 16 - 8 * b

        def load_half_steps(eng):
            eng.wait_ge(rounds_done, 1)
            return eng.value_load(half_steps[0:1, 0:1], min_val=0, max_val=E // 2 * (NT - 1)) + E // 2

        def gu_piece(i, c):
            if isinstance(i, int) and i == 0:
                return c, c, c % NRG, 1
            return 12 * i - 4 + c, (8 + c) % NST, (2 + c) % NRG, i + c // 4

        def down_piece(i, c):
            return 12 * i + 4 + c, 4 + c, (4 + c) % NRG, i + 1

        def last_piece(i, c):
            return 12 * i + 8 + c, 8 + c, (2 + c) % NRG, i + 1

        @block.sync
        def _(sp):
            def slice_in(m):
                if m >= 2:
                    sp.wait_ge(wlo_done, m - 1)
                if m == G:
                    sp.wait_ge(gate_slot_zero, 1)
                    for blk in range(4):
                        c = GATES + H * blk
                        sp.dma_start(w_st[:, m % 2, :, 32 * blk:32 * blk + H],
                                     w_in[0, :, c:c + H].rearrange("(p k) n -> p k n", k=KD)).then_inc(w_load[m % 2], 16)
                    return
                first = max(x for x in COL if x <= m)
                c = COL[first] + (m - first) * P
                sp.dma_start(w_st[:, m % 2, :, :],
                             w_in[0, :, c:c + P].rearrange("(p k) n -> p k n", k=KD)).then_inc(w_load[m % 2], 16)

            slice_in(0)
            slice_in(1)
            for dst, src in (
                (wpool[:, :, :], pool_w[0].rearrange("g c e -> c g e")),
                (pscale[:, :], pool_scale[0].rearrange("(g c) -> c g", c=P)),
                (hgain[:, :], head_norm_g[0].rearrange("(h c) -> c h", c=P)),
                (rw[:, :, 0:GR], router_group_w[0].rearrange("(p k) n -> p k n", k=KD)),
                (rw[:, :, GR:NL], router_expert_w[0].rearrange("(p k) g e -> p k (g e)", k=KD)),
                (rbias[:, 0:GR], router_group_b[0:1, :].broadcast_to([P, GR])),
                (rbias[:, GR:NL], router_expert_b[0:1].rearrange("a g e -> a (g e)").broadcast_to([P, E])),
            ):
                sp.dma_start(dst, src).then_inc(consts_in, 16)
            sp.wait_ge(bias_zero, 1)
            for d in range(2):
                for kind in range(2):
                    c = kind * 2 * H + d * H
                    sp.dma_start(gbias[32 * d:32 * d + H, kind:kind + 1],
                                 gate_b[0:1, c:c + H].rearrange("a h -> h a")).then_inc(consts_in, 16)
            for m in range(2, NSL):
                slice_in(m)
            for i in range(KD):
                if i < 2:
                    sp.wait_ge(wlo_done, NSL)
                else:
                    sp.wait_ge(wolo_done, i - 1)
                sp.dma_start(w_st[:, i % 2, :, :].rearrange("p k n -> p (k n)"),
                             w_out[0, i * P:(i + 1) * P, :]).then_inc(wo_load[i % 2], 16)
            for i in range(4):
                sp.wait_ge(ev_out[i], 16 * len(ring[i::4]))
            sp.wait_ge(h_done, NU)
            sp.wait_ge(state_done, NU)
            sp.dma_start(g2_b[:, :], norm2_g[0:1, :].broadcast_to([P, D])).then_inc(g2_in, 16)

            for i, t in enumerate(order):
                if i >= 2:
                    sp.wait_ge(mixlo_done, i - 1)
                sp.dma_start(mixf[:, i % 2, 0:NG, :], pooled_dram[:, t * P:(t + 1) * P]
                             .rearrange("(g p) n -> p g n", p=P)).then_inc(c_in[i % 2], 16)
                sp.dma_start(og[:, i % 2, :, :], ogate_dram[:, t * P:(t + 1) * P]
                             .rearrange("(g p) n -> p g n", p=P)).then_inc(c_in[i % 2], 16)
                sp.dma_start(x1[:, t, :], tokens(t, x_prompt, x_sample)).then_inc(xc_in[i % 2], 16)

            def piece_in(piece, src, d2):
                number, slot, _, _ = piece
                wait(sp, elo_done, number - NST + 1)
                dst = e_st[:, slot, :, :]
                sp.dma_start(dst if d2 else dst.rearrange("p a n -> p (a n)"), src).then_inc(e_load[slot], 16)

            def gu_in(i, c):
                w = expert_w_up if c % 2 else expert_w_gate
                kk = 2 * (c // 2)
                piece_in(gu_piece(i, c), w[0, bass.ds(i % E, 1), :, :]
                         .rearrange("a (p k) n -> p (a k) n", k=KD)[:, kk:kk + 2, :], True)

            def down_in(piece, e, c):
                piece_in(piece, expert_w_down[0, bass.ds(e % E, 1), :, :]
                         .rearrange("a (p k) n -> p (a k) n", k=KF)[:, c, :], False)

            sp.wait_ge(hss_done, NT)
            for c in range(4):
                gu_in(0, c)
            sp.wait_ge(out_ready, NT)
            sp.wait_ge(x1root_done, NT)
            for c in range(4, 8):
                gu_in(0, c)
            def step(i):
                for c in range(8):
                    gu_in(i, c)
                for c in range(4):
                    down_in(down_piece(i, c), i - 1, c)

            step(1)
            n_half = load_half_steps(sp)
            with sp.Fori(1, n_half) as j:
                step(2 * j)
                step(2 * j + 1)
            last = 2 * n_half - 1
            for c in range(4):
                down_in(last_piece(last, c), last, c)

            sp.wait_ge(y_out, 32 * n_half)
            sp.dma_start(gf_b[:, :], final_norm_g.rearrange("(a d) -> a d", a=1).broadcast_to([P, D])).then_inc(gf_in, 16)
            for t in range(NT):
                for k in range(2):
                    sp.dma_start(f_y[:, t, k, :], y_dram[k * T + t * P:k * T + (t + 1) * P, :]).then_inc(f_in[t], 16)
            for t in range(NT):
                sp.wait_ge(f_done, t + 1)
                sp.dma_start(tokens(t, y_prompt, y_sample), x1[:, t, :]).then_inc(f_out, 16)
            sp.wait_ge(f_out, 16 * NT)

        @block.gpsimd
        def _(pool):
            def x_in_tile(t):
                if t >= 3:
                    pool.wait_ge(xn_done, t - 2)
                pool.dma_start(x_in[:, t % 3, :], tokens(t, x_prompt, x_sample)).then_inc(x_load[t % 3], 16)

            for t in range(3):
                x_in_tile(t)
                if t == 0:
                    pool.dma_start(g1_b[:, :], norm1_g[0:1, :].broadcast_to([P, D])).then_inc(g1_in, 16)
            pool.memset(gbias[:, :], 0.0).then_inc(bias_zero, 1)
            pool.memset(ident[:, :], 0.0).then_inc(pool_step, 1)
            pool.memset(epsc[:, :], EPS).then_inc(consts_done, 1)
            pool.memset(onec[:, :], 1.0).then_inc(consts_done, 1)
            pool.wait_ge(pool_step, 1)
            pool.affine_select(out=ident[:, :], in_=ident[:, :], compare_op=ALU.not_equal, fill=1.0, base=0,
                               pattern=[[-1, P]], channel_multiplier=1).then_inc(consts_done, 1)
            for t in range(3, NT):
                x_in_tile(t)
            pool.memset(zero_row[:, :], 0.0).then_inc(consts_done, 1)
            pool.memset(onesb[:, :], 1.0).then_inc(consts_done, 1)
            for tile, value in ((identb[:, :], 0.0), (maskb[:, :, :], 0.0), (laterb[:, :], 1.0), (sel[:, :, :], 0.0),
                                (edge[:, :, :], 1.0)):
                pool.memset(tile, value).then_inc(pool_step, 1)
            pool.wait_ge(pool_step, 6)
            pool.affine_select(out=identb[:, :], in_=identb[:, :], compare_op=ALU.not_equal, fill=1.0, base=0,
                               pattern=[[-1, P]], channel_multiplier=1).then_inc(consts_done, 1)
            for d, sign in enumerate((1, -1)):
                pool.affine_select(out=maskb[:, d, :], in_=maskb[:, d, :], compare_op=ALU.is_ge, fill=MASKED, base=0,
                                   pattern=[[sign, P]], channel_multiplier=-sign).then_inc(consts_done, 1)
            pool.affine_select(out=laterb[:, :], in_=laterb[:, :], compare_op=ALU.is_ge, fill=0.0, base=-1,
                               pattern=[[1, P]], channel_multiplier=-1).then_inc(consts_done, 1)
            for r in range(2 * H):
                pool.affine_select(out=sel[:, r, :], in_=sel[:, r, :], compare_op=ALU.not_equal, fill=1.0,
                                   base=-(32 * (r // H) + r % H), pattern=[[0, P]],
                                   channel_multiplier=1).then_inc(consts_done, 1)
            for g, w in enumerate(WINDOWS):
                for j in range(w // 2):
                    pool.memset(edge[:, g, j:j + 1], w / (j + w // 2)).then_inc(edges_done, 1)
                for j in range(w // 2 - 1):
                    pool.memset(edge[:, g, 15 - j:16 - j], w / (j + 1 + w // 2)).then_inc(edges_done, 1)
            pool.iota(rowval[:, :, :], pattern=[[T, 2], [P, NT]], base=0, channel_multiplier=1).then_inc(consts_done, 1)
            pool.iota(sentinel[:, :], pattern=[[0, E * CAP // 80 // P], [1, P]], base=2 * T,
                      channel_multiplier=0).then_inc(pool_step, 1)
            pool.iota(ramp_i[:, 0:EPG], pattern=[[-1, EPG]], base=EPG, channel_multiplier=0).then_inc(pool_step, 1)
            pool.iota(ramp_i[:, EPG:EPG + E], pattern=[[CAP, E]], base=0, channel_multiplier=0).then_inc(pool_step, 1)
            pool.wait_ge(pool_step, 9)
            pool.tensor_copy(ramp[:, :], ramp_i[:, 0:EPG]).then_inc(consts_done, 1)
            pool.tensor_copy(ebase[:, :], ramp_i[:, EPG:EPG + E]).then_inc(consts_done, 1)
            pool.dma_start(list_dram.rearrange("(q n) a -> q (n a)", q=80), sentinel[:, :]).then_inc(list_set, 16)

            for i, (kind, c, s) in enumerate(ring):
                a, n = SEGS[s]
                dram = ogate_dram if kind == "o" else pooled_dram
                pool.wait_ge(ev_full, i + 1)
                pool.dma_start(dram[c * P:(c + 1) * P, a:a + n], ev[:, i % 4, 0:n]).then_inc(ev_out[i % 4], 16)

            pool.wait_ge(list_set, 16)

            for t in order:
                pool.wait_ge(h_done, complete_after(t))
                pool.tensor_tensor(h_fb[:, 0, t, :], h_fb[:, 0, t, :], h_fb[:, 1, t, :], ALU.add).then_inc(hsum_done, 1)

            def entries_out(i):
                pool.wait_ge(slots_done, i + 1)
                for k in range(2):
                    pool.indirect_dma_start(
                        out=list_dram, out_offset=bass.IndirectOffsetOnAxis(ap=slot_i[:, i, k:k + 1], axis=0),
                        in_=rowval[:, k, order[i]:order[i] + 1], in_offset=None).then_inc(list_out[i % 2], 16)

            for i, t in enumerate(order):
                pool.wait_ge(xn2_done, i + 1)
                pool.dma_start(xn2_dram[t * P:(t + 1) * P, :], xn2[:, i % 2, :]).then_inc(xn2_out[i % 2], 16)
                if i >= 3:
                    entries_out(i - 3)
            for i in range(NT - 3, NT):
                entries_out(i)
            for i in range(2):
                pool.wait_ge(list_out[i], 16 * NT)
                pool.wait_ge(xn2_out[i], 16 * (NT // 2))

            def list_in(i, b):
                wait(pool, rows_copied, i - 1)
                wait(pool, ext_ready, i - 1)
                pool.sem_inc(pool_past, 1)
                pool.dma_start(row_raw[:, b:b + 1],
                               list_dram[bass.ds((i % E) * CAP + (i // E) * P, P), :]).then_inc(row_load[b], 16)

            def rows_in(i, b):
                pool.wait_ge(row_done, i + 1)
                pool.sem_inc(pool_past, 1)
                pool.indirect_dma_start(
                    out=gx[:, b, :], out_offset=None, in_=xn2_dram,
                    in_offset=bass.IndirectOffsetOnAxis(ap=row_g[:, b:b + 1], axis=0)).then_inc(gx_load[b], 16)

            def rows_out(i, b):
                pool.wait_ge(y_left, i + 1)
                pool.wait_ge(y_right, i + 1)
                pool.sem_inc(pool_past, 1)
                pool.indirect_dma_start(
                    out=y_dram, out_offset=bass.IndirectOffsetOnAxis(ap=row_s[:, b:b + 1], axis=0),
                    in_=yo[:, b, :], in_offset=None).then_inc(y_out, 16)
                pool.wait_ge(y_out, 16 * (i + 1))

            list_in(0, 0)
            list_in(1, 1)
            rows_in(0, 0)
            rows_in(1, 1)
            list_in(2, 0)
            rows_in(2, 0)
            n_half = load_half_steps(pool)
            with pool.Fori(1, n_half) as j:
                list_in(2 * j + 1, 1)
                rows_in(2 * j + 1, 1)
                rows_out(2 * j - 2, 0)
                list_in(2 * j + 2, 0)
                rows_in(2 * j + 2, 0)
                rows_out(2 * j - 1, 1)
            rows_out(2 * n_half - 2, 0)
            rows_out(2 * n_half - 1, 1)

        @block.tensor
        def _(pe):
            def product3(out, a, b, start, stop):
                (a_hi, a_lo), (b_hi, b_lo) = a, b
                pe.matmul(out, a_hi, b_hi, start=start, stop=False)
                pe.matmul(out, a_hi, b_lo, start=False, stop=False)
                return pe.matmul(out, a_lo, b_hi, start=False, stop=stop)

            def x_transposes(t):
                pe.wait_ge(xn_done, t + 1)
                if t >= 2:
                    pe.wait_ge(xlo_done, t - 1)
                for k in range(KD):
                    last = pe.transpose(psum[:, 4 + 2 * (t % 2) + k // 4, (k % 4) * P:(k % 4 + 1) * P],
                                        xn[:, t % 2, k:D:KD], ident[:, :])
                last.then_inc(xt_ready, 1)

            pe.wait_ge(consts_done, 3)
            for t in range(4):
                x_transposes(t)

            def mix_pooled(g):
                pe.wait_ge(pooled, g + 1)
                for s in range(len(SEGS)):
                    j = 3 * g + s - 4
                    if j >= 0:
                        pe.wait_ge(ev_full, place["a", j // 3, j % 3] + 1)
                    out = psum[:, 4 + (3 * g + s) % 4, :]
                    a, n = SEGS[s]
                    parts = [(0, 0, S0), (S0, 1, a + n - S0)] if s == 0 else [(0, 1, n)]
                    for col, seq, m in parts:
                        first = pos[seq] + a + col - (S0 if seq else 0)
                        last = pe.matmul(out[:, col:col + m], wpool[:, g, :], u_ext[:, g, first:first + m],
                                         start=True, stop=True)
                    last.then_inc(mixer_ready, 1)

            pe.wait_ge(consts_in, 16 * 11)
            for n, (kind, m, s) in enumerate(proj):
                a, length = SEGS[s]
                pe.wait_ge(wlo_done, m + 1)
                pe.wait_ge(xlo_done, (a + length) // P)
                bank_free(pe, n)
                for k in range(KD):
                    last = product3(psum[:, n % 4, 0:length], (w_hi[:, m % 4, k, :], w_lo[:, m % 4, k, :]),
                                    (xT_hi[:, k, a:a + length], xT_lo[:, k, a:a + length]), k == 0, k == KD - 1)
                last.then_inc(proj_ready, 1)
                if n < NT - 4:
                    x_transposes(4 + n)
                for g in mixer_after.get(n, ()):
                    mix_pooled(g)
                if kind == "o" and n + 1 < NPROJ and proj[n + 1][0] == "k":
                    pe.wait_ge(ev_full, place["a", NG - 1, 2] + 1)
                    pe.wait_ge(rows_ready, 1)
                    for c in range(NT):
                        for kind4, row in enumerate((g_m, g_e, g_i, g_b)):
                            o = (c % 3) * 144 + kind4 * 36
                            last = pe.transpose(psum[:, 4 + c // 3, o:o + 36], row[0:36, c * P:(c + 1) * P],
                                                ident[0:36, 0:36])
                    last.then_inc(turned, 1)
                    for r in range(2 * H):
                        last = pe.matmul(psum[:, 7, 256 + r * NT:256 + (r + 1) * NT], sel[:, r, :], mlast[:, :],
                                         start=True, stop=True)
                    last.then_inc(dec_ready, 1)
            for t in range(NT):
                n = NPROJ + t
                if t == 0:
                    pe.wait_ge(wlo_done, NSL)
                bank_free(pe, n)
                for k in range(KD):
                    tok = slice(t * P, (t + 1) * P)
                    last = product3(psum[:, n % 4, :], (xT_hi[:, k, tok], xT_lo[:, k, tok]),
                                    (w_hi[:, :, k, :], w_lo[:, :, k, :]), k == 0, k == KD - 1)
                last.then_inc(proj_ready, 1)

            def unit_scores(n):
                step, pair, d, ck = unit(n)
                tok = slice(ck * P, (ck + 1) * P)
                heads = (2 * pair, 2 * pair + 1)
                if n >= 2:
                    pe.wait_ge(state_done, n - 1)
                    pe.wait_ge(wgt_done, n - 1)
                for hh_, h in enumerate(heads):
                    pe.transpose(psum[:, 4 * d, hh_ * P:(hh_ + 1) * P], kT[:, h, tok], ident[:, :])
                for hh_, h in enumerate(heads):
                    last = pe.matmul(psum[:, 4 * d, (2 + hh_) * P:(3 + hh_) * P], kT[:, h, tok], qT[:, h, tok],
                                     start=True, stop=True)
                last.then_inc(kq_ready, 1)
                for hh_, h in enumerate(heads):
                    out = psum[:, 4 * d + 1, hh_ * P:(hh_ + 1) * P]
                    pe.matmul(out, identb[:, :], maskb[:, d, :], start=True, stop=False)
                    last = pe.matmul(out, sel[:, d * H + h, :], negm[:, tok], start=False, stop=True)
                last.then_inc(nm_ready, 1)

            def unit_rows(n):
                step, pair, d, ck = unit(n)
                tok = slice(ck * P, (ck + 1) * P)
                heads = (2 * pair, 2 * pair + 1)
                if n >= 2:
                    pe.wait_ge(num_done, n - 1)
                if n >= 4:
                    pe.wait_ge(state_done, n - 3)
                for hh_, h in enumerate(heads):
                    pe.matmul(psum[:, 4 * d + 3, hh_ * (P + 1):(hh_ + 1) * (P + 1)], qT[:, h, tok],
                              state[:, d, h, :], start=True, stop=True)
                pe.wait_ge(s_done, n + 1)
                pe.wait_ge(uk_done, n + 1)
                for hh_, h in enumerate(heads):
                    last = pe.matmul(psum[:, 4 * d + 2, hh_ * (P + 1):(hh_ + 1) * (P + 1)], sT[:, d, hh_, :],
                                     v[:, ck, h, :], start=True, stop=True)
                if carries(step):
                    for hh_, h in enumerate(heads):
                        last = pe.matmul(psum[:, 4 * d, hh_ * (P + 1):(hh_ + 1) * (P + 1)], uk[:, d, hh_, :],
                                         v[:, ck, h, :], start=True, stop=True)
                last.then_inc(kv_ready, 1)

            pe.wait_ge(v_took, NT)
            pe.wait_ge(v_ones, 1)
            pe.wait_ge(state_zero, 1)
            pe.wait_ge(cols_done, 1)
            unit_scores(0)
            for n in range(NU):
                if n + 1 < NU:
                    unit_scores(n + 1)
                unit_rows(n)

            def h_transposes(i):
                pe.wait_ge(hn_done, i + 1)
                if i >= 1:
                    pe.wait_ge(mixf_done, i)
                for k in range(H):
                    last = pe.transpose(psum[:, 4, k * P:(k + 1) * P], h_fb[:, 0, order[i], k * P:(k + 1) * P],
                                        ident[:, :])
                last.then_inc(hT_ready, 1)

            def out_rows(t, half):
                if half == 0:
                    pe.wait_ge(mixlo_done, t + 1)
                    if t >= 2:
                        pe.wait_ge(x1_done, t - 1)
                for k in range(KD):
                    c = slice(half * 512, (half + 1) * 512)
                    last = product3(psum[:, 2 * (t % 2) + half, :], (mix_hi[:, t % 2, k, :], mix_lo[:, t % 2, k, :]),
                                    (wo_hi[:, k, c], wo_lo[:, k, c]), k == 0, k == KD - 1)
                if half == 1:
                    last.then_inc(out_ready, 1)

            def xn2_transposes(t):
                pe.wait_ge(xn2_done, t + 1)
                if t >= 1:
                    pe.wait_ge(xn2T_done, t)
                for k in range(KD):
                    last = pe.transpose(psum[:, 5 + k // 4, (k % 4) * P:(k % 4 + 1) * P], xn2[:, t % 2, k:D:KD],
                                        ident[:, :])
                last.then_inc(xn2T_ready, 1)

            def router(t, ranks_read):
                pe.wait_ge(xn2T_done, t + 1)
                if t >= 1:
                    pe.wait_ge(logits_taken, t)
                if ranks_read:
                    pe.wait_ge(slots_done, ranks_read)
                for k in range(KD):
                    last = pe.matmul(psum[:, 7, 0:NL], xn2T[:, k, :], rw[:, k, :], start=(k == 0), stop=(k == KD - 1))
                last.then_inc(logits_ready, 1)

            def ranks(t):
                pe.wait_ge(chosen_done, t + 1)
                for t2 in range(t):
                    pe.matmul(psum[:, 7, 64:64 + E], onesb[:, :], chosen[:, t2, :], start=(t2 == 0), stop=False)
                pe.matmul(psum[:, 7, 64:64 + E], laterb[:, :], chosen[:, t, :], start=(t == 0),
                          stop=True).then_inc(rank_ready, 1)

            pe.wait_ge(wolo_done, KD)
            pe.wait_ge(num_done, NU)
            pe.wait_ge(consts_done, N_CONST)
            h_transposes(0)
            h_transposes(1)
            for t in range(NT + 3):
                if 0 <= t - 3 < NT and t != NT + 1:
                    ranks(t - 3)
                if t < NT:
                    out_rows(t, 0)
                if t == NT + 1:
                    router(t - 2, t - 3)
                    ranks(t - 3)
                elif 0 <= t - 2 < NT:
                    router(t - 2, t - 2)
                if t + 2 < NT:
                    h_transposes(t + 2)
                if t < NT:
                    out_rows(t, 1)
                if 0 <= t - 1 < NT:
                    xn2_transposes(t - 1)
            pe.wait_ge(slots_done, NT)
            for t in range(NT):
                last = pe.matmul(psum[:, 7, 128:128 + E], onesb[:, :], chosen[:, t, :], start=(t == 0), stop=(t == NT - 1))
            last.then_inc(count_ready, 1)

            def ex_transposes(i, b):
                pe.wait_ge(gx_load[b], slot_loads(i, b))
                wait(pe, exlo_done, i)
                for k in range(KD):
                    last = pe.transpose(psum[:, 2 + k // 4, (k % 4) * P:(k % 4 + 1) * P], gx[:, b, k:D:KD], ident[:, :])
                last.then_inc(ext_ready, 1)

            def gate_up(i, b):
                pe.wait_ge(exlo_done, i + 1)
                wait(pe, h_ready, i)
                for c in range(8):
                    number, _, r, _ = gu_piece(i, c)
                    pe.wait_ge(elo_done, number + 1)
                    for kk in range(2):
                        k = 2 * (c // 2) + kk
                        last = product3(psum[:, c % 2, :], (ex_hi[:, b, k, :], ex_lo[:, b, k, :]),
                                        (e_hi[:, r, kk, :], e_lo[:, r, kk, :]), k == 0, k == KD - 1)
                    last.then_inc(piece_used, 1)

            def down(piece, i):
                pe.wait_ge(htlo_done, i + 1)
                wait(pe, y_left, i)
                wait(pe, y_right, i)
                for c in range(4):
                    number, _, r, _ = piece(c)
                    pe.wait_ge(elo_done, number + 1)
                    for half in range(2):
                        last = product3(psum[:, 4 + half, :], (ht_hi[:, c, :], ht_lo[:, c, :]),
                                        (e_hi[:, r, half, :], e_lo[:, r, half, :]), c == 0, c == 3)
                    last.then_inc(piece_used, 1)

            def h_turn(i):
                pe.wait_ge(h_ready, i + 1)
                for k in range(KF):
                    last = pe.transpose(psum[:, 6, k * P:(k + 1) * P], hh[:, k:F:KF], ident[:, :])
                last.then_inc(ht_ready, 1)

            def step(i, b):
                gate_up(i, b)
                ex_transposes(i + 1, 1 - b)
                down(lambda c: down_piece(i, c), i - 1)
                h_turn(i)

            ex_transposes(0, 0)
            gate_up(0, 0)
            ex_transposes(1, 1)
            h_turn(0)
            step(1, 1)
            n_half = load_half_steps(pe)
            with pe.Fori(1, n_half) as j:
                step(2 * j, 0)
                step(2 * j + 1, 1)
            last_i = 2 * n_half - 1
            down(lambda c: last_piece(last_i, c), last_i)

        @block.scalar
        def _(act):
            steps = [0]

            def link(ins):
                steps[0] += 1
                ins.then_inc(act_step, 1)
                act.wait_ge(act_step, steps[0])

            def w_part(m):
                act.wait_ge(w_load[m % 2], 16 * (m // 2 + 1 + (3 if m >= G and m % 2 == G % 2 else 0)))
                if m >= 4:
                    act.wait_ge(proj_ready, last_use[m - 4])
                act.activation(w_hi[:, m % 4, :, :], w_st[:, m % 2, :, :], ACT.Copy).then_inc(whi_done, 1)

            def x_part(t):
                act.wait_ge(xt_ready, t + 1)
                b = 4 + 2 * (t % 2)
                for half in range(2):
                    ins = act.activation(xT_hi[:, 4 * half:4 * half + 4, t * P:(t + 1) * P],
                                         psum[:, b + half, :].rearrange("p (k n) -> p k n", k=4), ACT.Copy)
                ins.then_inc(xhi_done, 1)

            def ring_slot(i):
                if i >= 4:
                    act.wait_ge(ev_out[i % 4], 16 * (i // 4))

            def take(n):
                kind, m, s = proj[n]
                a, length = SEGS[s]
                src = psum[:, n % 4, 0:length]
                if kind != "g":
                    act.wait_ge(proj_ready, n + 1)
                if kind == "u":
                    act.wait_ge(pads_zero, 1)
                    parts = [(0, pos[0], S0), (S0, pos[1], length - S0)] if s == 0 else [(0, pos[1] + a - S0, length)]
                    for col, first, w in parts:
                        ins = act.activation(u_ext[:, m, first:first + w], src[:, col:col + w], ACT.Copy)
                    ins.then_inc(act_took, 1)
                elif kind == "o":
                    i = place["o", m - O, s]
                    ring_slot(i)
                    act.activation(ev[:, i % 4, 0:length], src, ACT.Sigmoid).then_inc(ev_full, 1)
                elif kind == "k":
                    if m == K and s == 0:
                        act.wait_ge(dec_ready, 1)
                    act.activation(kT[:, m - K, a:a + length], src, ACT.Copy, scale=float(P) ** -0.5).then_inc(act_took, 1)
                elif kind == "q":
                    act.activation(qT[:, m - Q, a:a + length], src, ACT.Copy).then_inc(act_took, 1)
                if s == len(SEGS) - 1 and m + 4 < NSL:
                    w_part(m + 4)
                if kind == "o" and m == O + 1 and s == 0:
                    act.wait_ge(g_abs, 1)
                    act.activation(g_e[:, :], g_e[:, :], ACT.Exp).then_inc(g_exp, 1)
                    act.wait_ge(g_exp, 1)
                    act.activation(g_e[:, :], g_e[:, :], ACT.Ln, bias=onec[0:64, :], scale=1.0).then_inc(g_ln, 1)
                for g in mixer_after.get(n, ()):
                    for s2 in range(len(SEGS)):
                        i = place["a", g, s2]
                        ring_slot(i)
                        act.wait_ge(mixer_ready, 3 * g + s2 + 1)
                        act.activation(ev[:, i % 4, 0:SEGS[s2][1]], psum[:, 4 + (3 * g + s2) % 4, 0:SEGS[s2][1]],
                                       ACT.Copy, scale=pscale[:, g:g + 1]).then_inc(ev_full, 1)
            act.wait_ge(consts_done, 2)
            for t in range(NT):
                act.wait_ge(x_load[t % 3], 16 * (t // 3 + 1))
                act.activation(junk[:, :], x_in[:, t % 3, :], ACT.Square,
                               accum_out=stat[:, 0, t:t + 1]).then_inc(sq_done, 1)
                act.wait_ge(sq_done, t + 1)
                act.activation(stat[:, 1, t:t + 1], stat[:, 0, t:t + 1], ACT.Sqrt, bias=epsc[:, :],
                               scale=1.0 / D).then_inc(root_done, 1)
                if t == NT - 1:
                    take(0)
                if t >= 1:
                    x_part(t - 1)
                if 2 <= t < 6:
                    w_part(t - 2)
            take(1)
            x_part(NT - 1)
            for n in range(2, NPROJ):
                take(n)

            act.wait_ge(turned, 1)
            act.wait_ge(dec_ready, 1)
            for b in range(4):
                cs = min(3, NT - 3 * b)
                for kind4 in range(4):
                    for d in range(2):
                        src = psum[:, 4 + b, 0:cs * 144].rearrange("p (c r) -> p c r", c=cs)
                        o = kind4 * 36 + 32 * d
                        act.activation(cols[:, 3 * b:3 * b + cs, kind4, d * H:(d + 1) * H], src[:, :, o:o + H],
                                       ACT.Exp if kind4 else ACT.Copy)
            act.activation(decay[:, :, :], psum[:, 7, 256:256 + 2 * H * NT].rearrange("p (r c) -> p r c", r=2 * H),
                           ACT.Exp).then_inc(cols_done, 1)
            for t in range(NT):
                act.wait_ge(proj_ready, NPROJ + t + 1)
                src = psum[:, (NPROJ + t) % 4, :].rearrange("p (h n) -> p h n", h=H)
                if t == 0:
                    act.wait_ge(v_ones, 1)
                act.activation(v[:, t, 0:H - 1, 0:P], src[:, 1:H, :], ACT.Copy)
                act.activation(v[:, t, H - 1, 0:P], src[:, 0, :], ACT.Copy).then_inc(v_took, 1)
            for i in range(4):
                act.wait_ge(ev_out[i], 16 * len(ring[i::4]))

            act.wait_ge(cols_done, 1)
            def head_squares(i):
                t = order[i]
                act.wait_ge(hsum_done, i + 1)
                for h in range(H):
                    ins = act.activation(h_fb[:, 1, t, h * P:(h + 1) * P], h_fb[:, 0, t, h * P:(h + 1) * P],
                                         ACT.Square, accum_out=hstat[:, 0, i, h:h + 1])
                ins.then_inc(hss_done, 1)

            squared = 0
            for n in range(NU):
                step, pair, d, ck = unit(n)
                while squared < NT and complete_after(order[squared]) + 5 <= n:
                    head_squares(squared)
                    squared += 1
                act.wait_ge(kq_ready, n + 1)
                if n >= 2:
                    act.wait_ge(kv_ready, n - 1)
                for hh_ in range(2):
                    r = d * H + 2 * pair + hh_
                    ins = act.activation(uk[:, d, hh_, :], psum[:, 4 * d, hh_ * P:(hh_ + 1) * P], ACT.Copy,
                                         scale=cols[:, ck, 3, r:r + 1])
                ins.then_inc(uk_done, 1)
                act.wait_ge(nm_ready, n + 1)
                if n >= 2:
                    act.wait_ge(s_done, n - 1)
                for hh_ in range(2):
                    r = d * H + 2 * pair + hh_
                    ins = act.activation(wgt[:, d, hh_, :], psum[:, 4 * d + 1, hh_ * P:(hh_ + 1) * P], ACT.Exp,
                                         bias=cols[:, ck, 0, r:r + 1])
                ins.then_inc(wgt_done, 1)
                if n % 4 == 3 and step < KD:
                    i = step
                    act.wait_ge(wo_load[i % 2], 16 * (i // 2 + 1))
                    act.activation(wo_hi[:, i, :], w_st[:, i % 2, :, :].rearrange("p k n -> p (k n)"),
                                   ACT.Copy).then_inc(wohi_done, 1)

            def head_roots(first, stop):
                act.wait_ge(hss_done, stop)
                act.activation(hstat[:, 1, first:stop, :], hstat[:, 0, first:stop, :], ACT.Sqrt, bias=epsc[:, :],
                               scale=1.0 / P).then_inc(hroot_done, 1)

            def norm_heads(i):
                if i in (0, squared):
                    act.wait_ge(hrecip_done, 1 if i == 0 else 2)
                t = order[i]
                for h in range(H):
                    ins = act.activation(h_fb[:, 0, t, h * P:(h + 1) * P], h_fb[:, 0, t, h * P:(h + 1) * P], ACT.Copy,
                                         scale=hstat[:, 1, i, h:h + 1])
                ins.then_inc(hn_done, 1)

            def mix_hi_part(i):
                act.wait_ge(mixf_done, i + 1)
                if i >= 2:
                    act.wait_ge(out_ready, i - 1)
                act.activation(mix_hi[:, i % 2, :, :], mixf[:, i % 2, :, :], ACT.Copy).then_inc(mixhi_done, 1)

            def second_root(i):
                act.wait_ge(x1_done, i + 1)
                if i >= 1:
                    act.wait_ge(x1root_done, i)
                link(act.activation(sq_c[:, :], x1[:, order[i], :], ACT.Square, accum_out=stat[:, 2, i:i + 1]))
                act.activation(stat[:, 3, i:i + 1], stat[:, 2, i:i + 1], ACT.Sqrt, bias=epsc[:, :],
                               scale=1.0 / D).then_inc(x1root_done, 1)

            def xn2T_part(i):
                act.wait_ge(xn2T_ready, i + 1)
                if i >= 1:
                    act.wait_ge(logits_ready, i)
                for half in range(2):
                    ins = act.activation(xn2T[:, 4 * half:4 * half + 4, :],
                                         psum[:, 5 + half, :].rearrange("p (k n) -> p k n", k=4), ACT.Copy)
                ins.then_inc(xn2T_done, 1)

            assert squared == EARLY
            head_roots(0, squared)
            norm_heads(0)
            norm_heads(1)
            for i in range(squared, NT):
                head_squares(i)
            head_roots(squared, NT)
            act.wait_ge(h_done, NU)
            mix_hi_part(0)
            norm_heads(2)
            for t in range(NT + 2):
                if 0 <= t - 1 < NT:
                    second_root(t - 1)
                if 0 <= t - 2 < NT:
                    xn2T_part(t - 2)
                if t + 1 < NT:
                    mix_hi_part(t + 1)
                if t + 3 < NT:
                    norm_heads(t + 3)
            act.wait_ge(chosen_done, NT)
            act.activation(rgs[:, :, :], rgs[:, :, :], ACT.Exp)
            act.activation(rd21[:, :], rd21[:, :], ACT.Exp).then_inc(wexp_done, 1)

            def hi_part(piece):
                number, slot, r, loads = piece
                act.wait_ge(e_load[slot], 16 * loads)
                wait(act, piece_used, number - NRG + 1)
                act.activation(e_hi[:, r, :, :], e_st[:, slot, :, :], ACT.Copy).then_inc(ehi_done, 1)

            def ex_hi_part(i, b):
                act.wait_ge(ext_ready, i + 1)
                for half in range(2):
                    ins = act.activation(ex_hi[:, b, 4 * half:4 * half + 4, :],
                                         psum[:, 2 + half, :].rearrange("p (k n) -> p k n", k=4), ACT.Copy)
                ins.then_inc(exhi_done, 1)

            def ht_hi_part(i):
                act.wait_ge(ht_ready, i + 1)
                act.activation(ht_hi[:, :, :], psum[:, 6, :].rearrange("p (k n) -> p k n", k=KF),
                               ACT.Copy).then_inc(hthi_done, 1)

            def y_half(i, b, whole):
                act.wait_ge(piece_used, whole)
                act.activation(yo[:, b, 0:512], psum[:, 4, :], ACT.Copy).then_inc(y_left, 1)

            def silu(i):
                act.wait_ge(piece_used, gu_piece(i, 7)[0] + 1)
                wait(act, h_ready, i)
                act.activation(sg[:, :], psum[:, 0, :], ACT.Silu).then_inc(sg_done, 1)

            def step(i, b):
                for c in range(2):
                    hi_part(gu_piece(i, c))
                ht_hi_part(i - 1)
                hi_part(gu_piece(i, 2))
                if not isinstance(i, int) or i >= 2:
                    y_half(i - 2, b, down_piece(i - 1, 3)[0] + 1)
                for c in range(3, 8):
                    hi_part(gu_piece(i, c))
                for c in range(2):
                    hi_part(down_piece(i, c))
                silu(i)
                ex_hi_part(i + 1, 1 - b)
                for c in range(2, 4):
                    hi_part(down_piece(i, c))

            act.wait_ge(rounds_done, 1)
            for c in range(4):
                hi_part(gu_piece(0, c))
            ex_hi_part(0, 0)
            for c in range(4, 8):
                hi_part(gu_piece(0, c))
            silu(0)
            ex_hi_part(1, 1)
            step(1, 1)
            n_half = load_half_steps(act)
            with act.Fori(1, n_half) as j:
                step(2 * j, 0)
                step(2 * j + 1, 1)
            last_i = 2 * n_half - 1
            ht_hi_part(last_i)
            y_half(last_i - 1, 0, down_piece(last_i, 3)[0] + 1)
            for c in range(4):
                hi_part(last_piece(last_i, c))
            y_half(last_i, 1, last_piece(last_i, 3)[0] + 1)

            for t in range(NT):
                act.wait_ge(f_sum, t + 1)
                if t >= 1:
                    act.wait_ge(f_root, t)
                link(act.activation(f_sq[:, :], x1[:, t, :], ACT.Square, accum_out=wts[:, 2, t:t + 1]))
                act.activation(wts[:, 3, t:t + 1], wts[:, 2, t:t + 1], ACT.Sqrt, bias=epsc[:, :],
                               scale=1.0 / D).then_inc(f_root, 1)

        @block.vector
        def _(dve):
            steps = [0]

            def link(ins):
                steps[0] += 1
                ins.then_inc(dve_step, 1)
                dve.wait_ge(dve_step, steps[0])

            def w_part(m):
                dve.wait_ge(whi_done, m + 1)
                dve.tensor_tensor(w_lo[:, m % 4, :, :], w_st[:, m % 2, :, :], w_hi[:, m % 4, :, :].bitcast(F32),
                                  ALU.subtract).then_inc(wlo_done, 1)
                if m == G - 2:
                    dve.wait_ge(wlo_done, m + 1)
                    dve.memset(w_st[:, G % 2, :, :], 0.0).then_inc(gate_slot_zero, 1)

            def x_part(t):
                dve.wait_ge(xhi_done, t + 1)
                b = 4 + 2 * (t % 2)
                for half in range(2):
                    k = slice(4 * half, 4 * half + 4)
                    ins = dve.tensor_tensor(xT_lo[:, k, t * P:(t + 1) * P],
                                            psum[:, b + half, :].rearrange("p (k n) -> p k n", k=4),
                                            xT_hi[:, k, t * P:(t + 1) * P].bitcast(F32), ALU.subtract)
                ins.then_inc(xlo_done, 1)

            for first, width in ((0, 8), (pos[0] + S0, 8), (pos[1] + S1, 8)):
                ins = dve.memset(u_ext[:, :, first:first + width], 0.0)
            ins.then_inc(pads_zero, 1)
            dve.wait_ge(g1_in, 16)
            for t in range(NT):
                dve.wait_ge(root_done, t + 1)
                link(dve.reciprocal(stat[:, 1, t:t + 1], stat[:, 1, t:t + 1]))
                if t >= 2:
                    dve.wait_ge(xt_ready, t - 1)
                dve.scalar_tensor_tensor(out=xn[:, t % 2, :], in0=x_in[:, t % 3, :], scalar=stat[:, 1, t:t + 1],
                                         in1=g1_b[:, :], op0=ALU.mult, op1=ALU.mult).then_inc(xn_done, 1)
                if t >= 1:
                    x_part(t - 1)
                if 2 <= t < 6:
                    w_part(t - 2)
            x_part(NT - 1)

            def pool_group(g):
                w = WINDOWS[g]
                dve.wait_ge(act_took, 2 * NG + g + 1)
                wait(dve, pooled, g)
                src, bufs, r = u_ext[:, g, :], (ps_a, ps_b), 1
                link(dve.tensor_tensor(ps_a[:, 1:PADW], src[:, 0:PADW - 1], src[:, 1:PADW], ALU.add))
                lo, hi, cur = 1, PADW, 0
                while 2 * r < w:
                    lo, hi = lo + r, hi - r
                    link(dve.tensor_tensor(bufs[1 - cur][:, lo:hi], bufs[cur][:, lo - r:hi - r],
                                           bufs[cur][:, lo + r:hi + r], ALU.add))
                    cur, r = 1 - cur, 2 * r
                sums = bufs[cur]
                for seq, length in enumerate((S0, S1)):
                    for c, e in ((pos[seq], 0), (pos[seq] + length - 8, 8)):
                        ins = dve.tensor_tensor(sums[:, c:c + 8], sums[:, c:c + 8], edge[:, g, e:e + 8], ALU.mult)
                link(ins)
                for seq, length in enumerate((S0, S1)):
                    a = pos[seq]
                    ins = dve.scalar_tensor_tensor(out=u_ext[:, g, a:a + length], in0=sums[:, a:a + length],
                                                   scalar=1.0 / w, in1=u_ext[:, g, a:a + length],
                                                   op0=ALU.mult, op1=ALU.subtract)
                ins.then_inc(pooled, 1)

            def by_direction(fn):
                fn(slice(0, 32), slice(0, T), slice(0, T))
                ins = None
                for a, b in ((0, S0), (S0, T)):
                    rev = slice(b - 1, a - 1 if a else None, -1)
                    ins = fn(slice(32, 64), slice(a, b), rev)
                return ins

            def turn(dst, src):
                return by_direction(lambda r, o, i: dve.tensor_copy(dst[r, o], src[r, i]))

            def ends(x):
                return x[:, :].rearrange("p (c n) -> p c n", n=P)[:, :, P - 1]

            def starts(x):
                return x[:, :].rearrange("p (c n) -> p c n", n=P)[:, :, 0]

            def per_chunk(x):
                return x[:, :].unsqueeze(2).broadcast_to([64, NT, P])

            def chunked(x):
                return x[:, :].rearrange("p (c n) -> p c n", n=P)

            def gates_in(s, n):
                a, length = SEGS[s]
                dve.wait_ge(proj_ready, n + 1)
                if s == 0:
                    dve.wait_ge(consts_in, 16 * 11)
                dve.tensor_scalar(g_i[:, a:a + length], psum[0:64, n % 4, 0:length], gbias[:, 0:1], None, ALU.add)
                dve.tensor_scalar(g_f[:, a:a + length], psum[64:P, n % 4, 0:length], gbias[:, 1:2], None,
                                  ALU.add).then_inc(gates_took, 1)

            def gate_rows():
                dve.wait_ge(g_ln, 1)
                link(dve.scalar_tensor_tensor(out=g_f[:, :], in0=g_f[:, :], scalar=0.0, in1=g_e[:, :],
                                              op0=ALU.min, op1=ALU.subtract))
                turn(g_b, g_f)
                link(turn(g_e, g_i))
                for c in range(NT):
                    ins = dve.tensor_tensor_scan(g_f[:, c * P:(c + 1) * P], g_b[:, c * P:(c + 1) * P],
                                                 zero_row[:, :], 0.0, ALU.add, ALU.add)
                link(ins)
                dve.tensor_tensor(g_e[:, :], g_e[:, :], g_f[:, :], ALU.subtract)
                dve.memset(mprev[:, :], 0.0)
                link(dve.memset(g_b[:, :], 0.0))
                b_end, move = ends(g_f), starts(g_b)
                dve.tensor_copy(move[:, 1:C0], b_end[:, 0:C0 - 1])
                link(dve.tensor_copy(move[:, C0 + 1:NT], b_end[:, C0:NT - 1]))
                for a, b in ((0, S0), (S0, T)):
                    ins = dve.tensor_tensor_scan(g_m[:, a:b], g_b[:, a:b], g_e[:, a:b], 0.0, ALU.add, ALU.max)
                link(ins)
                m_end = ends(g_m)
                for a, b in ((0, C0), (C0, NT)):
                    dve.tensor_tensor(mprev[:, a + 1:b], m_end[:, a:b - 1], b_end[:, a:b - 1], ALU.add)
                link(dve.tensor_copy(mlast[:, :], m_end))
                dve.wait_ge(list_set, 16)
                by_direction(lambda r, o, i: dve.tensor_scalar(negm[r, o], g_m[r, i], -1.0, None, ALU.mult))
                dve.tensor_tensor(chunked(g_i), per_chunk(mprev), chunked(g_m), ALU.subtract)
                link(dve.scalar_tensor_tensor(out=g_b[:, :], in0=g_f[:, :], scalar=-1.0, in1=g_m[:, :],
                                              op0=ALU.mult, op1=ALU.subtract))
                link(dve.tensor_tensor(chunked(g_f), chunked(g_e), per_chunk(mlast), ALU.subtract))
                link(turn(g_m, g_e))
                link(turn(g_e, g_i))
                link(turn(g_i, g_b))
                turn(g_b, g_f)
                dve.tensor_tensor(mlast[:, :], mprev[:, :], mlast[:, :], ALU.subtract).then_inc(rows_ready, 1)

            for n, (kind, m, s) in enumerate(proj):
                if kind == "g":
                    gates_in(s, n)
                if s == len(SEGS) - 1 and m + 4 < NSL:
                    w_part(m + 4)
                if kind == "g" and s == len(SEGS) - 1:
                    dve.wait_ge(gates_took, 3)
                    dve.scalar_tensor_tensor(out=g_e[:, :], in0=g_f[:, :], scalar=-1.0, in1=g_f[:, :],
                                             op0=ALU.mult, op1=ALU.min).then_inc(g_abs, 1)
                    dve.wait_ge(edges_done, N_EDGE)
                    pool_group(0)
                    pool_group(1)
                    gate_rows()
                    pool_group(2)
                    pool_group(3)
            dve.wait_ge(dec_ready, 1)
            dve.memset(v[:, :, :, P:P + 1], 1.0).then_inc(v_ones, 1)
            dve.wait_ge(proj_ready, NPROJ + NT)
            dve.memset(state[:, :, :, :], 0.0).then_inc(state_zero, 1)

            def pair_of(x):
                return x[:, 0:2 * (P + 1)].rearrange("p (h n) -> p h n", h=2)

            def weighted(n):
                step, pair, d, ck = unit(n)
                dve.wait_ge(wgt_done, n + 1)
                if n >= 2:
                    dve.wait_ge(kv_ready, n - 1)
                dve.tensor_tensor(sT[:, d, :, :], psum[:, 4 * d, 2 * P:4 * P].rearrange("p (h n) -> p h n", h=2),
                                  wgt[:, d, :, :], ALU.mult).then_inc(s_done, 1)

            def heads_out(n):
                step, pair, d, ck = unit(n)
                r = d * H + 2 * pair
                dve.wait_ge(kv_ready, n + 1)
                if carries(step):
                    for hh_ in range(2):
                        ins = dve.scalar_tensor_tensor(
                            out=state[:, d, 2 * pair + hh_, :], in0=state[:, d, 2 * pair + hh_, :],
                            scalar=decay[:, r + hh_, step:step + 1],
                            in1=psum[:, 4 * d, hh_ * (P + 1):(hh_ + 1) * (P + 1)], op0=ALU.mult, op1=ALU.add)
                else:
                    ins = dve.memset(state[:, d, 2 * pair:2 * pair + 2, :], 0.0)
                ins.then_inc(state_done, 1)
                wait(dve, h_done, n - 1)
                link(dve.tensor_tensor(tq[:, d, :, :], pair_of(psum[:, 4 * d + 3, :]),
                                       cols[:, ck, 1, r:r + 2].unsqueeze(2).broadcast_to([P, 2, P + 1]), ALU.mult))
                dve.tensor_tensor(tq[:, d, :, :], tq[:, d, :, :], pair_of(psum[:, 4 * d + 2, :]), ALU.add).then_inc(num_done, 1)
                dve.wait_ge(num_done, n + 1)
                link(dve.tensor_tensor(dn[:, d, :], tq[:, d, :, P], cols[:, ck, 2, r:r + 2], ALU.max))
                link(dve.scalar_tensor_tensor(out=dn[:, d, :], in0=tq[:, d, :, P], scalar=-1.0,
                                              in1=dn[:, d, :], op0=ALU.mult, op1=ALU.max))
                link(dve.reciprocal(rdn[:, d, :], dn[:, d, :]))
                dve.tensor_tensor(h_fb[:, d, ck, 2 * pair * P:(2 * pair + 2) * P].rearrange("p (h n) -> p h n", h=2),
                                  tq[:, d, :, 0:P], rdn[:, d, :].unsqueeze(2).broadcast_to([P, 2, P]),
                                  ALU.mult).then_inc(h_done, 1)

            dve.wait_ge(cols_done, 1)
            for n in range(NU + 1):
                if n < NU:
                    weighted(n)
                if n >= 1:
                    heads_out(n - 1)
                if n % 4 == 0 and 1 <= n // 4 <= KD:
                    i = n // 4 - 1
                    dve.wait_ge(wohi_done, i + 1)
                    dve.tensor_tensor(wo_lo[:, i, :], w_st[:, i % 2, :, :].rearrange("p k n -> p (k n)"),
                                      wo_hi[:, i, :].bitcast(F32), ALU.subtract).then_inc(wolo_done, 1)

            def mix(i):
                b = i % 2
                dve.wait_ge(c_in[b], 32 * (i // 2 + 1))
                dve.wait_ge(hT_ready, i + 1)
                for k in range(H):
                    ins = dve.scalar_tensor_tensor(out=mixf[:, b, NG + k, :], in0=psum[:, 4, k * P:(k + 1) * P],
                                                   scalar=hgain[:, k:k + 1], in1=og[:, b, k, :],
                                                   op0=ALU.mult, op1=ALU.mult)
                ins.then_inc(mixf_done, 1)

            def mix_lo_part(i):
                b = i % 2
                dve.wait_ge(mixhi_done, i + 1)
                dve.tensor_tensor(mix_lo[:, b, :, :], mixf[:, b, :, :], mix_hi[:, b, :, :].bitcast(F32),
                                  ALU.subtract).then_inc(mixlo_done, 1)

            def residual(i):
                b, t = i % 2, order[i]
                dve.wait_ge(out_ready, i + 1)
                dve.wait_ge(xc_in[b], 16 * (i // 2 + 1))
                x1_t = x1[:, t, :].rearrange("p (a n) -> p a n", a=2)
                dve.tensor_tensor(x1_t, x1_t, two(2 * b), ALU.add).then_inc(x1_done, 1)

            def second_norm(i):
                b, t = i % 2, order[i]
                dve.wait_ge(x1root_done, i + 1)
                link(dve.reciprocal(stat[:, 3, i:i + 1], stat[:, 3, i:i + 1]))
                if i >= 2:
                    dve.wait_ge(xn2_out[b], 16 * (i // 2))
                    dve.wait_ge(xn2T_ready, i - 1)
                if i == 0:
                    dve.wait_ge(g2_in, 16)
                dve.scalar_tensor_tensor(out=xn2[:, b, :], in0=x1[:, t, :], scalar=stat[:, 3, i:i + 1],
                                         in1=g2_b[:, :], op0=ALU.mult, op1=ALU.mult).then_inc(xn2_done, 1)

            lg, el = rt[:, 16:16 + GR], rt[:, 16 + GR:16 + NL]
            gtop, gr, etop, er, etop2 = (rt[:, 52 + i:53 + i] for i in range(5))
            eq, oh_g, oh_e = rt[:, 60:68], rt[:, 68:72], rt[:, 72:88]
            esel, esel2 = rt[:, 88:96], rt[:, 96:104]
            emask, both, prod, rank = rt[:, 128:160], rt[:, 160:224], rt[:, 224:288], rt[:, 288:320]
            slot_f = rt[:, 320:322]

            def first_max(values, n, top, key, one_hot):
                link(dve.tensor_reduce(top, values, AX.X, ALU.max))
                link(dve.scalar_tensor_tensor(out=eq[:, 0:n], in0=values, scalar=top, in1=ramp[:, EPG - n:EPG],
                                              op0=ALU.is_ge, op1=ALU.mult))
                link(dve.tensor_reduce(key, eq[:, 0:n], AX.X, ALU.max))
                link(dve.tensor_scalar(one_hot, ramp[:, EPG - n:EPG], key, None, ALU.is_equal))

            def route(t):
                dve.wait_ge(logits_ready, t + 1)
                wait(dve, chosen_done, t)
                dve.tensor_tensor(rt[:, 16:16 + NL], psum[:, 7, 0:NL], rbias[:, :], ALU.add).then_inc(logits_taken, 1)
                dve.wait_ge(logits_taken, t + 1)
                first_max(lg, GR, gtop, gr, oh_g)
                dve.tensor_scalar(rgs[:, order[t], :], lg, gtop, None, ALU.subtract)
                by_group = emask.rearrange("p (g e) -> p g e", g=GR)
                link(dve.tensor_tensor(by_group, el.rearrange("p (g e) -> p g e", g=GR),
                                       oh_g.unsqueeze(2).broadcast_to([P, GR, EPG]), ALU.mult))
                link(dve.tensor_reduce(esel, emask.rearrange("p (g e) -> p e g", g=GR), AX.X, ALU.add))
                first_max(esel, EPG, etop, er, oh_e[:, 0:EPG])
                link(dve.scalar_tensor_tensor(out=esel2, in0=oh_e[:, 0:EPG], scalar=MASKED, in1=esel,
                                              op0=ALU.mult, op1=ALU.add))
                first_max(esel2, EPG, etop2, er, oh_e[:, EPG:2 * EPG])
                dve.tensor_tensor(rd21[:, order[t]:order[t] + 1], etop2, etop, ALU.subtract)
                for k in range(2):
                    ins = dve.tensor_tensor(both[:, k * E:(k + 1) * E].rearrange("p (g e) -> p g e", g=GR),
                                            oh_g.unsqueeze(2).broadcast_to([P, GR, EPG]),
                                            oh_e[:, k * EPG:(k + 1) * EPG].unsqueeze(1).broadcast_to([P, GR, EPG]),
                                            ALU.mult)
                link(ins)
                dve.tensor_tensor(chosen[:, t, :], both[:, 0:E], both[:, E:2 * E], ALU.add).then_inc(chosen_done, 1)

            def list_rows(t):
                dve.wait_ge(rank_ready, t + 1)
                wait(dve, slots_done, t)
                link(dve.tensor_tensor(rank, psum[:, 7, 64:64 + E], ebase[:, :], ALU.add))
                link(dve.tensor_tensor(prod.rearrange("p (k e) -> p k e", k=2), both.rearrange("p (k e) -> p k e", k=2),
                                       rank.unsqueeze(1).broadcast_to([P, 2, E]), ALU.mult))
                link(dve.tensor_reduce(slot_f, prod.rearrange("p (k e) -> p k e", k=2), AX.X, ALU.add))
                dve.tensor_copy(slot_i[:, t, :], slot_f).then_inc(slots_done, 1)

            def head_reciprocal(part, first, stop):
                dve.wait_ge(hroot_done, part)
                dve.reciprocal(hstat[:, 1, first:stop, :], hstat[:, 1, first:stop, :]).then_inc(hrecip_done, 1)

            dve.wait_ge(consts_done, N_CONST)
            dve.wait_ge(h_done, NU)
            head_reciprocal(1, 0, EARLY)
            mix(0)
            head_reciprocal(2, EARLY, NT)
            mix_lo_part(0)
            for t in range(NT + 3):
                if 0 <= t - 1 < NT:
                    residual(t - 1)
                if t + 1 < NT:
                    mix(t + 1)
                if 0 <= t - 3 < NT:
                    list_rows(t - 3)
                if 0 <= t - 1 < NT:
                    second_norm(t - 1)
                if t + 1 < NT:
                    mix_lo_part(t + 1)
                if 0 <= t - 2 < NT:
                    route(t - 2)
            dve.wait_ge(count_ready, 1)
            link(dve.tensor_reduce(rt[0:1, 330:331], psum[0:1, 7, 128:128 + E], AX.X, ALU.max))
            link(dve.tensor_scalar(half_steps[0:1, 1:2], rt[0:1, 330:331], -1.0, None, ALU.add))
            link(dve.tensor_scalar(half_steps[0:1, 2:3], half_steps[0:1, 1:2], 7, None, ALU.logical_shift_right))
            dve.tensor_scalar(half_steps[0:1, 0:1], half_steps[0:1, 2:3], 4, None,
                              ALU.logical_shift_left).then_inc(rounds_done, 1)
            dve.wait_ge(wexp_done, 1)
            dve.tensor_scalar(wts[:, 1, :], rd21[:, :], 1.0, None, ALU.add)
            link(dve.tensor_reduce(wts[:, 0, :], rgs[:, :, :], AX.X, ALU.add))
            link(dve.tensor_tensor(wts[:, 2, :], wts[:, 0, :], wts[:, 1, :], ALU.mult))
            link(dve.reciprocal(wts[:, 0, :], wts[:, 2, :]))
            link(dve.tensor_tensor(wts[:, 1, :], wts[:, 0, :], rd21[:, :], ALU.mult))

            def lo_part(piece):
                number, slot, r, _ = piece
                dve.wait_ge(ehi_done, number + 1)
                dve.tensor_tensor(e_lo[:, r, :, :], e_st[:, slot, :, :], e_hi[:, r, :, :].bitcast(F32),
                                  ALU.subtract).then_inc(elo_done, 1)

            def ex_lo_part(i, b):
                dve.wait_ge(exhi_done, i + 1)
                for half in range(2):
                    k = slice(4 * half, 4 * half + 4)
                    ins = dve.tensor_tensor(ex_lo[:, b, k, :], psum[:, 2 + half, :].rearrange("p (k n) -> p k n", k=4),
                                            ex_hi[:, b, k, :].bitcast(F32), ALU.subtract)
                ins.then_inc(exlo_done, 1)

            def ht_lo_part(i):
                dve.wait_ge(hthi_done, i + 1)
                dve.tensor_tensor(ht_lo[:, :, :], psum[:, 6, :].rearrange("p (k n) -> p k n", k=KF),
                                  ht_hi[:, :, :].bitcast(F32), ALU.subtract).then_inc(htlo_done, 1)

            def source_rows(i, b):
                dve.wait_ge(row_load[b], slot_loads(i, b))
                wait(dve, row_done, i)
                dve.tensor_copy(row_f[:, 0:1], row_raw[:, b:b + 1]).then_inc(row_step, 1)
                dve.wait_ge(row_step, 3 * i + 1)
                dve.tensor_scalar(row_f[:, 1:2], row_f[:, 0:1], float(T), float(T), ALU.is_ge, ALU.mult).then_inc(row_step, 1)
                dve.wait_ge(row_step, 3 * i + 2)
                dve.tensor_tensor(row_f[:, 2:3], row_f[:, 0:1], row_f[:, 1:2], ALU.subtract).then_inc(row_step, 1)
                dve.wait_ge(row_step, 3 * i + 3)
                dve.tensor_scalar(row_g[:, b:b + 1], row_f[:, 2:3], float(T - 1), None, ALU.min).then_inc(row_done, 1)

            def keep_rows(i, b):
                wait(dve, y_out, 16 * (i - 1))
                dve.tensor_copy(row_s[:, b:b + 1], row_raw[:, b:b + 1]).then_inc(rows_copied, 1)

            def y_half(i, b, whole):
                dve.wait_ge(piece_used, whole)
                dve.tensor_copy(yo[:, b, 512:1024], psum[:, 5, :]).then_inc(y_right, 1)

            def hidden(i):
                dve.wait_ge(sg_done, i + 1)
                wait(dve, ht_ready, i)
                dve.tensor_tensor(hh[:, :], psum[:, 1, :], sg[:, :], ALU.mult).then_inc(h_ready, 1)

            def step(i, b):
                for c in range(2):
                    lo_part(gu_piece(i, c))
                ht_lo_part(i - 1)
                source_rows(i + 1, 1 - b)
                lo_part(gu_piece(i, 2))
                if not isinstance(i, int) or i >= 2:
                    y_half(i - 2, b, down_piece(i - 1, 3)[0] + 1)
                for c in range(3, 8):
                    lo_part(gu_piece(i, c))
                for c in range(2):
                    lo_part(down_piece(i, c))
                hidden(i)
                ex_lo_part(i + 1, 1 - b)
                for c in range(2, 4):
                    lo_part(down_piece(i, c))
                keep_rows(i, b)

            for c in range(2):
                lo_part(gu_piece(0, c))
            source_rows(0, 0)
            source_rows(1, 1)
            for c in range(2, 4):
                lo_part(gu_piece(0, c))
            ex_lo_part(0, 0)
            for c in range(4, 8):
                lo_part(gu_piece(0, c))
            hidden(0)
            ex_lo_part(1, 1)
            keep_rows(0, 0)
            step(1, 1)
            n_half = load_half_steps(dve)
            with dve.Fori(1, n_half) as j:
                step(2 * j, 0)
                step(2 * j + 1, 1)
            last_i = 2 * n_half - 1
            ht_lo_part(last_i)
            y_half(last_i - 1, 0, down_piece(last_i, 3)[0] + 1)
            for c in range(4):
                lo_part(last_piece(last_i, c))
            y_half(last_i, 1, last_piece(last_i, 3)[0] + 1)

            def final_sum(t):
                dve.wait_ge(f_in[t], 32)
                link(dve.scalar_tensor_tensor(out=x1[:, t, :], in0=f_y[:, t, 0, :], scalar=wts[:, 0, t:t + 1],
                                              in1=x1[:, t, :], op0=ALU.mult, op1=ALU.add))
                dve.scalar_tensor_tensor(out=x1[:, t, :], in0=f_y[:, t, 1, :], scalar=wts[:, 1, t:t + 1],
                                         in1=x1[:, t, :], op0=ALU.mult, op1=ALU.add).then_inc(f_sum, 1)

            def final_norm(t):
                dve.wait_ge(f_root, t + 1)
                link(dve.reciprocal(wts[:, 3, t:t + 1], wts[:, 3, t:t + 1]))
                if t == 0:
                    dve.wait_ge(gf_in, 16)
                dve.scalar_tensor_tensor(out=x1[:, t, :], in0=x1[:, t, :], scalar=wts[:, 3, t:t + 1],
                                         in1=gf_b[:, :], op0=ALU.mult, op1=ALU.mult).then_inc(f_done, 1)

            for t in range(NT + 1):
                if t < NT:
                    final_sum(t)
                if t >= 1:
                    final_norm(t - 1)


_INS = ["x_prompt", "x_sample", "norm1_g", "w_in", "pool_w", "pool_scale", "gate_b", "head_norm_g", "w_out",
        "norm2_g", "router_group_w", "router_group_b", "router_expert_w", "router_expert_b",
        "expert_w_gate", "expert_w_up", "expert_w_down", "final_norm_g"]


def kernel(**inputs):
    import numpy as _np
    import concourse.bacc as _bacc
    from concourse import mybir as _mybir
    from concourse.bass_utils import run_bass_kernel_spmd as _run

    nc = _bacc.Bacc("TRN2", target_bir_lowering=False, num_devices=1)
    arrays, args = {}, []
    for name in _INS:
        a = _np.ascontiguousarray(inputs[name])
        arrays[f"in_{name}_dram"] = a
        args.append(nc.dram_tensor(f"in_{name}_dram", a.shape, _mybir.dt.from_np(a.dtype), kind="ExternalInput").ap())
    for i, name in enumerate(("x_prompt", "x_sample")):
        args.append(nc.dram_tensor(f"out_{i}_dram", inputs[name].shape, _mybir.dt.float32, kind="ExternalOutput").ap())
    build(nc, *args)
    r = _run(nc, [arrays], core_ids=[0])
    return tuple(r.results[0][f"out_{i}_dram"] for i in range(2))
```

```python
from contextlib import ExitStack

import numpy as np

import concourse.bass as bass
from concourse import mybir

F32 = mybir.dt.float32
F32R = mybir.dt.float32r
BF16 = mybir.dt.bfloat16
I32 = mybir.dt.int32
ALU = mybir.AluOpType
ACT = mybir.ActivationFunctionType
AX = mybir.AxisListType

P = 128
KB = 1024
EPS = 1e-6
MASKED = -1e30


def build(nc, x_prompt, x_sample, norm1_g, w_in, pool_w, pool_scale, gate_b, head_norm_g, w_out,
          norm2_g, router_group_w, router_group_b, router_expert_w, router_expert_b,
          expert_w_gate, expert_w_up, expert_w_down, final_norm_g, y_prompt, y_sample):
    S0, D = x_prompt.shape[1:]
    S1 = x_sample.shape[1]
    T = S0 + S1
    NT = T // P
    C0 = S0 // P
    KD = D // P
    NG = pool_w.shape[1]
    WINDOWS = (2, 4, 8, 16)
    H = head_norm_g.shape[1] // P
    PW, MW = NG * P, H * P
    GR = router_group_w.shape[2]
    EPG = router_expert_w.shape[3]
    E = GR * EPG
    F = expert_w_gate.shape[3]
    KF = F // P
    NL = GR + E
    CAP = T
    SEGS = [(0, 512), (512, 512), (1024, 256)]
    assert (NT, KD, NG, H, KF, E) == (10, 8, 4, 4, 4, 32) and D == 1024

    xn2_dram = nc.dram_tensor("xn2_scratch", (T, D), F32).ap()
    y_dram = nc.dram_tensor("expert_rows", (2 * T + P, D), F32).ap()
    list_dram = nc.dram_tensor("row_lists", (E * CAP, 1), I32).ap()
    pooled_dram = nc.dram_tensor("pooledT", (PW, T), F32).ap()
    ogate_dram = nc.dram_tensor("ogateT", (MW, T), F32).ap()

    def tokens(t, a, b):
        return (a[0, t * P:(t + 1) * P, :] if t < C0 else b[0, (t - C0) * P:(t - C0 + 1) * P, :])

    base = (nc.sbuf_base + 63) // 64 * 64
    top = [base]

    def at(name, off, shape, dt):
        return nc.alloc_sbuf_tensor_at(name, shape, dt, offset=off)

    def const(name, shape, dt=F32):
        size = int(np.prod(shape[1:])) * (2 if dt == BF16 else 4)
        off = top[0]
        top[0] += (size + 31) // 32 * 32
        return at(name, off, shape, dt)

    ident = const("ident", [P, P])
    identb = const("identb", [P, P], BF16)
    maskb = const("maskb", [P, 2, P], BF16)
    laterb = const("laterb", [P, P], BF16)
    onesb = const("onesb", [P, P], BF16)
    zero_row = const("zero_row", [64, P])
    edge = const("edge", [P, NG, 16])
    wpool = const("wpool", [P, NG, P])
    pscale = const("pscale", [P, NG])
    hgain = const("hgain", [P, H])
    gbias = const("gbias", [64, 2])
    rw = const("rw", [P, KD, NL])
    rbias = const("rbias", [P, NL])
    ramp_i = const("ramp_i", [P, EPG + E], I32)
    ramp = const("ramp", [P, EPG])
    ebase = const("ebase", [P, E])
    rowval = const("rowval", [P, 2, NT], I32)
    epsc = const("epsc", [P, 1])
    onec = const("onec", [P, 1])
    cols = const("cols", [P, NT, 3, 8])
    decay = const("decay", [P, 8, NT])
    stat = const("stat", [P, 4, NT])
    hstat = const("hstat", [P, 2, NT, H])
    slot_i = const("slot_i", [P, NT, 2], I32)
    row_picks = const("row_picks", [P, 8], F32R)
    e_inter = const("e_inter", [P, T], F32R)
    negm = const("negm", [P, T], F32R)
    rt = at("rt", top[0] - 4 * T, [P, 512], F32)
    sentinel = at("sentinel", top[0] - 4 * T, [80, E * CAP // 80], I32)
    mprev = const("mprev", [64, NT])
    mlast = const("mlast", [64, NT])
    rgs = const("rgs", [P, NT, GR])
    rd21 = const("rd21", [P, NT])
    wts = const("wts", [P, 4, NT])
    chosen = const("chosen", [P, NT, E], BF16)
    half_steps = const("half_steps", [1, 4], I32)

    X0 = (top[0] + 63) // 64 * 64
    xT_hi = at("xT_hi", X0, [P, KD, T], F32R)
    xT_lo = at("xT_lo", X0 + 40 * KB, [P, KD, T], F32R)
    W0 = X0 + 80 * KB
    w_hi = at("w_hi", W0, [P, 4, KD, P], F32R)
    w_lo = at("w_lo", W0 + 16 * KB, [P, 4, KD, P], F32R)
    w_st = at("w_st", W0 + 32 * KB, [P, 2, KD, P], F32)
    Q0 = W0 + 40 * KB
    qT = at("qT", Q0, [P, H, T], F32)
    kT = at("kT", Q0 + 20 * KB, [P, H, T], F32)
    v = at("v", Q0 + 40 * KB, [P, NT, H, P + 1], F32)
    PADW = 8 + S0 + 8 + S1 + 8
    pos = [8, 16 + S0]
    u_ext = at("u_ext", Q0, [P, NG, PADW], F32)
    ps_a = at("ps_a", Q0 + 4 * NG * PADW, [P, PADW], F32)
    ps_b = at("ps_b", Q0 + 4 * (NG + 1) * PADW, [P, PADW], F32)
    A0 = Q0 + 4 * (NG + 2) * PADW
    x_in = at("x_in", A0, [P, 3, D], F32)
    xn = at("xn", A0 + 12 * KB, [P, 2, D], F32)
    g1_b = at("g1_b", A0 + 20 * KB, [P, D], F32)
    junk = at("junk", A0 + 24 * KB, [P, D], F32)
    g_i, g_f, g_e, g_b, g_m = (at(n, A0 + 5 * KB * i, [64, T], F32)
                               for i, n in enumerate(("g_i", "g_f", "g_e", "g_b", "g_m")))
    V0 = Q0 + 40 * KB + 4 * NT * H * (P + 1)
    ev = at("ev", V0, [P, 4, 512], F32)
    END = V0 + 8 * KB
    assert END <= nc.sbuf_usable_end

    h_fb = at("h_fb", X0, [P, 2, NT, MW], F32)
    wo_hi = at("wo_hi", X0 + 40 * KB, [P, KD, D], F32R)
    state = at("state", X0 + 72 * KB, [P, 2, H, P + 1], F32)
    dn = at("dn", X0 + 77 * KB, [P, 2, 2], F32)
    rdn = at("rdn", X0 + 77 * KB + 64, [P, 2, 2], F32)
    wo_lo = at("wo_lo", W0, [P, KD, D], F32R)
    uk = at("uk", V0, [P, 2, 2, P], F32)
    wgt = at("wgt", V0 + 2 * KB, [P, 2, 2, P], F32)
    sT = at("sT", V0 + 4 * KB, [P, 2, 2, P], F32)
    qi = at("qi", X0 + 77 * KB + 128, [P, 2, 2, P], F32)

    c_off = [Q0]

    def cbuf(name, shape, dt=F32):
        off = c_off[0]
        c_off[0] += (int(np.prod(shape[1:])) * 4 + 31) // 32 * 32
        return at(name, off, shape, dt)

    mixf = cbuf("mixf", [P, 2, KD, P])
    mix_hi = cbuf("mix_hi", [P, 2, KD, P], F32R)
    mix_lo = cbuf("mix_lo", [P, 2, KD, P], F32R)
    xn2T = cbuf("xn2T", [P, KD, P])
    x1 = at("x1", END - 4 * NT * D, [P, NT, D], F32)
    g2_b = at("g2_b", X0 + 72 * KB, [P, D], F32)
    og = at("og", X0 + 76 * KB, [P, 2, H, P], F32)
    xn2 = at("xn2", W0 + 32 * KB, [P, 2, D], F32)
    sq_c = at("sq_c", X0 + 36 * KB, [P, D], F32)
    assert c_off[0] <= END - 4 * NT * D

    m_off = [X0]

    def mbuf(name, shape, dt=F32):
        off = m_off[0]
        m_off[0] += (int(np.prod(shape[1:])) * 4 + 31) // 32 * 32
        return at(name, off, shape, dt)

    NST, NRG = 12, 6
    gx = mbuf("gx", [P, 2, D])
    yo = mbuf("yo", [P, 2, D])
    sg = mbuf("sg", [P, F])
    hh = mbuf("hh", [P, F])
    e_st = mbuf("e_st", [P, NST, 2, 512])
    e_hi = mbuf("e_hi", [P, NRG, 2, 512], F32R)
    e_lo = mbuf("e_lo", [P, NRG, 2, 512], F32R)
    ex_hi = mbuf("ex_hi", [P, 2, KD, P], F32R)
    ex_lo = mbuf("ex_lo", [P, 2, KD, P], F32R)
    ht_hi = mbuf("ht_hi", [P, 2, KF, P], F32R)
    ht_lo = mbuf("ht_lo", [P, 2, KF, P], F32R)
    row_raw = mbuf("row_raw", [P, 2], I32)
    row_s = mbuf("row_s", [P, 2], I32)
    row_g = mbuf("row_g", [P, 2], I32)
    row_f = mbuf("row_f", [P, 4])
    assert m_off[0] <= END - 4 * NT * D
    gf_b = at("gf_b", X0, [P, D], F32)
    f_y = at("f_y", X0 + 4 * KB, [P, NT, 2, D], F32)
    f_sq = at("f_sq", X0 + (4 + 8 * NT) * KB, [P, D], F32)

    psum = nc.alloc_psum_tensor("psum", [P, 8, 512], F32)

    def two(i):
        return psum[:, i:i + 2, :]

    ctx = ExitStack()
    with ctx:
        ctx.enter_context(nc.allow_non_contiguous_dma(reason="one word to a partition"))

        def sem(name):
            return ctx.enter_context(nc.semaphore(name))

        consts_in, g1_in, list_set = sem("consts_in"), sem("g1_in"), sem("list_set")
        x_load = [sem(f"x_load{i}") for i in range(3)]
        w_load = [sem(f"w_load{i}") for i in range(2)]
        ev_out = [sem(f"ev_out{i}") for i in range(4)]
        small_done, first_load = sem("small_done"), sem("first_load")
        pool_step, consts_done, bias_zero, edges_done, gate_slot_zero = (
            sem(n) for n in ("pool_step", "consts_done", "bias_zero", "edges_done", "gate_slot_zero"))
        sq_done, root_done, xn_done, xt_ready, xhi_done, xlo_done = (
            sem(n) for n in ("sq_done", "root_done", "xn_done", "xt_ready", "xhi_done", "xlo_done"))
        pads_zero, whi_done, wlo_done, proj_ready, act_took, gates_took, v_took = (
            sem(n) for n in ("pads_zero", "whi_done", "wlo_done", "proj_ready", "act_took", "gates_took", "v_took"))
        pooled, mixer_ready, ev_full = sem("pooled"), sem("mixer_ready"), sem("ev_full")
        (g_abs, g_exp, g_ln, rows_ready, turned, dec_ready, cols_done, v_ones, state_zero, e_inter_exp, e_inter_hi,
         e_inter_done) = (
            sem(n) for n in ("g_abs", "g_exp", "g_ln", "rows_ready", "turned", "dec_ready", "cols_done", "v_ones",
                             "state_zero", "e_inter_exp", "e_inter_hi", "e_inter_done"))
        kq_ready, nm_ready, uk_done, wgt_done, s_done, qi_done, kv_ready, rdn_done, state_done, h_done = (
            sem(n) for n in ("kq_ready", "nm_ready", "uk_done", "wgt_done", "s_done", "qi_done", "kv_ready", "rdn_done",
                             "state_done", "h_done"))
        wo_load = [sem(f"wo_load{i}") for i in range(2)]
        wohi_done, wolo_done = sem("wohi_done"), sem("wolo_done")
        c_in = [sem(f"c_in{i}") for i in range(2)]
        g2_in = sem("g2_in")
        xc_in = [sem(f"xc_in{i}") for i in range(2)]
        hsum_done, hss_done, hroot_done, hrecip_done, hn_done, hT_ready, mixf_done, mixhi_done, mixlo_done = (
            sem(n) for n in ("hsum_done", "hss_done", "hroot_done", "hrecip_done", "hn_done", "hT_ready", "mixf_done",
                             "mixhi_done", "mixlo_done"))
        out_ready, x1_done, x1root_done, xn2_done, xn2T_ready, xn2T_done, logits_ready, logits_taken = (
            sem(n) for n in ("out_ready", "x1_done", "x1root_done", "xn2_done", "xn2T_ready", "xn2T_done", "logits_ready",
                             "logits_taken"))
        xn2_out = [sem(f"xn2_out{i}") for i in range(2)]
        list_out = [sem(f"list_out{i}") for i in range(2)]
        chosen_done, rank_ready, slots_done, count_ready, rounds_done, wexp_done = (
            sem(n) for n in ("chosen_done", "rank_ready", "slots_done", "count_ready", "rounds_done", "wexp_done"))
        e_load = [sem(f"e_load{i}") for i in range(NST)]
        row_load = [sem(f"row_load{i}") for i in range(2)]
        gx_load = [sem(f"gx_load{i}") for i in range(2)]
        ehi_done, elo_done, piece_used, row_done, rows_copied, ext_ready, exhi_done, exlo_done = (
            sem(n) for n in ("ehi_done", "elo_done", "piece_used", "row_done", "rows_copied",
                             "ext_ready", "exhi_done", "exlo_done"))
        sg_done, h_ready, ht_ready, hthi_done, htlo_done, y_left, y_right, y_out, row_step = (
            sem(n) for n in ("sg_done", "h_ready", "ht_ready", "hthi_done", "htlo_done", "y_left", "y_right", "y_out",
                             "row_step"))
        f_in = [sem(f"f_in{i}") for i in range(NT)]
        f_out, gf_in, f_sum, f_root, f_done = sem("f_out"), sem("gf_in"), sem("f_sum"), sem("f_root"), sem("f_done")
        pool_past = sem("pool_past")
        dve_step, act_step = sem("dve_step"), sem("act_step")

        block = ctx.enter_context(nc.Block())

        U, G, U_LAST, O, K, Q, VV = 0, NG - 1, NG, NG + 1, NG + 1 + H, NG + 1 + 2 * H, NG + 1 + 3 * H
        NSL = VV + H
        COL = {U: 0, U_LAST: (NG - 1) * P, Q: PW, K: PW + MW, VV: PW + 2 * MW, O: PW + 3 * MW}
        GATES = PW + 4 * MW
        N_EDGE = sum(w - 1 for w in WINDOWS)
        N_CONST = 10

        proj, mixer_after = [], {}
        NS = len(SEGS)
        proj += [("u", U + c, 0) for c in range(NG - 1)]
        proj += [("g", G, s) for s in range(NS)]
        proj += [("u", U + c, s) for s in range(1, NS) for c in range(NG - 1)]
        for first, count, kind in ((U_LAST, 1, "u"), (O, H, "o"), (K, H, "k"), (Q, H, "q")):
            for s in range(NS):
                proj += [(kind, first + c, s) for c in range(count)]
                if kind == "o" and s > 0:
                    mixer_after[len(proj) - count] = (2 * s - 2, 2 * s - 1)
        NPROJ = len(proj)

        last_use = {m: n + 1 for n, (_, m, _) in enumerate(proj)}
        parts_after = {}
        for m in range(NSL - 4):
            parts_after.setdefault(max(last_use[x] for x in range(m + 1)) - 1, []).append(m + 4)

        def act_results(n):
            return sum(kind in "ukq" for kind, _, _ in proj[:n])

        def bank_free(eng, n):
            if n < 4:
                return
            m = n - 4
            if m < NPROJ and proj[m][0] == "g":
                eng.wait_ge(gates_took, proj[m][2] + 1)
            elif m < NPROJ and proj[m][0] == "o":
                eng.wait_ge(ev_full, place["o", proj[m][1] - O, proj[m][2]] + 1)
            elif m < NPROJ:
                eng.wait_ge(act_took, act_results(m + 1))
            else:
                eng.wait_ge(v_took, m - NPROJ + 1)

        ring = []
        for n, (kind, m, s) in enumerate(proj):
            if kind == "o":
                ring.append(("o", m - O, s))
            for g in mixer_after.get(n, ()):
                ring += [("a", g, s2) for s2 in range(len(SEGS))]
        place = {key: i for i, key in enumerate(ring)}

        def chunk_of(step, back):
            if not back:
                return step
            return C0 - 1 - step if step < C0 else NT - 1 - (step - C0)

        NU = 4 * NT

        def unit(n):
            step, pair, d = n // 4, n // 2 % 2, n % 2
            return step, pair, d, chunk_of(step, d)

        def complete_after(t):
            return 4 * (C0 if t < C0 else max(t, NT - 1 + C0 - t) + 1)

        order = sorted(range(NT), key=complete_after)
        EARLY = NT - 4

        def carries(step):
            return step not in (C0 - 1, NT - 1)

        def wait(eng, s, value):
            if not isinstance(value, int) or value >= 1:
                eng.wait_ge(s, value)

        def slot_loads(i, b):
            return 8 * i + 16 - 8 * b

        def load_half_steps(eng):
            eng.wait_ge(rounds_done, 1)
            return eng.value_load(half_steps[0:1, 0:1], min_val=0, max_val=E // 2 * (NT - 1)) + E // 2

        def gu_piece(i, c):
            if isinstance(i, int) and i == 0:
                return c, c, c % NRG, 1
            return 12 * i - 4 + c, (8 + c) % NST, (2 + c) % NRG, i + c // 4

        def down_piece(i, c):
            return 12 * i + 4 + c, 4 + c, (4 + c) % NRG, i + 1

        def last_piece(i, c):
            return 12 * i + 8 + c, 8 + c, (2 + c) % NRG, i + 1

        @block.sync
        def _(sp):
            def slice_in(m):
                if m >= 2:
                    sp.wait_ge(wlo_done, m - 1)
                if m == G:
                    sp.wait_ge(gate_slot_zero, 1)
                    for blk in range(4):
                        c = GATES + H * blk
                        sp.dma_start(w_st[:, m % 2, :, 32 * blk:32 * blk + H],
                                     w_in[0, :, c:c + H].rearrange("(p k) n -> p k n", k=KD)).then_inc(w_load[m % 2], 16)
                    return
                first = max(x for x in COL if x <= m)
                c = COL[first] + (m - first) * P
                sp.dma_start(w_st[:, m % 2, :, :],
                             w_in[0, :, c:c + P].rearrange("(p k) n -> p k n", k=KD)).then_inc(w_load[m % 2], 16)

            sp.dma_start(x_in[:, 0, :], tokens(0, x_prompt, x_sample)).then_inc(first_load, 16)
            sp.dma_start(g1_b[:, :], norm1_g[0:1, :].broadcast_to([P, D])).then_inc(g1_in, 16)
            slice_in(0)
            slice_in(1)
            for dst, src in (
                (wpool[:, :, :], pool_w[0].rearrange("g c e -> c g e")),
                (pscale[:, :], pool_scale[0].rearrange("(g c) -> c g", c=P)),
                (hgain[:, :], head_norm_g[0].rearrange("(h c) -> c h", c=P)),
                (rw[:, :, 0:GR], router_group_w[0].rearrange("(p k) n -> p k n", k=KD)),
                (rw[:, :, GR:NL], router_expert_w[0].rearrange("(p k) g e -> p k (g e)", k=KD)),
                (rbias[:, 0:GR], router_group_b[0:1, :].broadcast_to([P, GR])),
                (rbias[:, GR:NL], router_expert_b[0:1].rearrange("a g e -> a (g e)").broadcast_to([P, E])),
            ):
                sp.dma_start(dst, src).then_inc(consts_in, 16)
            sp.wait_ge(bias_zero, 1)
            for d in range(2):
                for kind in range(2):
                    c = kind * 2 * H + d * H
                    sp.dma_start(gbias[32 * d:32 * d + H, kind:kind + 1],
                                 gate_b[0:1, c:c + H].rearrange("a h -> h a")).then_inc(consts_in, 16)
            for m in range(2, NSL):
                slice_in(m)
            for i in range(KD):
                if i < 2:
                    sp.wait_ge(wlo_done, NSL)
                else:
                    sp.wait_ge(wolo_done, i - 1)
                sp.dma_start(w_st[:, i % 2, :, :].rearrange("p k n -> p (k n)"),
                             w_out[0, i * P:(i + 1) * P, :]).then_inc(wo_load[i % 2], 16)
            for i in range(4):
                sp.wait_ge(ev_out[i], 16 * len(ring[i::4]))
            sp.wait_ge(h_done, NU)
            sp.wait_ge(state_done, NU)
            for i, t in enumerate(order):
                if i >= 2:
                    sp.wait_ge(mixlo_done, i - 1)
                sp.dma_start(mixf[:, i % 2, 0:NG, :], pooled_dram[:, t * P:(t + 1) * P]
                             .rearrange("(g p) n -> p g n", p=P)).then_inc(c_in[i % 2], 16)
                sp.dma_start(og[:, i % 2, :, :], ogate_dram[:, t * P:(t + 1) * P]
                             .rearrange("(g p) n -> p g n", p=P)).then_inc(c_in[i % 2], 16)
                sp.dma_start(x1[:, t, :], tokens(t, x_prompt, x_sample)).then_inc(xc_in[i % 2], 16)
                if i == 0:
                    sp.dma_start(g2_b[:, :], norm2_g[0:1, :].broadcast_to([P, D])).then_inc(g2_in, 16)

            def piece_in(piece, src, d2):
                number, slot, _, _ = piece
                wait(sp, elo_done, number - NST + 1)
                dst = e_st[:, slot, :, :]
                sp.dma_start(dst if d2 else dst.rearrange("p a n -> p (a n)"), src).then_inc(e_load[slot], 16)

            def gu_in(i, c):
                w = expert_w_up if c % 2 else expert_w_gate
                kk = 2 * (c // 2)
                piece_in(gu_piece(i, c), w[0, bass.ds(i % E, 1), :, :]
                         .rearrange("a (p k) n -> p (a k) n", k=KD)[:, kk:kk + 2, :], True)

            def down_in(piece, e, c):
                piece_in(piece, expert_w_down[0, bass.ds(e % E, 1), :, :]
                         .rearrange("a (p k) n -> p (a k) n", k=KF)[:, c, :], False)

            sp.wait_ge(hss_done, NT)
            for c in range(4):
                gu_in(0, c)
            sp.wait_ge(out_ready, NT)
            sp.wait_ge(x1root_done, NT)
            for c in range(4, 8):
                gu_in(0, c)
            def step(i):
                for c in range(8):
                    gu_in(i, c)
                for c in range(4):
                    down_in(down_piece(i, c), i - 1, c)

            step(1)
            n_half = load_half_steps(sp)
            with sp.Fori(1, n_half) as j:
                step(2 * j)
                step(2 * j + 1)
            last = 2 * n_half - 1
            for c in range(4):
                down_in(last_piece(last, c), last, c)

            sp.wait_ge(y_out, 32 * n_half)
            sp.dma_start(gf_b[:, :], final_norm_g.rearrange("(a d) -> a d", a=1).broadcast_to([P, D])).then_inc(gf_in, 16)
            for t in range(NT):
                for k in range(2):
                    sp.dma_start(f_y[:, t, k, :], y_dram[k * T + t * P:k * T + (t + 1) * P, :]).then_inc(f_in[t], 16)
            for t in range(NT):
                sp.wait_ge(f_done, t + 1)
                sp.dma_start(tokens(t, y_prompt, y_sample), x1[:, t, :]).then_inc(f_out, 16)
            sp.wait_ge(f_out, 16 * NT)

        @block.gpsimd
        def _(pool):
            def x_in_tile(t):
                if t >= 3:
                    pool.wait_ge(xn_done, t - 2)
                pool.dma_start(x_in[:, t % 3, :], tokens(t, x_prompt, x_sample)).then_inc(x_load[t % 3], 16)

            for t in range(1, 3):
                x_in_tile(t)
            pool.memset(gbias[:, :], 0.0).then_inc(bias_zero, 1)
            pool.memset(ident[:, :], 0.0).then_inc(pool_step, 1)
            pool.wait_ge(pool_step, 1)
            pool.affine_select(out=ident[:, :], in_=ident[:, :], compare_op=ALU.not_equal, fill=1.0, base=0,
                               pattern=[[-1, P]], channel_multiplier=1).then_inc(consts_done, 1)
            for t in range(3, NT):
                x_in_tile(t)
                if t == 5:
                    pool.wait_ge(wlo_done, G - 1)
                    pool.memset(w_st[:, G % 2, :, :], 0.0).then_inc(gate_slot_zero, 1)
            pool.memset(zero_row[:, :], 0.0).then_inc(consts_done, 1)
            pool.memset(onesb[:, :], 1.0).then_inc(consts_done, 1)
            for tile, value in ((identb[:, :], 0.0), (maskb[:, :, :], 0.0), (laterb[:, :], 1.0),
                                (edge[:, :, :], 1.0)):
                pool.memset(tile, value).then_inc(pool_step, 1)
            pool.wait_ge(pool_step, 5)
            pool.affine_select(out=identb[:, :], in_=identb[:, :], compare_op=ALU.not_equal, fill=1.0, base=0,
                               pattern=[[-1, P]], channel_multiplier=1).then_inc(consts_done, 1)
            for d, sign in enumerate((1, -1)):
                pool.affine_select(out=maskb[:, d, :], in_=maskb[:, d, :], compare_op=ALU.is_ge, fill=MASKED, base=0,
                                   pattern=[[sign, P]], channel_multiplier=-sign).then_inc(consts_done, 1)
            pool.affine_select(out=laterb[:, :], in_=laterb[:, :], compare_op=ALU.is_ge, fill=0.0, base=-1,
                               pattern=[[1, P]], channel_multiplier=-1).then_inc(consts_done, 1)
            for g, w in enumerate(WINDOWS):
                for j in range(w // 2):
                    pool.memset(edge[:, g, j:j + 1], w / (j + w // 2)).then_inc(edges_done, 1)
                for j in range(w // 2 - 1):
                    pool.memset(edge[:, g, 15 - j:16 - j], w / (j + 1 + w // 2)).then_inc(edges_done, 1)
            pool.iota(rowval[:, :, :], pattern=[[T, 2], [P, NT]], base=0, channel_multiplier=1).then_inc(consts_done, 1)
            pool.iota(sentinel[:, :], pattern=[[0, E * CAP // 80 // P], [1, P]], base=2 * T,
                      channel_multiplier=0).then_inc(pool_step, 1)
            pool.iota(ramp_i[:, 0:EPG], pattern=[[-1, EPG]], base=EPG, channel_multiplier=0).then_inc(pool_step, 1)
            pool.iota(ramp_i[:, EPG:EPG + E], pattern=[[CAP, E]], base=0, channel_multiplier=0).then_inc(pool_step, 1)
            pool.wait_ge(pool_step, 8)
            pool.tensor_copy(ramp[:, :], ramp_i[:, 0:EPG]).then_inc(consts_done, 1)
            pool.tensor_copy(ebase[:, :], ramp_i[:, EPG:EPG + E]).then_inc(consts_done, 1)
            pool.dma_start(list_dram.rearrange("(q n) a -> q (n a)", q=80), sentinel[:, :]).then_inc(list_set, 16)

            for i, (kind, c, s) in enumerate(ring):
                a, n = SEGS[s]
                dram = ogate_dram if kind == "o" else pooled_dram
                pool.wait_ge(ev_full, i + 1)
                pool.dma_start(dram[c * P:(c + 1) * P, a:a + n], ev[:, i % 4, 0:n]).then_inc(ev_out[i % 4], 16)

            pool.wait_ge(list_set, 16)

            for t in order:
                pool.wait_ge(h_done, complete_after(t))
                pool.tensor_tensor(h_fb[:, 0, t, :], h_fb[:, 0, t, :], h_fb[:, 1, t, :], ALU.add).then_inc(hsum_done, 1)

            def entries_out(i):
                pool.wait_ge(slots_done, i + 1)
                for k in range(2):
                    pool.indirect_dma_start(
                        out=list_dram, out_offset=bass.IndirectOffsetOnAxis(ap=slot_i[:, i, k:k + 1], axis=0),
                        in_=rowval[:, k, order[i]:order[i] + 1], in_offset=None).then_inc(list_out[i % 2], 16)

            for i, t in enumerate(order):
                pool.wait_ge(xn2_done, i + 1)
                pool.dma_start(xn2_dram[t * P:(t + 1) * P, :], xn2[:, i % 2, :]).then_inc(xn2_out[i % 2], 16)
                if i >= 3:
                    entries_out(i - 3)
            for i in range(NT - 3, NT):
                entries_out(i)
            for i in range(2):
                pool.wait_ge(list_out[i], 16 * NT)
                pool.wait_ge(xn2_out[i], 16 * (NT // 2))

            def list_in(i, b):
                wait(pool, rows_copied, i - 1)
                wait(pool, ext_ready, i - 1)
                pool.sem_inc(pool_past, 1)
                pool.dma_start(row_raw[:, b:b + 1],
                               list_dram[bass.ds((i % E) * CAP + (i // E) * P, P), :]).then_inc(row_load[b], 16)

            def rows_in(i, b):
                pool.wait_ge(row_done, i + 1)
                pool.sem_inc(pool_past, 1)
                pool.indirect_dma_start(
                    out=gx[:, b, :], out_offset=None, in_=xn2_dram,
                    in_offset=bass.IndirectOffsetOnAxis(ap=row_g[:, b:b + 1], axis=0)).then_inc(gx_load[b], 16)

            def rows_out(i, b):
                pool.wait_ge(y_left, i + 1)
                pool.wait_ge(y_right, i + 1)
                pool.sem_inc(pool_past, 1)
                pool.indirect_dma_start(
                    out=y_dram, out_offset=bass.IndirectOffsetOnAxis(ap=row_s[:, b:b + 1], axis=0),
                    in_=yo[:, b, :], in_offset=None).then_inc(y_out, 16)
                pool.wait_ge(y_out, 16 * (i + 1))

            list_in(0, 0)
            list_in(1, 1)
            rows_in(0, 0)
            rows_in(1, 1)
            list_in(2, 0)
            rows_in(2, 0)
            n_half = load_half_steps(pool)
            with pool.Fori(1, n_half) as j:
                list_in(2 * j + 1, 1)
                rows_in(2 * j + 1, 1)
                rows_out(2 * j - 2, 0)
                list_in(2 * j + 2, 0)
                rows_in(2 * j + 2, 0)
                rows_out(2 * j - 1, 1)
            rows_out(2 * n_half - 2, 0)
            rows_out(2 * n_half - 1, 1)

        @block.tensor
        def _(pe):
            def product3(out, a, b, start, stop):
                (a_hi, a_lo), (b_hi, b_lo) = a, b
                pe.matmul(out, a_hi, b_hi, start=start, stop=False)
                pe.matmul(out, a_hi, b_lo, start=False, stop=False)
                return pe.matmul(out, a_lo, b_hi, start=False, stop=stop)

            def picks(r):
                return row_picks[:, r:r + 1].broadcast_to([P, P])

            def one_row(row):
                return ident[0:64, row:row + 1].broadcast_to([64, P])

            def x_transposes(t):
                pe.wait_ge(xn_done, t + 1)
                if t >= 2:
                    pe.wait_ge(xlo_done, t - 1)
                for k in range(KD):
                    last = pe.transpose(psum[:, 4 + 2 * (t % 2) + k // 4, (k % 4) * P:(k % 4 + 1) * P],
                                        xn[:, t % 2, k:D:KD], ident[:, :])
                last.then_inc(xt_ready, 1)

            pe.wait_ge(consts_done, 1)
            for t in range(4):
                x_transposes(t)
            transposed_after = {0: (4,), 1: (5, 6), 2: (7, 8), 3: (9,)}

            def mix_pooled(g):
                if g == 0:
                    pe.wait_ge(consts_in, 16 * 11)
                pe.wait_ge(pooled, g + 1)
                for s in range(len(SEGS)):
                    j = 3 * g + s - 4
                    if j >= 0:
                        pe.wait_ge(ev_full, place["a", j // 3, j % 3] + 1)
                    out = psum[:, 4 + (3 * g + s) % 4, :]
                    a, n = SEGS[s]
                    parts = [(0, 0, S0), (S0, 1, a + n - S0)] if s == 0 else [(0, 1, n)]
                    for col, seq, m in parts:
                        first = pos[seq] + a + col - (S0 if seq else 0)
                        last = pe.matmul(out[:, col:col + m], wpool[:, g, :], u_ext[:, g, first:first + m],
                                         start=True, stop=True)
                    last.then_inc(mixer_ready, 1)

            for n, (kind, m, s) in enumerate(proj):
                a, length = SEGS[s]
                pe.wait_ge(wlo_done, m + 1)
                pe.wait_ge(xlo_done, (a + length) // P)
                bank_free(pe, n)
                for k in range(KD):
                    last = product3(psum[:, n % 4, 0:length], (w_hi[:, m % 4, k, :], w_lo[:, m % 4, k, :]),
                                    (xT_hi[:, k, a:a + length], xT_lo[:, k, a:a + length]), k == 0, k == KD - 1)
                last.then_inc(proj_ready, 1)
                for t in transposed_after.get(n, ()):
                    x_transposes(t)
                for g in mixer_after.get(n, ()):
                    mix_pooled(g)
                if kind == "o" and n + 1 < NPROJ and proj[n + 1][0] == "k":
                    pe.wait_ge(ev_full, place["a", NG - 1, 2] + 1)
                    pe.wait_ge(rows_ready, 1)
                    for c in range(NT):
                        for kind, row in enumerate((g_m, g_i, g_b)):
                            o = (c % 3) * 108 + kind * 36
                            last = pe.transpose(psum[:, 4 + c // 3, o:o + 36], row[0:36, c * P:(c + 1) * P],
                                                ident[0:36, 0:36])
                    last.then_inc(turned, 1)
                    for r in range(2 * H):
                        last = pe.matmul(psum[:, 7, 256 + r * NT:256 + (r + 1) * NT],
                                         one_row(32 * (r // H) + r % H), mlast[:, :], start=True, stop=True)
                    last.then_inc(dec_ready, 1)
            for t in range(NT):
                n = NPROJ + t
                if t == 0:
                    pe.wait_ge(wlo_done, NSL)
                bank_free(pe, n)
                for k in range(KD):
                    tok = slice(t * P, (t + 1) * P)
                    last = product3(psum[:, n % 4, :], (xT_hi[:, k, tok], xT_lo[:, k, tok]),
                                    (w_hi[:, :, k, :], w_lo[:, :, k, :]), k == 0, k == KD - 1)
                last.then_inc(proj_ready, 1)

            def unit_scores(n):
                step, pair, d, ck = unit(n)
                tok = slice(ck * P, (ck + 1) * P)
                heads = (2 * pair, 2 * pair + 1)
                if n >= 2:
                    pe.wait_ge(qi_done, n - 1)
                for hh_, h in enumerate(heads):
                    pe.transpose(psum[:, 4 * d, hh_ * P:(hh_ + 1) * P], kT[:, h, tok], ident[:, :])
                for hh_, h in enumerate(heads):
                    last = pe.matmul(psum[:, 4 * d, (2 + hh_) * P:(3 + hh_) * P], kT[:, h, tok], qT[:, h, tok],
                                     start=True, stop=True)
                last.then_inc(kq_ready, 1)
                for hh_, h in enumerate(heads):
                    out = psum[:, 4 * d + 1, hh_ * P:(hh_ + 1) * P]
                    pe.matmul(out, identb[:, :], maskb[:, d, :], start=True, stop=False)
                    pe.matmul(out, picks(d * H + h), negm[:, tok], start=False, stop=True)
                for hh_, h in enumerate(heads):
                    last = pe.matmul(psum[:, 4 * d + 1, (2 + hh_) * P:(3 + hh_) * P],
                                     picks(d * H + h), e_inter[:, tok], start=True, stop=True)
                last.then_inc(nm_ready, 1)

            def unit_rows(n):
                step, pair, d, ck = unit(n)
                heads = (2 * pair, 2 * pair + 1)
                pe.wait_ge(qi_done, n + 1)
                if n >= 2:
                    pe.wait_ge(h_done, n - 1)
                    pe.wait_ge(state_done, n - 1)
                for hh_, h in enumerate(heads):
                    out = psum[:, 4 * d + 2, hh_ * (P + 1):(hh_ + 1) * (P + 1)]
                    pe.matmul(out, qi[:, d, hh_, :], state[:, d, h, :], start=True, stop=False)
                    last = pe.matmul(out, sT[:, d, hh_, :], v[:, ck, h, :], start=False, stop=True)
                if carries(step):
                    for hh_, h in enumerate(heads):
                        last = pe.matmul(psum[:, 4 * d + 3, hh_ * (P + 1):(hh_ + 1) * (P + 1)], uk[:, d, hh_, :],
                                         v[:, ck, h, :], start=True, stop=True)
                last.then_inc(kv_ready, 1)

            pe.wait_ge(v_took, NT)
            pe.wait_ge(v_ones, 1)
            pe.wait_ge(state_zero, 1)
            pe.wait_ge(cols_done, 1)
            unit_scores(0)
            for n in range(NU):
                if n + 1 < NU:
                    unit_scores(n + 1)
                unit_rows(n)

            def h_transposes(i):
                pe.wait_ge(hn_done, i + 1)
                if i >= 1:
                    pe.wait_ge(mixf_done, i)
                for k in range(H):
                    last = pe.transpose(psum[:, 4, k * P:(k + 1) * P], h_fb[:, 0, order[i], k * P:(k + 1) * P],
                                        ident[:, :])
                last.then_inc(hT_ready, 1)

            def out_rows(t, half):
                if half == 0:
                    pe.wait_ge(mixlo_done, t + 1)
                    if t >= 2:
                        pe.wait_ge(x1_done, t - 1)
                for k in range(KD):
                    c = slice(half * 512, (half + 1) * 512)
                    last = product3(psum[:, 2 * (t % 2) + half, :], (mix_hi[:, t % 2, k, :], mix_lo[:, t % 2, k, :]),
                                    (wo_hi[:, k, c], wo_lo[:, k, c]), k == 0, k == KD - 1)
                if half == 1:
                    last.then_inc(out_ready, 1)

            def xn2_transposes(t):
                pe.wait_ge(xn2_done, t + 1)
                if t >= 1:
                    pe.wait_ge(xn2T_done, t)
                for k in range(KD):
                    last = pe.transpose(psum[:, 5 + k // 4, (k % 4) * P:(k % 4 + 1) * P], xn2[:, t % 2, k:D:KD],
                                        ident[:, :])
                last.then_inc(xn2T_ready, 1)

            def router(t, ranks_read):
                pe.wait_ge(xn2T_done, t + 1)
                if t >= 1:
                    pe.wait_ge(logits_taken, t)
                if ranks_read:
                    pe.wait_ge(slots_done, ranks_read)
                for k in range(KD):
                    last = pe.matmul(psum[:, 7, 0:NL], xn2T[:, k, :], rw[:, k, :], start=(k == 0), stop=(k == KD - 1))
                last.then_inc(logits_ready, 1)

            def ranks(t):
                pe.wait_ge(chosen_done, t + 1)
                for t2 in range(t):
                    pe.matmul(psum[:, 7, 64:64 + E], onesb[:, :], chosen[:, t2, :], start=(t2 == 0), stop=False)
                pe.matmul(psum[:, 7, 64:64 + E], laterb[:, :], chosen[:, t, :], start=(t == 0),
                          stop=True).then_inc(rank_ready, 1)

            pe.wait_ge(wolo_done, KD)
            pe.wait_ge(h_done, NU)
            pe.wait_ge(consts_done, N_CONST)
            h_transposes(0)
            h_transposes(1)
            for t in range(NT + 3):
                if 0 <= t - 3 < NT and t != NT + 1:
                    ranks(t - 3)
                if t < NT:
                    out_rows(t, 0)
                if t == NT + 1:
                    router(t - 2, t - 3)
                    ranks(t - 3)
                elif 0 <= t - 2 < NT:
                    router(t - 2, t - 2)
                if t + 2 < NT:
                    h_transposes(t + 2)
                if t < NT:
                    out_rows(t, 1)
                if 0 <= t - 1 < NT:
                    xn2_transposes(t - 1)
            pe.wait_ge(slots_done, NT)
            for t in range(NT):
                last = pe.matmul(psum[:, 7, 128:128 + E], onesb[:, :], chosen[:, t, :], start=(t == 0), stop=(t == NT - 1))
            last.then_inc(count_ready, 1)

            def ex_transposes(i, b):
                pe.wait_ge(gx_load[b], slot_loads(i, b))
                wait(pe, exlo_done, i)
                for k in range(KD):
                    last = pe.transpose(psum[:, 2 + k // 4, (k % 4) * P:(k % 4 + 1) * P], gx[:, b, k:D:KD], ident[:, :])
                last.then_inc(ext_ready, 1)

            def gate_up(i, b):
                pe.wait_ge(exlo_done, i + 1)
                wait(pe, h_ready, i)
                for c in range(8):
                    number, _, r, _ = gu_piece(i, c)
                    pe.wait_ge(elo_done, number + 1)
                    for kk in range(2):
                        k = 2 * (c // 2) + kk
                        last = product3(psum[:, c % 2, :], (ex_hi[:, b, k, :], ex_lo[:, b, k, :]),
                                        (e_hi[:, r, kk, :], e_lo[:, r, kk, :]), k == 0, k == KD - 1)
                    last.then_inc(piece_used, 1)

            def down(piece, i, b, turned=None):
                pe.wait_ge(htlo_done, i + 1)
                wait(pe, y_left, i)
                wait(pe, y_right, i)
                for c in range(4):
                    number, _, r, _ = piece(c)
                    pe.wait_ge(elo_done, number + 1)
                    for half in range(2):
                        last = product3(psum[:, 4 + half, :], (ht_hi[:, b, c, :], ht_lo[:, b, c, :]),
                                        (e_hi[:, r, half, :], e_lo[:, r, half, :]), c == 0, c == 3)
                    last.then_inc(piece_used, 1)
                    if turned is not None and c == 1:
                        h_turn(turned)

            def h_turn(i):
                pe.wait_ge(h_ready, i + 1)
                for k in range(KF):
                    last = pe.transpose(psum[:, 6, k * P:(k + 1) * P], hh[:, k:F:KF], ident[:, :])
                last.then_inc(ht_ready, 1)

            def step(i, b):
                gate_up(i, b)
                ex_transposes(i + 1, 1 - b)
                down(lambda c: down_piece(i, c), i - 1, 1 - b, turned=i)

            ex_transposes(0, 0)
            gate_up(0, 0)
            ex_transposes(1, 1)
            h_turn(0)
            step(1, 1)
            n_half = load_half_steps(pe)
            with pe.Fori(1, n_half) as j:
                step(2 * j, 0)
                step(2 * j + 1, 1)
            last_i = 2 * n_half - 1
            down(lambda c: last_piece(last_i, c), last_i, 1)

        @block.scalar
        def _(act):
            steps = [0]

            def link(ins):
                steps[0] += 1
                ins.then_inc(act_step, 1)
                act.wait_ge(act_step, steps[0])

            def w_part(m):
                act.wait_ge(w_load[m % 2], 16 * (m // 2 + 1 + (3 if m >= G and m % 2 == G % 2 else 0)))
                if m >= 4:
                    act.wait_ge(proj_ready, last_use[m - 4])
                act.activation(w_hi[:, m % 4, :, :], w_st[:, m % 2, :, :], ACT.Copy).then_inc(whi_done, 1)

            def x_part(t):
                act.wait_ge(xt_ready, t + 1)
                b = 4 + 2 * (t % 2)
                for half in range(2):
                    ins = act.activation(xT_hi[:, 4 * half:4 * half + 4, t * P:(t + 1) * P],
                                         psum[:, b + half, :].rearrange("p (k n) -> p k n", k=4), ACT.Copy)
                ins.then_inc(xhi_done, 1)

            def ring_slot(i):
                if i >= 4:
                    act.wait_ge(ev_out[i % 4], 16 * (i // 4))

            def take(n):
                kind, m, s = proj[n]
                a, length = SEGS[s]
                src = psum[:, n % 4, 0:length]
                if kind != "g":
                    act.wait_ge(proj_ready, n + 1)
                if kind == "u":
                    g = min(m, NG - 1)
                    act.wait_ge(pads_zero, 1)
                    parts = [(0, pos[0], S0), (S0, pos[1], length - S0)] if s == 0 else [(0, pos[1] + a - S0, length)]
                    for col, first, w in parts:
                        ins = act.activation(u_ext[:, g, first:first + w], src[:, col:col + w], ACT.Copy)
                    ins.then_inc(act_took, 1)
                elif kind == "o":
                    i = place["o", m - O, s]
                    ring_slot(i)
                    act.activation(ev[:, i % 4, 0:length], src, ACT.Sigmoid).then_inc(ev_full, 1)
                elif kind == "k":
                    if m == K and s == 0:
                        act.wait_ge(dec_ready, 1)
                        act.activation(g_e[:, :], g_e[:, :], ACT.Exp).then_inc(e_inter_exp, 1)
                        act.wait_ge(e_inter_exp, 1)
                        act.activation(e_inter[0:64, :], g_e[:, :], ACT.Copy).then_inc(e_inter_hi, 1)
                        act.wait_ge(e_inter_done, 1)
                    act.activation(kT[:, m - K, a:a + length], src, ACT.Copy, scale=float(P) ** -0.5).then_inc(act_took, 1)
                elif kind == "q":
                    act.activation(qT[:, m - Q, a:a + length], src, ACT.Copy).then_inc(act_took, 1)
                for m2 in parts_after.get(n, ()):
                    w_part(m2)
                if kind == "u" and proj[n - 1][0] == "u" and proj[n - 2][0] == "g":
                    act.wait_ge(g_abs, 1)
                    act.activation(g_e[:, :], g_e[:, :], ACT.Exp).then_inc(g_exp, 1)
                    act.wait_ge(g_exp, 1)
                    act.activation(g_e[:, :], g_e[:, :], ACT.Ln, bias=onec[0:64, :], scale=1.0).then_inc(g_ln, 1)
                for g in mixer_after.get(n, ()):
                    for s2 in range(len(SEGS)):
                        i = place["a", g, s2]
                        ring_slot(i)
                        act.wait_ge(mixer_ready, 3 * g + s2 + 1)
                        act.activation(ev[:, i % 4, 0:SEGS[s2][1]], psum[:, 4 + (3 * g + s2) % 4, 0:SEGS[s2][1]],
                                       ACT.Copy, scale=pscale[:, g:g + 1]).then_inc(ev_full, 1)
            act.wait_ge(small_done, 1)
            act.activation(stat[:, 1, 0:1], epsc[:, :], ACT.Sqrt).then_inc(root_done, 1)
            act.wait_ge(root_done, 1)
            for t in range(NT):
                if t == 0:
                    act.wait_ge(first_load, 16)
                else:
                    act.wait_ge(x_load[t % 3], 16 * (t // 3 + (t % 3 > 0)))
                act.activation(junk[:, :], x_in[:, t % 3, :], ACT.Square,
                               accum_out=stat[:, 0, t:t + 1]).then_inc(sq_done, 1)
                act.wait_ge(sq_done, t + 1)
                act.activation(stat[:, 1, t:t + 1], stat[:, 0, t:t + 1], ACT.Sqrt, bias=epsc[:, :],
                               scale=1.0 / D).then_inc(root_done, 1)
                if t >= NT - 2:
                    take(t - NT + 2)
                if t >= 1:
                    x_part(t - 1)
                if 3 <= t < 7:
                    w_part(t - 3)
            x_part(NT - 1)
            for n in range(2, NPROJ):
                take(n)

            act.wait_ge(turned, 1)
            act.wait_ge(dec_ready, 1)
            for b in range(4):
                cs = min(3, NT - 3 * b)
                for kind in range(3):
                    for d in range(2):
                        src = psum[:, 4 + b, 0:cs * 108].rearrange("p (c r) -> p c r", c=cs)
                        o = kind * 36 + 32 * d
                        act.activation(cols[:, 3 * b:3 * b + cs, kind, d * H:(d + 1) * H], src[:, :, o:o + H],
                                       ACT.Exp if kind else ACT.Copy)
            act.activation(decay[:, :, :], psum[:, 7, 256:256 + 2 * H * NT].rearrange("p (r c) -> p r c", r=2 * H),
                           ACT.Exp).then_inc(cols_done, 1)
            for t in range(NT):
                act.wait_ge(proj_ready, NPROJ + t + 1)
                src = psum[:, (NPROJ + t) % 4, :].rearrange("p (h n) -> p h n", h=H)
                if t == 0:
                    act.wait_ge(v_ones, 1)
                act.activation(v[:, t, 0:H - 1, 0:P], src[:, 1:H, :], ACT.Copy)
                act.activation(v[:, t, H - 1, 0:P], src[:, 0, :], ACT.Copy).then_inc(v_took, 1)
            for i in range(4):
                act.wait_ge(ev_out[i], 16 * len(ring[i::4]))

            act.wait_ge(cols_done, 1)
            def head_squares(i):
                t = order[i]
                act.wait_ge(hsum_done, i + 1)
                for h in range(H):
                    ins = act.activation(h_fb[:, 1, t, h * P:(h + 1) * P], h_fb[:, 0, t, h * P:(h + 1) * P],
                                         ACT.Square, accum_out=hstat[:, 0, i, h:h + 1])
                ins.then_inc(hss_done, 1)

            squared = 0
            for n in range(NU):
                step, pair, d, ck = unit(n)
                while squared < NT and complete_after(order[squared]) + 5 <= n:
                    head_squares(squared)
                    squared += 1
                act.wait_ge(kq_ready, n + 1)
                if n >= 2:
                    act.wait_ge(kv_ready, n - 1)
                for hh_ in range(2):
                    r = d * H + 2 * pair + hh_
                    ins = act.activation(uk[:, d, hh_, :], psum[:, 4 * d, hh_ * P:(hh_ + 1) * P], ACT.Copy,
                                         scale=cols[:, ck, 2, r:r + 1])
                ins.then_inc(uk_done, 1)
                act.wait_ge(nm_ready, n + 1)
                if n >= 2:
                    act.wait_ge(s_done, n - 1)
                for hh_ in range(2):
                    r = d * H + 2 * pair + hh_
                    ins = act.activation(wgt[:, d, hh_, :], psum[:, 4 * d + 1, hh_ * P:(hh_ + 1) * P], ACT.Exp,
                                         bias=cols[:, ck, 0, r:r + 1])
                ins.then_inc(wgt_done, 1)
                if n % 4 == 3 and step < KD:
                    i = step
                    act.wait_ge(wo_load[i % 2], 16 * (i // 2 + 1))
                    act.activation(wo_hi[:, i, :], w_st[:, i % 2, :, :].rearrange("p k n -> p (k n)"),
                                   ACT.Copy).then_inc(wohi_done, 1)

            def head_roots(first, stop):
                act.wait_ge(hss_done, stop)
                act.activation(hstat[:, 1, first:stop, :], hstat[:, 0, first:stop, :], ACT.Sqrt, bias=epsc[:, :],
                               scale=1.0 / P).then_inc(hroot_done, 1)

            def norm_heads(i):
                if i in (0, squared):
                    act.wait_ge(hrecip_done, 1 if i == 0 else 2)
                t = order[i]
                for h in range(H):
                    ins = act.activation(h_fb[:, 0, t, h * P:(h + 1) * P], h_fb[:, 0, t, h * P:(h + 1) * P], ACT.Copy,
                                         scale=hstat[:, 1, i, h:h + 1])
                ins.then_inc(hn_done, 1)

            def mix_hi_part(i):
                act.wait_ge(mixf_done, i + 1)
                if i >= 2:
                    act.wait_ge(out_ready, i - 1)
                act.activation(mix_hi[:, i % 2, :, :], mixf[:, i % 2, :, :], ACT.Copy).then_inc(mixhi_done, 1)

            def second_root(i):
                act.wait_ge(x1_done, i + 1)
                if i >= 1:
                    act.wait_ge(x1root_done, i)
                link(act.activation(sq_c[:, :], x1[:, order[i], :], ACT.Square, accum_out=stat[:, 2, i:i + 1]))
                act.activation(stat[:, 3, i:i + 1], stat[:, 2, i:i + 1], ACT.Sqrt, bias=epsc[:, :],
                               scale=1.0 / D).then_inc(x1root_done, 1)

            def xn2T_part(i):
                act.wait_ge(xn2T_ready, i + 1)
                if i >= 1:
                    act.wait_ge(logits_ready, i)
                for half in range(2):
                    ins = act.activation(xn2T[:, 4 * half:4 * half + 4, :],
                                         psum[:, 5 + half, :].rearrange("p (k n) -> p k n", k=4), ACT.Copy)
                ins.then_inc(xn2T_done, 1)

            assert squared == EARLY

            def hi_part(piece):
                number, slot, r, loads = piece
                act.wait_ge(e_load[slot], 16 * loads)
                wait(act, piece_used, number - NRG + 1)
                act.activation(e_hi[:, r, :, :], e_st[:, slot, :, :], ACT.Copy).then_inc(ehi_done, 1)

            head_roots(0, squared)
            norm_heads(0)
            norm_heads(1)
            act.wait_ge(h_done, NU)
            mix_hi_part(0)
            norm_heads(2)
            for t in range(NT + 2):
                if 0 <= t - 2 < NT:
                    xn2T_part(t - 2)
                if 0 <= t - 1 < NT:
                    second_root(t - 1)
                if t + 1 < NT:
                    mix_hi_part(t + 1)
                if t - 2 == NT - 1:
                    act.wait_ge(xn2_done, NT)
                    for c in range(6):
                        hi_part(gu_piece(0, c))
                if t == 0:
                    for i in range(squared, NT):
                        head_squares(i)
                    head_roots(squared, NT)
                if t + 3 < NT:
                    norm_heads(t + 3)
            act.wait_ge(chosen_done, NT)
            act.activation(rgs[:, :, :], rgs[:, :, :], ACT.Exp)
            act.activation(rd21[:, :], rd21[:, :], ACT.Exp).then_inc(wexp_done, 1)

            def ex_hi_part(i, b):
                act.wait_ge(ext_ready, i + 1)
                for half in range(2):
                    ins = act.activation(ex_hi[:, b, 4 * half:4 * half + 4, :],
                                         psum[:, 2 + half, :].rearrange("p (k n) -> p k n", k=4), ACT.Copy)
                ins.then_inc(exhi_done, 1)

            def ht_hi_part(i, b):
                act.wait_ge(ht_ready, i + 1)
                act.activation(ht_hi[:, b, :, :], psum[:, 6, :].rearrange("p (k n) -> p k n", k=KF),
                               ACT.Copy).then_inc(hthi_done, 1)

            def y_half(i, b, whole):
                act.wait_ge(piece_used, whole)
                act.activation(yo[:, b, 0:512], psum[:, 4, :], ACT.Copy).then_inc(y_left, 1)

            def silu(i):
                act.wait_ge(piece_used, gu_piece(i, 7)[0] + 1)
                wait(act, h_ready, i)
                act.activation(sg[:, :], psum[:, 0, :], ACT.Silu).then_inc(sg_done, 1)

            def step(i, b, split=0):
                for c in range(split, 2):
                    hi_part(gu_piece(i, c))
                if not split:
                    hi_part(gu_piece(i, 2))
                if not isinstance(i, int) or i >= 2:
                    y_half(i - 2, b, down_piece(i - 1, 3)[0] + 1)
                for c in range(max(split, 3), 8):
                    hi_part(gu_piece(i, c))
                for c in range(2):
                    hi_part(down_piece(i, c))
                silu(i)
                ex_hi_part(i + 1, 1 - b)
                for c in range(2, 4):
                    hi_part(down_piece(i, c))
                ht_hi_part(i, b)

            ex_hi_part(0, 0)
            for c in range(6, 8):
                hi_part(gu_piece(0, c))
            for c in range(4):
                hi_part(gu_piece(1, c))
            silu(0)
            ex_hi_part(1, 1)
            ht_hi_part(0, 0)
            step(1, 1, split=4)
            n_half = load_half_steps(act)
            with act.Fori(1, n_half) as j:
                step(2 * j, 0)
                step(2 * j + 1, 1)
            last_i = 2 * n_half - 1
            for c in range(4):
                hi_part(last_piece(last_i, c))
                if c == 0:
                    y_half(last_i - 1, 0, down_piece(last_i, 3)[0] + 1)
            y_half(last_i, 1, last_piece(last_i, 3)[0] + 1)

            for t in range(NT):
                act.wait_ge(f_sum, t + 1)
                if t >= 1:
                    act.wait_ge(f_root, t)
                link(act.activation(f_sq[:, :], x1[:, t, :], ACT.Square, accum_out=wts[:, 2, t:t + 1]))
                act.activation(wts[:, 3, t:t + 1], wts[:, 2, t:t + 1], ACT.Sqrt, bias=epsc[:, :],
                               scale=1.0 / D).then_inc(f_root, 1)

        @block.vector
        def _(dve):
            steps = [0]

            def link(ins):
                steps[0] += 1
                ins.then_inc(dve_step, 1)
                dve.wait_ge(dve_step, steps[0])

            def w_part(m):
                dve.wait_ge(whi_done, m + 1)
                dve.tensor_tensor(w_lo[:, m % 4, :, :], w_st[:, m % 2, :, :], w_hi[:, m % 4, :, :].bitcast(F32),
                                  ALU.subtract).then_inc(wlo_done, 1)

            def x_part(t):
                dve.wait_ge(xhi_done, t + 1)
                b = 4 + 2 * (t % 2)
                for half in range(2):
                    k = slice(4 * half, 4 * half + 4)
                    ins = dve.tensor_tensor(xT_lo[:, k, t * P:(t + 1) * P],
                                            psum[:, b + half, :].rearrange("p (k n) -> p k n", k=4),
                                            xT_hi[:, k, t * P:(t + 1) * P].bitcast(F32), ALU.subtract)
                ins.then_inc(xlo_done, 1)

            dve.memset(epsc[:, :], EPS)
            dve.memset(onec[:, :], 1.0).then_inc(small_done, 1)
            for first, width in ((0, 8), (pos[0] + S0, 8), (pos[1] + S1, 8)):
                ins = dve.memset(u_ext[:, :, first:first + width], 0.0)
            ins.then_inc(pads_zero, 1)
            dve.wait_ge(g1_in, 16)
            for t in range(NT):
                dve.wait_ge(root_done, t + 2)
                link(dve.reciprocal(stat[:, 1, t:t + 1], stat[:, 1, t:t + 1]))
                if t >= 2:
                    dve.wait_ge(xt_ready, t - 1)
                dve.scalar_tensor_tensor(out=xn[:, t % 2, :], in0=x_in[:, t % 3, :], scalar=stat[:, 1, t:t + 1],
                                         in1=g1_b[:, :], op0=ALU.mult, op1=ALU.mult).then_inc(xn_done, 1)
                if t >= 1:
                    x_part(t - 1)
                if 3 <= t < 7:
                    w_part(t - 3)
            x_part(NT - 1)

            def pool_group(g):
                w = WINDOWS[g]
                dve.wait_ge(act_took, act_results(last_use[g if g < NG - 1 else U_LAST]))
                wait(dve, pooled, g)
                src, bufs, r = u_ext[:, g, :], (ps_a, ps_b), 1
                link(dve.tensor_tensor(ps_a[:, 1:PADW], src[:, 0:PADW - 1], src[:, 1:PADW], ALU.add))
                lo, hi, cur = 1, PADW, 0
                while 2 * r < w:
                    lo, hi = lo + r, hi - r
                    link(dve.tensor_tensor(bufs[1 - cur][:, lo:hi], bufs[cur][:, lo - r:hi - r],
                                           bufs[cur][:, lo + r:hi + r], ALU.add))
                    cur, r = 1 - cur, 2 * r
                sums = bufs[cur]
                for seq, length in enumerate((S0, S1)):
                    for c, e in ((pos[seq], 0), (pos[seq] + length - 8, 8)):
                        ins = dve.tensor_tensor(sums[:, c:c + 8], sums[:, c:c + 8], edge[:, g, e:e + 8], ALU.mult)
                link(ins)
                for seq, length in enumerate((S0, S1)):
                    a = pos[seq]
                    ins = dve.scalar_tensor_tensor(out=u_ext[:, g, a:a + length], in0=sums[:, a:a + length],
                                                   scalar=1.0 / w, in1=u_ext[:, g, a:a + length],
                                                   op0=ALU.mult, op1=ALU.subtract)
                ins.then_inc(pooled, 1)

            def by_direction(fn):
                fn(slice(0, 32), slice(0, T), slice(0, T))
                ins = None
                for a, b in ((0, S0), (S0, T)):
                    rev = slice(b - 1, a - 1 if a else None, -1)
                    ins = fn(slice(32, 64), slice(a, b), rev)
                return ins

            def turn(dst, src):
                return by_direction(lambda r, o, i: dve.tensor_copy(dst[r, o], src[r, i]))

            def ends(x):
                return x[:, :].rearrange("p (c n) -> p c n", n=P)[:, :, P - 1]

            def starts(x):
                return x[:, :].rearrange("p (c n) -> p c n", n=P)[:, :, 0]

            def per_chunk(x):
                return x[:, :].unsqueeze(2).broadcast_to([64, NT, P])

            def chunked(x):
                return x[:, :].rearrange("p (c n) -> p c n", n=P)

            def gates_in(s, n):
                a, length = SEGS[s]
                dve.wait_ge(proj_ready, n + 1)
                if s == 0:
                    dve.wait_ge(consts_in, 16 * 11)
                dve.tensor_scalar(g_i[:, a:a + length], psum[0:64, n % 4, 0:length], gbias[:, 0:1], None, ALU.add)
                dve.tensor_scalar(g_f[:, a:a + length], psum[64:P, n % 4, 0:length], gbias[:, 1:2], None,
                                  ALU.add).then_inc(gates_took, 1)

            def gate_rows():
                dve.wait_ge(g_ln, 1)
                dve.wait_ge(consts_done, 2)
                link(dve.scalar_tensor_tensor(out=g_f[:, :], in0=g_f[:, :], scalar=0.0, in1=g_e[:, :],
                                              op0=ALU.min, op1=ALU.subtract))
                turn(g_b, g_f)
                link(turn(g_e, g_i))
                for c in range(NT):
                    ins = dve.tensor_tensor_scan(g_f[:, c * P:(c + 1) * P], g_b[:, c * P:(c + 1) * P],
                                                 zero_row[:, :], 0.0, ALU.add, ALU.add)
                link(ins)

            def gate_rows_stabilised():
                dve.tensor_tensor(g_e[:, :], g_e[:, :], g_f[:, :], ALU.subtract)
                dve.memset(mprev[:, :], 0.0)
                link(dve.memset(g_b[:, :], 0.0))
                b_end, move = ends(g_f), starts(g_b)
                dve.tensor_copy(move[:, 1:C0], b_end[:, 0:C0 - 1])
                link(dve.tensor_copy(move[:, C0 + 1:NT], b_end[:, C0:NT - 1]))
                for a, b in ((0, S0), (S0, T)):
                    ins = dve.tensor_tensor_scan(g_m[:, a:b], g_b[:, a:b], g_e[:, a:b], 0.0, ALU.add, ALU.max)
                link(ins)
                m_end = ends(g_m)
                for a, b in ((0, C0), (C0, NT)):
                    dve.tensor_tensor(mprev[:, a + 1:b], m_end[:, a:b - 1], b_end[:, a:b - 1], ALU.add)
                link(dve.tensor_copy(mlast[:, :], m_end))
                dve.wait_ge(list_set, 16)
                link(by_direction(lambda r, o, i: dve.tensor_scalar(negm[r, o], g_m[r, i], -1.0, None, ALU.mult)))
                by_direction(lambda r, o, i: dve.scalar_tensor_tensor(
                    out=negm[64 + r.start:64 + r.stop, o], in0=g_m[r, i], scalar=-1.0, in1=negm[r, o].bitcast(F32),
                    op0=ALU.mult, op1=ALU.subtract))
                for d in range(2):
                    dve.tensor_tensor(row_picks[:, d * H:(d + 1) * H], ident[:, 32 * d:32 * d + H],
                                      ident[:, 64 + 32 * d:64 + 32 * d + H], ALU.add)
                dve.tensor_tensor(chunked(g_i), per_chunk(mprev), chunked(g_m), ALU.subtract)
                link(dve.scalar_tensor_tensor(out=g_b[:, :], in0=g_f[:, :], scalar=-1.0, in1=g_m[:, :],
                                              op0=ALU.mult, op1=ALU.subtract))
                link(dve.tensor_tensor(chunked(g_f), chunked(g_e), per_chunk(mlast), ALU.subtract))
                link(turn(g_m, g_e))
                link(turn(g_e, g_i))
                link(turn(g_i, g_b))
                turn(g_b, g_f)
                dve.tensor_tensor(mlast[:, :], mprev[:, :], mlast[:, :], ALU.subtract).then_inc(rows_ready, 1)

            for n, (kind, m, s) in enumerate(proj):
                if kind == "g":
                    if s == 0:
                        dve.wait_ge(xlo_done, NT)
                    gates_in(s, n)
                if kind == "k" and m == K and s == 0:
                    dve.wait_ge(e_inter_hi, 1)
                    dve.tensor_tensor(e_inter[64:P, :], g_e[:, :], e_inter[0:64, :].bitcast(F32),
                                      ALU.subtract).then_inc(e_inter_done, 1)
                for m2 in parts_after.get(n, ()):
                    w_part(m2)
                if kind == "g" and s == NS - 1:
                    dve.wait_ge(gates_took, 3)
                    dve.scalar_tensor_tensor(out=g_e[:, :], in0=g_f[:, :], scalar=-1.0, in1=g_f[:, :],
                                             op0=ALU.mult, op1=ALU.min).then_inc(g_abs, 1)
                    gate_rows()
                if n + 1 == last_use[NG - 2]:
                    gate_rows_stabilised()
                if n + 1 == last_use[U_LAST]:
                    dve.wait_ge(edges_done, N_EDGE)
                    for g in range(NG):
                        pool_group(g)
            dve.wait_ge(e_inter_done, 1)
            dve.memset(v[:, :, :, P:P + 1], 1.0).then_inc(v_ones, 1)
            dve.wait_ge(proj_ready, NPROJ + NT)
            dve.memset(state[:, :, :, :], 0.0).then_inc(state_zero, 1)

            def pair_of(x):
                return x[:, 0:2 * (P + 1)].rearrange("p (h n) -> p h n", h=2)

            def weighted(n):
                step, pair, d, ck = unit(n)
                tok = slice(ck * P, (ck + 1) * P)
                dve.wait_ge(wgt_done, n + 1)
                if n >= 2:
                    dve.wait_ge(kv_ready, n - 1)
                dve.tensor_tensor(sT[:, d, :, :], psum[:, 4 * d, 2 * P:4 * P].rearrange("p (h n) -> p h n", h=2),
                                  wgt[:, d, :, :], ALU.mult).then_inc(s_done, 1)
                dve.tensor_tensor(qi[:, d, :, :], qT[:, 2 * pair:2 * pair + 2, tok],
                                  psum[:, 4 * d + 1, 2 * P:4 * P].rearrange("p (h n) -> p h n", h=2),
                                  ALU.mult).then_inc(qi_done, 1)

            def heads_out(n):
                step, pair, d, ck = unit(n)
                r = d * H + 2 * pair
                dve.wait_ge(kv_ready, n + 1)
                num = pair_of(psum[:, 4 * d + 2, :])
                wait(dve, h_done, n - 1)
                link(dve.tensor_tensor(dn[:, d, :], num[:, :, P], cols[:, ck, 1, r:r + 2], ALU.max))
                link(dve.scalar_tensor_tensor(out=dn[:, d, :], in0=num[:, :, P], scalar=-1.0,
                                              in1=dn[:, d, :], op0=ALU.mult, op1=ALU.max))
                dve.reciprocal(rdn[:, d, :], dn[:, d, :]).then_inc(rdn_done, 1)
                if carries(step):
                    for hh_ in range(2):
                        ins = dve.scalar_tensor_tensor(
                            out=state[:, d, 2 * pair + hh_, :], in0=state[:, d, 2 * pair + hh_, :],
                            scalar=decay[:, r + hh_, step:step + 1],
                            in1=psum[:, 4 * d + 3, hh_ * (P + 1):(hh_ + 1) * (P + 1)], op0=ALU.mult, op1=ALU.add)
                else:
                    ins = dve.memset(state[:, d, 2 * pair:2 * pair + 2, :], 0.0)
                ins.then_inc(state_done, 1)
                dve.wait_ge(rdn_done, n + 1)
                dve.tensor_tensor(h_fb[:, d, ck, 2 * pair * P:(2 * pair + 2) * P].rearrange("p (h n) -> p h n", h=2),
                                  num[:, :, 0:P], rdn[:, d, :].unsqueeze(2).broadcast_to([P, 2, P]),
                                  ALU.mult).then_inc(h_done, 1)

            dve.wait_ge(cols_done, 1)
            for n in range(NU + 1):
                if n < NU:
                    weighted(n)
                if n >= 1:
                    heads_out(n - 1)
                if n % 4 == 0 and 1 <= n // 4 <= KD:
                    i = n // 4 - 1
                    dve.wait_ge(wohi_done, i + 1)
                    dve.tensor_tensor(wo_lo[:, i, :], w_st[:, i % 2, :, :].rearrange("p k n -> p (k n)"),
                                      wo_hi[:, i, :].bitcast(F32), ALU.subtract).then_inc(wolo_done, 1)

            def mix(i):
                b = i % 2
                dve.wait_ge(c_in[b], 32 * (i // 2 + 1))
                dve.wait_ge(hT_ready, i + 1)
                for k in range(H):
                    ins = dve.scalar_tensor_tensor(out=mixf[:, b, NG + k, :], in0=psum[:, 4, k * P:(k + 1) * P],
                                                   scalar=hgain[:, k:k + 1], in1=og[:, b, k, :],
                                                   op0=ALU.mult, op1=ALU.mult)
                ins.then_inc(mixf_done, 1)

            def mix_lo_part(i):
                b = i % 2
                dve.wait_ge(mixhi_done, i + 1)
                dve.tensor_tensor(mix_lo[:, b, :, :], mixf[:, b, :, :], mix_hi[:, b, :, :].bitcast(F32),
                                  ALU.subtract).then_inc(mixlo_done, 1)

            def residual(i):
                b, t = i % 2, order[i]
                dve.wait_ge(out_ready, i + 1)
                dve.wait_ge(xc_in[b], 16 * (i // 2 + 1))
                x1_t = x1[:, t, :].rearrange("p (a n) -> p a n", a=2)
                dve.tensor_tensor(x1_t, x1_t, two(2 * b), ALU.add).then_inc(x1_done, 1)

            def second_norm(i):
                b, t = i % 2, order[i]
                dve.wait_ge(x1root_done, i + 1)
                link(dve.reciprocal(stat[:, 3, i:i + 1], stat[:, 3, i:i + 1]))
                if i >= 2:
                    dve.wait_ge(xn2_out[b], 16 * (i // 2))
                    dve.wait_ge(xn2T_ready, i - 1)
                if i == 0:
                    dve.wait_ge(g2_in, 16)
                dve.scalar_tensor_tensor(out=xn2[:, b, :], in0=x1[:, t, :], scalar=stat[:, 3, i:i + 1],
                                         in1=g2_b[:, :], op0=ALU.mult, op1=ALU.mult).then_inc(xn2_done, 1)

            lg, el = rt[:, 16:16 + GR], rt[:, 16 + GR:16 + NL]
            gtop, gr, etop, er, etop2 = (rt[:, 52 + i:53 + i] for i in range(5))
            eq, oh_g, oh_e = rt[:, 60:68], rt[:, 68:72], rt[:, 72:88]
            esel, esel2 = rt[:, 88:96], rt[:, 96:104]
            emask, both, prod, rank = rt[:, 128:160], rt[:, 160:224], rt[:, 224:288], rt[:, 288:320]
            slot_f = rt[:, 320:322]

            def first_max(values, n, top, key, one_hot):
                link(dve.tensor_reduce(top, values, AX.X, ALU.max))
                link(dve.scalar_tensor_tensor(out=eq[:, 0:n], in0=values, scalar=top, in1=ramp[:, EPG - n:EPG],
                                              op0=ALU.is_ge, op1=ALU.mult))
                link(dve.tensor_reduce(key, eq[:, 0:n], AX.X, ALU.max))
                link(dve.tensor_scalar(one_hot, ramp[:, EPG - n:EPG], key, None, ALU.is_equal))

            def route(t):
                dve.wait_ge(logits_ready, t + 1)
                wait(dve, chosen_done, t)
                dve.tensor_tensor(rt[:, 16:16 + NL], psum[:, 7, 0:NL], rbias[:, :], ALU.add).then_inc(logits_taken, 1)
                dve.wait_ge(logits_taken, t + 1)
                first_max(lg, GR, gtop, gr, oh_g)
                dve.tensor_scalar(rgs[:, order[t], :], lg, gtop, None, ALU.subtract)
                by_group = emask.rearrange("p (g e) -> p g e", g=GR)
                link(dve.tensor_tensor(by_group, el.rearrange("p (g e) -> p g e", g=GR),
                                       oh_g.unsqueeze(2).broadcast_to([P, GR, EPG]), ALU.mult))
                link(dve.tensor_reduce(esel, emask.rearrange("p (g e) -> p e g", g=GR), AX.X, ALU.add))
                first_max(esel, EPG, etop, er, oh_e[:, 0:EPG])
                link(dve.scalar_tensor_tensor(out=esel2, in0=oh_e[:, 0:EPG], scalar=MASKED, in1=esel,
                                              op0=ALU.mult, op1=ALU.add))
                first_max(esel2, EPG, etop2, er, oh_e[:, EPG:2 * EPG])
                dve.tensor_tensor(rd21[:, order[t]:order[t] + 1], etop2, etop, ALU.subtract)
                for k in range(2):
                    ins = dve.tensor_tensor(both[:, k * E:(k + 1) * E].rearrange("p (g e) -> p g e", g=GR),
                                            oh_g.unsqueeze(2).broadcast_to([P, GR, EPG]),
                                            oh_e[:, k * EPG:(k + 1) * EPG].unsqueeze(1).broadcast_to([P, GR, EPG]),
                                            ALU.mult)
                link(ins)
                dve.tensor_tensor(chosen[:, t, :], both[:, 0:E], both[:, E:2 * E], ALU.add).then_inc(chosen_done, 1)

            def list_rows(t):
                dve.wait_ge(rank_ready, t + 1)
                wait(dve, slots_done, t)
                link(dve.tensor_tensor(rank, psum[:, 7, 64:64 + E], ebase[:, :], ALU.add))
                link(dve.tensor_tensor(prod.rearrange("p (k e) -> p k e", k=2), both.rearrange("p (k e) -> p k e", k=2),
                                       rank.unsqueeze(1).broadcast_to([P, 2, E]), ALU.mult))
                link(dve.tensor_reduce(slot_f, prod.rearrange("p (k e) -> p k e", k=2), AX.X, ALU.add))
                dve.tensor_copy(slot_i[:, t, :], slot_f).then_inc(slots_done, 1)

            def lo_part(piece):
                number, slot, r, _ = piece
                dve.wait_ge(ehi_done, number + 1)
                dve.tensor_tensor(e_lo[:, r, :, :], e_st[:, slot, :, :], e_hi[:, r, :, :].bitcast(F32),
                                  ALU.subtract).then_inc(elo_done, 1)

            def head_reciprocal(part, first, stop):
                dve.wait_ge(hroot_done, part)
                dve.reciprocal(hstat[:, 1, first:stop, :], hstat[:, 1, first:stop, :]).then_inc(hrecip_done, 1)

            dve.wait_ge(consts_done, N_CONST)
            dve.wait_ge(h_done, NU)
            head_reciprocal(1, 0, EARLY)
            mix(0)
            mix_lo_part(0)
            for t in range(NT + 3):
                if 0 <= t - 1 < NT:
                    residual(t - 1)
                if t + 1 < NT:
                    mix(t + 1)
                if 0 <= t - 3 < NT:
                    list_rows(t - 3)
                if 0 <= t - 1 < NT:
                    second_norm(t - 1)
                if t + 1 < NT:
                    mix_lo_part(t + 1)
                if 0 <= t - 2 < NT:
                    route(t - 2)
                if t == 0:
                    head_reciprocal(2, EARLY, NT)
            dve.wait_ge(count_ready, 1)
            link(dve.tensor_reduce(rt[0:1, 330:331], psum[0:1, 7, 128:128 + E], AX.X, ALU.max))
            link(dve.tensor_scalar(half_steps[0:1, 1:2], rt[0:1, 330:331], -1.0, None, ALU.add))
            link(dve.tensor_scalar(half_steps[0:1, 2:3], half_steps[0:1, 1:2], 7, None, ALU.logical_shift_right))
            dve.tensor_scalar(half_steps[0:1, 0:1], half_steps[0:1, 2:3], 4, None,
                              ALU.logical_shift_left).then_inc(rounds_done, 1)
            dve.wait_ge(wexp_done, 1)
            dve.tensor_scalar(wts[:, 1, :], rd21[:, :], 1.0, None, ALU.add)
            link(dve.tensor_reduce(wts[:, 0, :], rgs[:, :, :], AX.X, ALU.add))
            link(dve.tensor_tensor(wts[:, 2, :], wts[:, 0, :], wts[:, 1, :], ALU.mult))
            link(dve.reciprocal(wts[:, 0, :], wts[:, 2, :]))
            link(dve.tensor_tensor(wts[:, 1, :], wts[:, 0, :], rd21[:, :], ALU.mult))

            def ex_lo_part(i, b):
                dve.wait_ge(exhi_done, i + 1)
                for half in range(2):
                    k = slice(4 * half, 4 * half + 4)
                    ins = dve.tensor_tensor(ex_lo[:, b, k, :], psum[:, 2 + half, :].rearrange("p (k n) -> p k n", k=4),
                                            ex_hi[:, b, k, :].bitcast(F32), ALU.subtract)
                ins.then_inc(exlo_done, 1)

            def ht_lo_part(i, b):
                dve.wait_ge(hthi_done, i + 1)
                dve.tensor_tensor(ht_lo[:, b, :, :], psum[:, 6, :].rearrange("p (k n) -> p k n", k=KF),
                                  ht_hi[:, b, :, :].bitcast(F32), ALU.subtract).then_inc(htlo_done, 1)

            def source_rows(i, b):
                dve.wait_ge(row_load[b], slot_loads(i, b))
                wait(dve, row_done, i)
                dve.tensor_copy(row_f[:, 0:1], row_raw[:, b:b + 1]).then_inc(row_step, 1)
                dve.wait_ge(row_step, 3 * i + 1)
                dve.tensor_scalar(row_f[:, 1:2], row_f[:, 0:1], float(T), float(T), ALU.is_ge, ALU.mult).then_inc(row_step, 1)
                dve.wait_ge(row_step, 3 * i + 2)
                dve.tensor_tensor(row_f[:, 2:3], row_f[:, 0:1], row_f[:, 1:2], ALU.subtract).then_inc(row_step, 1)
                dve.wait_ge(row_step, 3 * i + 3)
                dve.tensor_scalar(row_g[:, b:b + 1], row_f[:, 2:3], float(T - 1), None, ALU.min).then_inc(row_done, 1)

            def keep_rows(i, b):
                wait(dve, y_out, 16 * (i - 1))
                dve.tensor_copy(row_s[:, b:b + 1], row_raw[:, b:b + 1]).then_inc(rows_copied, 1)

            def y_half(i, b, whole):
                dve.wait_ge(piece_used, whole)
                dve.tensor_copy(yo[:, b, 512:1024], psum[:, 5, :]).then_inc(y_right, 1)

            def hidden(i):
                dve.wait_ge(sg_done, i + 1)
                wait(dve, ht_ready, i)
                dve.tensor_tensor(hh[:, :], psum[:, 1, :], sg[:, :], ALU.mult).then_inc(h_ready, 1)

            def step(i, b, split=0):
                for c in range(split, 2):
                    lo_part(gu_piece(i, c))
                source_rows(i + 1, 1 - b)
                if not split:
                    lo_part(gu_piece(i, 2))
                if not isinstance(i, int) or i >= 2:
                    y_half(i - 2, b, down_piece(i - 1, 3)[0] + 1)
                for c in range(max(split, 3), 8):
                    lo_part(gu_piece(i, c))
                for c in range(2):
                    lo_part(down_piece(i, c))
                hidden(i)
                ex_lo_part(i + 1, 1 - b)
                for c in range(2, 4):
                    lo_part(down_piece(i, c))
                ht_lo_part(i, b)
                keep_rows(i, b)

            for c in range(2):
                lo_part(gu_piece(0, c))
            source_rows(0, 0)
            source_rows(1, 1)
            for c in range(2, 6):
                if c == 5:
                    dve.wait_ge(xn2_out[0], 16 * (NT // 2))
                lo_part(gu_piece(0, c))
            ex_lo_part(0, 0)
            for c in range(6, 8):
                lo_part(gu_piece(0, c))
            for c in range(4):
                lo_part(gu_piece(1, c))
            hidden(0)
            ex_lo_part(1, 1)
            ht_lo_part(0, 0)
            keep_rows(0, 0)
            step(1, 1, split=4)
            n_half = load_half_steps(dve)
            with dve.Fori(1, n_half) as j:
                step(2 * j, 0)
                step(2 * j + 1, 1)
            last_i = 2 * n_half - 1
            for c in range(4):
                lo_part(last_piece(last_i, c))
                if c == 0:
                    y_half(last_i - 1, 0, down_piece(last_i, 3)[0] + 1)
            y_half(last_i, 1, last_piece(last_i, 3)[0] + 1)

            def final_sum(t):
                dve.wait_ge(f_in[t], 32)
                link(dve.scalar_tensor_tensor(out=x1[:, t, :], in0=f_y[:, t, 0, :], scalar=wts[:, 0, t:t + 1],
                                              in1=x1[:, t, :], op0=ALU.mult, op1=ALU.add))
                dve.scalar_tensor_tensor(out=x1[:, t, :], in0=f_y[:, t, 1, :], scalar=wts[:, 1, t:t + 1],
                                         in1=x1[:, t, :], op0=ALU.mult, op1=ALU.add).then_inc(f_sum, 1)

            def final_norm(t):
                dve.wait_ge(f_root, t + 1)
                link(dve.reciprocal(wts[:, 3, t:t + 1], wts[:, 3, t:t + 1]))
                if t == 0:
                    dve.wait_ge(gf_in, 16)
                dve.scalar_tensor_tensor(out=x1[:, t, :], in0=x1[:, t, :], scalar=wts[:, 3, t:t + 1],
                                         in1=gf_b[:, :], op0=ALU.mult, op1=ALU.mult).then_inc(f_done, 1)

            for t in range(NT + 1):
                if t < NT:
                    final_sum(t)
                if t >= 1:
                    final_norm(t - 1)


_INS = ["x_prompt", "x_sample", "norm1_g", "w_in", "pool_w", "pool_scale", "gate_b", "head_norm_g", "w_out",
        "norm2_g", "router_group_w", "router_group_b", "router_expert_w", "router_expert_b",
        "expert_w_gate", "expert_w_up", "expert_w_down", "final_norm_g"]


def kernel(**inputs):
    import numpy as _np
    import concourse.bacc as _bacc
    from concourse import mybir as _mybir
    from concourse.bass_utils import run_bass_kernel_spmd as _run

    nc = _bacc.Bacc("TRN2", target_bir_lowering=False, num_devices=1)
    arrays, args = {}, []
    for name in _INS:
        a = _np.ascontiguousarray(inputs[name])
        arrays[f"in_{name}_dram"] = a
        args.append(nc.dram_tensor(f"in_{name}_dram", a.shape, _mybir.dt.from_np(a.dtype), kind="ExternalInput").ap())
    for i, name in enumerate(("x_prompt", "x_sample")):
        args.append(nc.dram_tensor(f"out_{i}_dram", inputs[name].shape, _mybir.dt.float32, kind="ExternalOutput").ap())
    build(nc, *args)
    r = _run(nc, [arrays], core_ids=[0])
    return tuple(r.results[0][f"out_{i}_dram"] for i in range(2))
```
